# Optimizing a Trainium2 kernel written in Bass

```python
import math
import jax, jax.numpy as jnp
from jax import lax
import numpy as np

D_MODEL = 1024
BATCH = 1
SEQ = 256
DEPTH = 2

N_MIXERS = 2
N_META = 16
Q_BLOCK = 128
SB_HEADS = 16
SB_HEAD_DIM = D_MODEL // SB_HEADS
DIFF_HEAD_DIM = 64
DIFF_HEADS = D_MODEL // (2 * DIFF_HEAD_DIM)
ROPE_THETA = 10000.0
D_FF = 2816
N_EXPERTS = 8
TOP_K = 2
D_FF_EXPERT = 3584
NORM_EPS = 1e-6
N_SB = (DEPTH + 1) // 2
N_DIFF = DEPTH // 2
N_DENSE = (DEPTH + 1) // 2
N_MOE = DEPTH // 2

kernel_name = "hybrid_stickbreaking_diffattn_moe"

def _rmsnorm(x, g):
    xf = x.astype(jnp.float32)
    y = xf * lax.rsqrt(jnp.mean(xf * xf, axis=-1, keepdims=True) + NORM_EPS)
    return (y * g.astype(jnp.float32)).astype(x.dtype)

def _sweep_query_blocks(block_fn, q):
    b, l = q.shape[0], q.shape[1]
    rest = q.shape[2:]
    n_blk = (l - N_META) // Q_BLOCK
    o_meta = block_fn(q[:, :N_META], jnp.arange(N_META, dtype=jnp.int32))
    q_real = jnp.moveaxis(q[:, N_META:].reshape((b, n_blk, Q_BLOCK) + rest), 1, 0)
    pos = N_META + jnp.arange(n_blk * Q_BLOCK, dtype=jnp.int32).reshape(n_blk, Q_BLOCK)
    o_real = lax.map(lambda a: block_fn(a[0], a[1]), (q_real, pos))
    o_real = jnp.moveaxis(o_real, 0, 1)
    o_real = o_real.reshape((b, n_blk * Q_BLOCK) + o_real.shape[3:])
    return jnp.concatenate([o_meta, o_real], axis=1)

def _stick_breaking_mixer(h, w_qkv, w_o):
    b, l, _ = h.shape
    q, k, v = jnp.split(h @ w_qkv, 3, axis=-1)
    q = q.reshape(b, l, SB_HEADS, SB_HEAD_DIM)
    k = k.reshape(b, l, SB_HEADS, SB_HEAD_DIM)
    v = v.reshape(b, l, SB_HEADS, SB_HEAD_DIM)
    scale = SB_HEAD_DIM ** -0.5
    k_pos = jnp.arange(l, dtype=jnp.int32)

    def block(qb, q_pos):
        z = jnp.einsum('bqhd,bkhd->bhqk', qb, k).astype(jnp.float32) * scale
        strict = k_pos[None, :] < q_pos[:, None]
        log_beta = jax.nn.log_sigmoid(z)
        log_keep = jnp.where(strict, jax.nn.log_sigmoid(-z), 0.0)
        log_keep_after = lax.cumsum(log_keep, axis=3, reverse=True) - log_keep
        a = jnp.where(strict, jnp.exp(log_beta + log_keep_after), 0.0)
        return jnp.einsum('bhqk,bkhd->bqhd', a.astype(v.dtype), v)

    o = _sweep_query_blocks(block, q)
    return o.reshape(b, l, D_MODEL) @ w_o

def _rope_tables(l):
    inv = ROPE_THETA ** (-jnp.arange(0, DIFF_HEAD_DIM, 2, dtype=jnp.float32) / DIFF_HEAD_DIM)
    ang = jnp.arange(l, dtype=jnp.float32)[:, None] * inv[None, :]
    return jnp.cos(ang), jnp.sin(ang)

def _apply_rope(x, cos, sin):
    c = cos[:, None, None, :]
    s = sin[:, None, None, :]
    xf = x.astype(jnp.float32)
    x1, x2 = jnp.split(xf, 2, axis=-1)
    return jnp.concatenate([x1 * c - x2 * s, x2 * c + x1 * s], axis=-1).astype(x.dtype)

def _diff_mixer(h, w_qkv, w_o, subln_g, lq1, lk1, lq2, lk2, lambda_init):
    b, l, _ = h.shape
    q, k, v = jnp.split(h @ w_qkv, 3, axis=-1)
    q = q.reshape(b, l, DIFF_HEADS, 2, DIFF_HEAD_DIM)
    k = k.reshape(b, l, DIFF_HEADS, 2, DIFF_HEAD_DIM)
    v = v.reshape(b, l, DIFF_HEADS, 2 * DIFF_HEAD_DIM)
    cos, sin = _rope_tables(l)
    q = _apply_rope(q, cos, sin)
    k = _apply_rope(k, cos, sin)
    lam = (jnp.exp(jnp.sum(lq1.astype(jnp.float32) * lk1.astype(jnp.float32)))
           - jnp.exp(jnp.sum(lq2.astype(jnp.float32) * lk2.astype(jnp.float32)))
           + lambda_init)
    scale = DIFF_HEAD_DIM ** -0.5
    k_pos = jnp.arange(l, dtype=jnp.int32)

    def block(qb, q_pos):
        s = jnp.einsum('bqhcd,bkhcd->bhcqk', qb, k).astype(jnp.float32) * scale
        causal = k_pos[None, :] <= q_pos[:, None]
        p = jax.nn.softmax(jnp.where(causal, s, -jnp.inf), axis=-1)
        w = p[:, :, 0] - lam * p[:, :, 1]
        return jnp.einsum('bhqk,bkhe->bqhe', w.astype(v.dtype), v)

    o = _sweep_query_blocks(block, q)
    o = _rmsnorm(o, subln_g) * (1.0 - lambda_init)
    return o.reshape(b, l, D_MODEL) @ w_o

def _swiglu(x, w_gate, w_up, w_down):
    return (jax.nn.silu(x @ w_gate) * (x @ w_up)) @ w_down

def _moe(h, w_router, w_gate, w_up, w_down):
    b, l, d = h.shape
    x = h.reshape(b * l, d)
    logits = (x @ w_router).astype(jnp.float32)
    top_v, top_i = lax.top_k(logits, TOP_K)
    gates = jax.nn.softmax(top_v, axis=-1)
    combine = jnp.sum(jax.nn.one_hot(top_i, N_EXPERTS, dtype=jnp.float32) * gates[..., None], axis=1)
    out = jnp.zeros_like(x)
    for e in range(N_EXPERTS):
        out = out + combine[:, e:e + 1].astype(x.dtype) * _swiglu(x, w_gate[e], w_up[e], w_down[e])
    return out.reshape(b, l, d)

def setup_inputs(seed: int = 0) -> dict:
    key = jax.random.key(seed)
    ks = jax.random.split(key, 20)
    f32 = jnp.float32

    def w(k, shape, fan_in):
        return jax.random.normal(k, shape, f32) * (fan_in ** -0.5)

    return {
        "x": jax.random.normal(ks[0], (BATCH, SEQ, D_MODEL), f32),
        "meta_tokens": jax.random.normal(ks[1], (N_META, D_MODEL), f32),
        "norm_gains": 1.0 + 0.05 * jax.random.normal(ks[2], (DEPTH, 2, D_MODEL), f32),
        "sb_w_qkv": w(ks[3], (N_SB, D_MODEL, 3 * D_MODEL), D_MODEL),
        "sb_w_o": w(ks[4], (N_SB, D_MODEL, D_MODEL), D_MODEL),
        "diff_w_qkv": w(ks[5], (N_DIFF, D_MODEL, 3 * D_MODEL), D_MODEL),
        "diff_w_o": w(ks[6], (N_DIFF, D_MODEL, D_MODEL), D_MODEL),
        "diff_subln": 1.0 + 0.05 * jax.random.normal(ks[7], (N_DIFF, 2 * DIFF_HEAD_DIM), f32),
        "diff_lambda_q1": 0.1 * jax.random.normal(ks[8], (N_DIFF, DIFF_HEAD_DIM), f32),
        "diff_lambda_k1": 0.1 * jax.random.normal(ks[9], (N_DIFF, DIFF_HEAD_DIM), f32),
        "diff_lambda_q2": 0.1 * jax.random.normal(ks[10], (N_DIFF, DIFF_HEAD_DIM), f32),
        "diff_lambda_k2": 0.1 * jax.random.normal(ks[11], (N_DIFF, DIFF_HEAD_DIM), f32),
        "ffn_w_gate": w(ks[12], (N_DENSE, D_MODEL, D_FF), D_MODEL),
        "ffn_w_up": w(ks[13], (N_DENSE, D_MODEL, D_FF), D_MODEL),
        "ffn_w_down": w(ks[14], (N_DENSE, D_FF, D_MODEL), D_FF),
        "moe_router": w(ks[15], (N_MOE, D_MODEL, N_EXPERTS), D_MODEL),
        "moe_w_gate": w(ks[16], (N_MOE, N_EXPERTS, D_MODEL, D_FF_EXPERT), D_MODEL),
        "moe_w_up": w(ks[17], (N_MOE, N_EXPERTS, D_MODEL, D_FF_EXPERT), D_MODEL),
        "moe_w_down": w(ks[18], (N_MOE, N_EXPERTS, D_FF_EXPERT, D_MODEL), D_FF_EXPERT),
        "final_norm": 1.0 + 0.05 * jax.random.normal(ks[19], (D_MODEL,), f32),
    }

def reference(x, meta_tokens, norm_gains, sb_w_qkv, sb_w_o, diff_w_qkv, diff_w_o, diff_subln,
              diff_lambda_q1, diff_lambda_k1, diff_lambda_q2, diff_lambda_k2,
              ffn_w_gate, ffn_w_up, ffn_w_down, moe_router, moe_w_gate, moe_w_up, moe_w_down,
              final_norm):
    b = x.shape[0]
    meta = jnp.broadcast_to(meta_tokens.astype(x.dtype)[None], (b, N_META, x.shape[-1]))
    h = jnp.concatenate([meta, x], axis=1)
    for i in range(DEPTH):
        j = i // N_MIXERS
        hn = _rmsnorm(h, norm_gains[i, 0])
        if i % N_MIXERS == 0:
            h = h + _stick_breaking_mixer(hn, sb_w_qkv[j], sb_w_o[j])
        else:
            lambda_init = 0.8 - 0.6 * math.exp(-0.3 * i)
            h = h + _diff_mixer(hn, diff_w_qkv[j], diff_w_o[j], diff_subln[j],
                                diff_lambda_q1[j], diff_lambda_k1[j],
                                diff_lambda_q2[j], diff_lambda_k2[j], lambda_init)
        hn = _rmsnorm(h, norm_gains[i, 1])
        if i % 2 == 0:
            h = h + _swiglu(hn, ffn_w_gate[j], ffn_w_up[j], ffn_w_down[j])
        else:
            h = h + _moe(hn, moe_router[j], moe_w_gate[j], moe_w_up[j], moe_w_down[j])
    h = _rmsnorm(h, final_norm)
    return h[:, N_META:]


_drawn_inputs = setup_inputs


def setup_inputs(seed=0):
    import zlib

    import numpy as np

    out = dict(_drawn_inputs(seed))
    spreads = {}
    factors = {'diff_lambda_k1': 8.0, 'diff_lambda_q2': 8.0}
    for name, (base, spread) in spreads.items():
        noise = np.random.default_rng([zlib.crc32(name.encode()), seed]).standard_normal(out[name].shape)
        drawn = base * np.exp(spread * noise) if base else spread * noise
        out[name] = __import__('jax').numpy.asarray(drawn.astype(out[name].dtype))
    for name, factor in factors.items():
        out[name] = (out[name] * factor).astype(out[name].dtype)
    return out
```

```python
import math
from contextlib import ExitStack

import numpy as np

import concourse.bass as bass
from concourse import mybir

F32 = mybir.dt.float32
F32R = mybir.dt.float32r
I32 = mybir.dt.int32
ALU = mybir.AluOpType
ACT = mybir.ActivationFunctionType
AX_X = mybir.AxisListType.X

P = 128
D = 1024
KD = D // P
META = 16
SEQ = 256
L = META + SEQ
HD = 64
SB_HEADS = D // HD
DIFF_HEADS = D // (2 * HD)
FF = 2816
NF = FF // P
E = 8
FE = 3584
EPS = 1e-6
LAMBDA_INIT = 0.8 - 0.6 * math.exp(-0.3)
SCALE = HD ** -0.5
MASKED = -1e30

CHUNK = 4096
WIDE = CHUNK // KD
HALF = WIDE // P * P
QT = SEQ // P
BANK = 512

KT0 = (0, 0, L)
KT1 = (P, L, L - P)
KT2 = (2 * P, 2 * L - P, L - 2 * P)
KEY_TILES = (KT0, KT1, KT2)
SCW = KT2[1] + KT2[2]

C_SB_QKV = 0
C_SB_O = 6
C_UP = 8
N_UP = -(-FF // WIDE)
C_DOWN = C_UP + 2 * N_UP
N_DOWN = -(-NF // 4)
C_D_QKV = C_DOWN + N_DOWN
C_D_O = C_D_QKV + 6
C_MOE = C_D_O + 2
FC = FE // WIDE
CPU = 3 * FC
MAX_UNITS = E + 3


def up_tiles(i):
    return min(4, NF - 4 * i)


def constants():
    r = np.arange(P)
    ident = np.eye(P, dtype=np.float32)
    from_here = (r[:, None] >= r[None, :]).astype(np.float32)
    ones = np.ones((P, P), np.float32)
    before = (r[:, None] < r[None, :]).astype(np.float32)
    keep = np.zeros((P, SCW), np.float32)
    for first, col, width in KEY_TILES:
        key = first + r[:, None]
        query = first + np.arange(width)[None, :]
        keep[:, col:col + width] = key < query
    neg_keep = -keep
    strict_bias = np.where(keep > 0, np.float32(0), np.float32(MASKED)).astype(np.float32)
    causal_bias = np.zeros((P, L), np.float32)
    causal_bias[:, L - P:] = np.where(r[None, :] <= r[:, None], 0.0, MASKED)
    swap = np.zeros((P, P), np.float32)
    swap[r, r ^ 32] = 1.0
    inv = (np.float32(10000.0) ** (-np.arange(0, HD, 2, dtype=np.float32) / np.float32(HD))).astype(np.float32)
    ang = np.arange(L, dtype=np.float32)[None, :] * inv[r % 32][:, None]
    cos = np.cos(ang).astype(np.float32)
    sin = (np.sin(ang) * np.where(r % HD < 32, -1.0, 1.0)[:, None]).astype(np.float32)
    slots = np.broadcast_to(np.arange(1, P + 1, dtype=np.float32), (P, P))
    desc = np.broadcast_to(np.arange(E, 0, -1, dtype=np.float32), (P, E))
    return {
        "c_base": np.concatenate([ident, from_here, ones], 1),
        "c_strict": np.concatenate([neg_keep, strict_bias], 1).astype(np.float32),
        "c_diff": np.concatenate([causal_bias, swap, cos, sin], 1).astype(np.float32),
        "c_route": np.ascontiguousarray(np.concatenate([before, slots, desc], 1).astype(np.float32)),
    }


def build(nc, x, meta, gains, sb_qkv, sb_o, d_qkv, d_o, subln, lq1, lk1, lq2, lk2,
          ffn_gate, ffn_up, ffn_down, router, moe_gate, moe_up, moe_down, final_norm,
          c_base, c_strict, c_diff, c_route, out):
    ctx = ExitStack()
    with ctx:
        def sb(name, shape, dt=F32, where=ctx):
            return where.enter_context(nc.sbuf_tensor(name, shape, dt))

        def sem(name):
            return ctx.enter_context(nc.semaphore(name))

        ps = ctx.enter_context(nc.psum_tensor("ps", [P, 8, BANK], F32))

        raw = sb("raw", [P, 3, CHUNK])
        wh = sb("wh", [P, 2, CHUNK], F32R)
        wl = sb("wl", [P, 2, CHUNK], F32R)
        hT = sb("hT", [P, KD, L])
        xn = sb("xn", [P, KD * L])
        xh = sb("xh", [P, KD * L + P - META], F32R)
        xl = sb("xl", [P, KD * L + P - META], F32R)
        base = sb("base", [P, 3 * P])
        ident, from_here, ones = (base[:, i * P:(i + 1) * P] for i in range(3))
        rs = sb("rs", [P, L])
        vec_rows = sb("vec_rows", [48, P])
        vecs = sb("vecs", [P, 48])
        eps = sb("eps", [P, 1])
        small = sb("small", [P, 16])
        neg_lam = sb("neg_lam", [P, 1])
        gsub = sb("gsub", [P, 1])
        xn3 = xn[:].rearrange("p (k t) -> p k t", t=L)

        def phase(make):
            with ExitStack() as own:
                return make(own)

        def layer0(own):
            b = {}
            b["q"] = sb("q0", [P, KD, L], where=own)
            b["k"] = sb("k0", [P, KD * L + P - META], where=own)
            b["v"] = sb("v0", [P, 3, D], where=own)
            b["soft"] = sb("soft", [P, 2, SCW], where=own)
            b["keepers"] = sb("keepers", [P, 3, SCW], where=own)
            b["att"] = sb("att", [P, 2, SCW], where=own)
            b["strict"] = sb("strict", [P, 2, SCW], where=own)
            return b

        def feed_forward(own):
            return {"ah": sb("ah", [P, NF, L], F32R, where=own), "al": sb("al", [P, NF, L], F32R, where=own)}

        def layer1(own):
            b = {}
            b["q"] = sb("q1", [P, DIFF_HEADS * SEQ], where=own)
            b["k"] = sb("k1", [P, KD * L], where=own)
            b["v"] = sb("v1", [P, 3, D], where=own)
            b["probs"] = sb("probs", [P, 2, 4, L], where=own)
            b["wT"] = sb("wT", [P, 2, 3 * P + SEQ], where=own)
            b["con"] = sb("con", [P, L + P + 2 * L], where=own)
            b["stat"] = sb("stat", [P, 2, 16], where=own)
            return b

        def experts(own):
            b = {}
            b["tok"] = sb("tok", [P, QT, D], where=own)
            b["acc"] = sb("acc", [P, QT, D], where=own)
            b["gh"] = sb("gh", [P, KD * P], F32R, where=own)
            b["gl"] = sb("gl", [P, KD * P], F32R, where=own)
            b["pick"] = sb("pick", [P, QT, P], where=own)
            b["pay"] = sb("pay", [P, QT, P], where=own)
            b["payT"] = sb("payT", [P, SEQ], where=own)
            b["sil"] = sb("sil", [P, BANK], where=own)
            b["act"] = sb("act", [P, BANK], where=own)
            b["ah"] = sb("eah", [P, BANK], F32R, where=own)
            b["al"] = sb("eal", [P, BANK], F32R, where=own)
            b["y"] = sb("y", [P, D], where=own)
            b["con"] = sb("rcon", [P, 2 * P + E], where=own)
            b["wr"] = sb("wr", [P, KD, E], where=own)
            b["r"] = sb("r", [P, 14, QT, E], where=own)
            b["one"] = sb("one", [P, 12, QT], where=own)
            b["pos"] = sb("pos", [P, QT, 12], where=own)
            b["gate"] = sb("gate", [P, QT, 12], where=own)
            b["over"] = sb("over", [P, 6, E], where=own)
            b["unit_f"] = sb("unit_f", [P, 16], where=own)
            b["unit_i"] = sb("unit_i", [1, 16], I32, where=own)
            return b

        b0, bf, b1, bm = phase(layer0), phase(feed_forward), phase(layer1), phase(experts)
        tokens_in = b0["v"]

        raw_landed = [sem(f"raw_landed{i}") for i in range(3)]
        wh_ready, wl_ready = sem("wh_ready"), sem("wl_ready")
        wh_used, w_used = sem("wh_used"), sem("w_used")
        base_in, strict_in, diff_in, route_in = sem("base_in"), sem("strict_in"), sem("diff_in"), sem("route_in")
        x_in, vec_in, gain_in, rows_zero, stores = sem("x_in"), sem("vec_in"), sem("gain_in"), sem("rows_zero"), sem("stores")
        pads, turned, turned_ev = sem("pads"), sem("turned"), sem("turned_ev")
        vec_turned, vec_ev, lam_sum, lam_exp = sem("vec_turned"), sem("vec_ev"), sem("lam_sum"), sem("lam_exp")
        dve_step = sem("dve_step")
        residual, squared, summed, rooted = sem("residual"), sem("squared"), sem("summed"), sem("rooted")
        normed, xh_ready, xl_ready = sem("normed"), sem("xh_ready"), sem("xl_ready")
        tile_done, tile_ev = sem("tile_done"), sem("tile_ev")
        v_done, v_ev = sem("v_done"), sem("v_ev")
        add_done, tile_free = sem("add_done"), sem("tile_free")
        lam_sum_in, pv_done, ds_free, fin_rec = sem("lam_sum_in"), sem("pv_done"), sem("ds_free"), sem("fin_rec")
        score_done, abs_done, soft_done, keep_ready = sem("score_done"), sem("abs_done"), sem("soft_done"), sem("keep_ready")
        log_done, expo_ready, att_ready = sem("log_done"), sem("expo_ready"), sem("att_ready")
        oh_ready, ol_ready = sem("oh_ready"), sem("ol_ready")
        g_done, sil_ready, u_done, prod_ready = sem("g_done"), sem("sil_ready"), sem("u_done"), sem("prod_ready")
        ah_ready, al_ready = sem("ah_ready"), sem("al_ready")
        swap_done, rope_done = sem("swap_done"), sem("rope_done")
        ds_done, max_ready, probs_ready, mix_ready = sem("ds_done"), sem("max_ready"), sem("probs_ready"), sem("mix_ready")
        wt_done, wt_ev_a, wt_ev_m, do_done, do_ev = sem("wt_done"), sem("wt_ev_a"), sem("wt_ev_m"), sem("do_done"), sem("do_ev")
        sub_sq, sub_sum, sub_root = sem("sub_sq"), sem("sub_sum"), sem("sub_root")
        logit_done, back_done, back_ev = sem("logit_done"), sem("back_done"), sem("back_ev")
        gap_ready, gap_exp, sel_ready, pos_done, routed = sem("gap_ready"), sem("gap_exp"), sem("sel_ready"), sem("pos_done"), sem("routed")
        pick_ready, gathered, gh_ready, gl_ready = sem("pick_ready"), sem("gathered"), sem("gh_ready"), sem("gl_ready")
        esil_ready, eprod_ready = sem("esil_ready"), sem("eprod_ready")
        eT_done, eah_ready, eal_ready = sem("eT_done"), sem("eah_ready"), sem("eal_ready")
        pay_ready, payT_done, payT_ev = sem("pay_ready"), sem("payT_done"), sem("payT_ev")
        y0_ev, y1_ev, sc_done, acc_done = sem("y0_ev"), sem("y1_ev"), sem("sc_done"), sem("acc_done")
        fin_sq, fin_root, fin_ready = sem("fin_sq"), sem("fin_root"), sem("fin_ready")

        def cols(w, i):
            return w[:, WIDE * i:min(WIDE * (i + 1), w.shape[1])].rearrange("(k p) n -> p k n", p=P)

        def rows(w, i):
            return w[WIDE * i:min(WIDE * (i + 1), w.shape[0]), :].rearrange("(k p) n -> p k n", p=P)

        sources = [cols(sb_qkv[0], i) for i in range(6)] + [cols(sb_o[0], i) for i in range(2)]
        for i in range(N_UP):
            sources += [cols(ffn_gate[0], i), cols(ffn_up[0], i)]
        sources += [rows(ffn_down[0], i) for i in range(N_DOWN)]
        sources += [cols(d_qkv[0], i) for i in range(6)] + [cols(d_o[0], i) for i in range(2)]
        assert len(sources) == C_MOE
        size = [s.shape[1] * s.shape[2] for s in sources] + [CHUNK] * 4
        weights_of = {"g": moe_gate.rearrange("a e k n -> (a e k) n"), "u": moe_up.rearrange("a e k n -> (a e k) n"),
                      "d": moe_down.rearrange("a e k n -> (a e k) n")}
        unit_chunks = [("g", 0), ("u", 0)]
        for i in range(1, FC):
            unit_chunks += [("g", i), ("u", i), ("d", i - 1)]
        unit_chunks += [("d", FC - 1)]
        at = {c: j for j, c in enumerate(unit_chunks)}

        def raw_f(w):
            return w.bitcast(F32)

        def await_tile(eng, done, before, c, m, tiles):
            if m == tiles - 1:
                eng.wait_ge(w_used, c + 1)
            else:
                eng.wait_ge(done, before + m + 1)

        def tile_signal(ins, done, m, tiles):
            ins.then_inc(w_used if m == tiles - 1 else done, 1)

        block = ctx.enter_context(nc.Block())

        @block.sync
        def _(sp):
            sp.dma_start(tokens_in[0:META, 0, :], meta).then_inc(x_in, 16)
            sp.dma_start(tokens_in[META:P, 0, :], x[0, 0:P - META]).then_inc(x_in, 16)
            sp.dma_start(tokens_in[:, 1, :], x[0, P - META:2 * P - META]).then_inc(x_in, 16)
            sp.dma_start(tokens_in[0:META, 2, :], x[0, 2 * P - META:SEQ]).then_inc(x_in, 16)

            for c, src in enumerate(sources):
                if c >= 3:
                    sp.wait_ge(wl_ready, c - 2)
                dst = raw[:, c % 3, 0:size[c]].rearrange("p (k n) -> p k n", n=src.shape[2])
                sp.dma_start(dst, src).then_inc(raw_landed[c % 3], 16)

            def load_unit(u, e):
                for j, (kind, i) in enumerate(unit_chunks):
                    slot = (C_MOE + j) % 3
                    sp.wait_ge(wl_ready, u * CPU + C_MOE + j - 2)
                    w = weights_of[kind]
                    if kind == "d":
                        src = w[bass.ds(e * FE + WIDE * i, WIDE), :]
                    else:
                        src = w[bass.ds(e * D, D), WIDE * i:WIDE * (i + 1)]
                    src = src.rearrange("(k p) n -> p k n", p=P)
                    dst = raw[:, slot, :].rearrange("p (k n) -> p k n", n=src.shape[2])
                    sp.dma_start(dst, src).then_inc(raw_landed[slot], 16)

            with sp.Fori(0, E) as u:
                load_unit(u, u)
            sp.wait_ge(routed, 1)
            units = sp.value_load(bm["unit_i"][0:1, 15:16], min_val=E, max_val=MAX_UNITS)
            with sp.If(units > E):
                with sp.Fori(E, units) as u:
                    e = sp.value_load(bm["unit_i"][0:1, bass.ds(u, 1)], min_val=0, max_val=E - 1)
                    load_unit(u, e)

            for t in range(QT):
                sp.wait_ge(fin_ready, t + 1)
                sp.dma_start(out[0, t * P:(t + 1) * P], bm["tok"][:, t, :]).then_inc(stores, 16)
            sp.wait_ge(stores, 16 * QT)

        @block.gpsimd
        def _(pool):
            pool.dma_start(base[:], c_base).then_inc(base_in, 16)
            pool.wait_ge(rows_zero, 1)
            pool.dma_start(vec_rows[0:32, :], gains.rearrange("a b (k p) -> (a b k) p", p=P)).then_inc(vec_in, 16)
            pool.dma_start(vec_rows[32:33, :], subln).then_inc(vec_in, 16)
            for n, v in enumerate((lq1, lk1, lq2, lk2)):
                pool.dma_start(vec_rows[33 + n:34 + n, 0:HD], v).then_inc(vec_in, 16)
            pool.dma_start(b0["strict"][:].rearrange("p a n -> p (a n)"), c_strict).then_inc(strict_in, 16)
            pool.wait_ge(residual, 3)
            pool.dma_start(b1["con"][:], c_diff).then_inc(diff_in, 16)
            pool.wait_ge(residual, 4)
            pool.dma_start(bm["con"][:], c_route).then_inc(route_in, 16)
            pool.dma_start(bm["wr"][:], router[0].rearrange("(k p) e -> p k e", p=P)).then_inc(route_in, 16)
            pool.wait_ge(routed, 1)
            pool.wait_ge(back_done, 4)
            pool.dma_start(xn[:, 0:D], final_norm[None, :].to_broadcast([P, D])).then_inc(gain_in, 16)

        @block.scalar
        def _(act):
            def split_high(c):
                act.wait_ge(raw_landed[c % 3], 16 * (c // 3 + 1))
                if c >= 2:
                    act.wait_ge(wh_used, c - 1)
                    act.wait_ge(wl_ready, c - 1)
                n = size[c]
                act.copy(wh[:, c % 2, 0:n], raw[:, c % 3, 0:n]).then_inc(wh_ready, 1)

            def norm(n, last_residual):
                act.wait_ge(residual, last_residual)
                act.activation(xn[:], hT[:].rearrange("p k t -> p (k t)"), ACT.Square).then_inc(squared, 1)
                act.wait_ge(summed, n + 1)
                act.activation(rs[:], ps[:, 7, 0:L], ACT.Sqrt, bias=eps[:, 0:1], scale=1.0 / D).then_inc(rooted, 1)
                for h in range(2):
                    s = slice(h * 4 * L, (h + 1) * 4 * L)
                    act.wait_ge(normed, KD * n + 4 * (h + 1))
                    act.copy(xh[:, s], xn[:, s]).then_inc(xh_ready, 1)

            split_high(0)
            for n in range(6):
                t, g = n // 2, n % 2
                w = P if t < 2 else META
                act.wait_ge(turned, n + 1)
                src = ps[:, n % 4, 0:4 * w].rearrange("p (k t) -> p k t", t=w)
                act.copy(hT[:, 4 * g:4 * g + 4, t * P:t * P + w], src).then_inc(turned_ev, 1)
            split_high(1)
            act.wait_ge(vec_turned, 1)
            act.copy(vecs[:], ps[:, 4, 0:48]).then_inc(vec_ev, 1)
            act.wait_ge(lam_sum, 1)
            act.activation(small[:, 2:4], ps[:, 5, 0:2], ACT.Exp).then_inc(lam_exp, 1)

            norm(0, 1)
            for c in range(4):
                for m in range(4):
                    tt = 4 * c + m
                    await_tile(act, tile_done, 3 * c, c, m, 4)
                    if c < 2:
                        act.mul(b0["q"][:, tt, :], ps[:, tt % 4, 0:L], SCALE).then_inc(tile_ev, 1)
                    else:
                        act.copy(b0["k"][:, (tt - KD) * L:(tt - KD + 1) * L], ps[:, tt % 4, 0:L]).then_inc(tile_ev, 1)
                split_high(c + 2)
            for c in range(4, 6):
                for t in range(3):
                    vi = 3 * (c - 4) + t
                    await_tile(act, v_done, 2 * (c - 4), c, t, 3)
                    act.copy(b0["v"][:, t, (c - 4) * BANK:(c - 3) * BANK], ps[:, 4 + vi % 4, :]).then_inc(v_ev, 1)
                split_high(c + 2)

            for n in range(SB_HEADS + 4):
                if n < SB_HEADS:
                    a = b0["soft"][:, n % 2, :]
                    act.wait_ge(score_done, n + 1)
                    if n >= 2:
                        act.wait_ge(keep_ready, n - 1)
                    act.activation(a, ps[:, n % 4, 0:SCW], ACT.Abs).then_inc(abs_done, 1)
                    act.wait_ge(abs_done, 2 * n + 1)
                    act.activation(a, a, ACT.Exp, scale=-1.0).then_inc(abs_done, 1)
                    act.wait_ge(abs_done, 2 * n + 2)
                    act.activation(a, a, ACT.Ln, bias=1.0).then_inc(log_done, 1)
                m = n - 2
                if 0 <= m < SB_HEADS:
                    act.wait_ge(expo_ready, m + 1)
                    a = b0["att"][:, m % 2, :]
                    act.activation(a, a, ACT.Exp).then_inc(att_ready, 1)
                m = n - 4
                if 0 <= m < SB_HEADS and m % 2 == 1:
                    i = m // 2
                    act.wait_ge(pv_done, 2 * i + 2)
                    act.copy(xh[:, i * L:(i + 1) * L], ps[:, 4 + i % 2, 0:L]).then_inc(oh_ready, 1)
            for c in range(C_SB_O, C_SB_O + 2):
                split_high(c + 2)

            norm(1, 2)
            for i in range(N_UP):
                for f in range(4 * i, 4 * i + up_tiles(i)):
                    await_tile(act, g_done, 3 * i, C_UP + 2 * i, f - 4 * i, up_tiles(i))
                    if f >= 8:
                        act.wait_ge(al_ready, f - 7)
                    act.activation(xn3[:, f % 8, :], ps[:, f % 4, 0:L], ACT.Silu).then_inc(sil_ready, 1)
                split_high(C_UP + 2 * i + 2)
                for f in range(4 * i, 4 * i + up_tiles(i)):
                    act.wait_ge(prod_ready, f + 1)
                    act.copy(bf["ah"][:, f, :], xn3[:, f % 8, :]).then_inc(ah_ready, 1)
                split_high(C_UP + 2 * i + 3)
            for i in range(N_DOWN):
                split_high(C_DOWN + i + 2)

            norm(2, 3)
            for c in range(4):
                for m in range(4):
                    tt = 4 * c + m
                    await_tile(act, tile_done, 12 + 3 * c, C_D_QKV + c, m, 4)
                    if tt >= 8:
                        act.wait_ge(rope_done, tt - 7)
                    if c < 2:
                        act.mul(xn3[:, tt % 8, 0:SEQ], ps[:, tt % 4, 0:SEQ], SCALE).then_inc(tile_ev, 1)
                    else:
                        act.copy(xn3[:, tt % 8, :], ps[:, tt % 4, 0:L]).then_inc(tile_ev, 1)
                split_high(C_D_QKV + c + 2)
            for c in range(4, 6):
                for t in range(3):
                    vi = 3 * (c - 4) + t
                    await_tile(act, v_done, 4 + 2 * (c - 4), C_D_QKV + c, t, 3)
                    act.copy(b1["v"][:, t, (c - 4) * BANK:(c - 3) * BANK], ps[:, vi % 4, :]).then_inc(v_ev, 1)
                split_high(C_D_QKV + c + 2)

            for n in range(DIFF_HEADS + 3):
                if n < DIFF_HEADS:
                    act.wait_ge(max_ready, n + 1)
                    st = b1["stat"][:, n % 2, :]
                    for j in range(4):
                        w = P + META if j < 2 else L
                        pr = b1["probs"][:, n % 2, j, 0:w]
                        act.activation(pr, pr, ACT.Exp, bias=st[:, 4 + j:5 + j],
                                       accum_out=st[:, 8 + j:9 + j]).then_inc(probs_ready, 1)
                m = n - 2
                if 0 <= m < DIFF_HEADS:
                    act.wait_ge(wt_done, m + 1)
                    if m >= 2:
                        act.wait_ge(do_done, m - 1)
                    act.copy(b1["wT"][:, m % 2, 0:3 * P], ps[:, 4 + m % 2, 0:3 * P]).then_inc(wt_ev_a, 1)
                m = n - 3
                if 0 <= m < DIFF_HEADS:
                    act.wait_ge(do_done, m + 1)
                    act.copy(xn[:, m * SEQ:(m + 1) * SEQ], ps[:, 7, 0:SEQ]).then_inc(do_ev, 1)
            act.wait_ge(do_ev, DIFF_HEADS)
            nd = DIFF_HEADS * SEQ
            act.activation(b1["q"][:], xn[:, 0:nd], ACT.Square).then_inc(sub_sq, 1)
            act.wait_ge(sub_sum, 4)
            act.activation(b1["k"][:, 0:nd], ps[:, 0:4, :].rearrange("p b n -> p (b n)"), ACT.Sqrt,
                           bias=eps[:, 0:1], scale=1.0 / (2 * HD)).then_inc(sub_root, 1)
            act.wait_ge(normed, 3 * KD + 1)
            act.copy(xh[:, 0:nd], xn[:, 0:nd]).then_inc(oh_ready, 1)
            for c in range(C_D_O, C_D_O + 2):
                if c + 2 < C_MOE:
                    split_high(c + 2)

            act.wait_ge(residual, 4)
            act.activation(xn[:], hT[:].rearrange("p k t -> p (k t)"), ACT.Square).then_inc(squared, 1)
            act.wait_ge(summed, 4)
            act.activation(rs[:], ps[:, 7, 0:L], ACT.Sqrt, bias=eps[:, 0:1], scale=1.0 / D).then_inc(rooted, 1)
            for n in range(8):
                act.wait_ge(back_done, n + 1)
                dst = bm["tok"] if n < 4 else bm["acc"]
                act.copy(dst[:, n % 4 // 2, n % 2 * BANK:(n % 2 + 1) * BANK], ps[:, 1 + n % 6, :]).then_inc(back_ev, 1)
            act.wait_ge(gap_ready, 1)
            act.activation(bm["one"][:, 5, :], bm["one"][:, 4, :], ACT.Exp).then_inc(gap_exp, 1)

            act.wait_ge(routed, 1)
            units = act.value_load(bm["unit_i"][0:1, 15:16], min_val=E, max_val=MAX_UNITS)

            def gathered_high(k):
                for h in range(2):
                    s = slice(h * BANK, (h + 1) * BANK)
                    act.copy(bm["gh"][:, s], ps[:, 5 + h, :]).then_inc(gh_ready, 1)

            act.wait_ge(gathered, 1)
            gathered_high(0)
            with act.Fori(0, units) as u:
                def unit_split(j):
                    slot = (C_MOE + j) % 3
                    act.wait_ge(raw_landed[slot], u * (16 * FC) + 16 * ((C_MOE + j) // 3 + 1))
                    free = C_MOE + j - (1 if j else 0)
                    act.wait_ge(wh_used, u * CPU + free)
                    act.wait_ge(wl_ready, u * CPU + free)
                    act.copy(wh[:, j % 2, :], raw[:, slot, :]).then_inc(wh_ready, 1)

                def turned_high(i):
                    act.wait_ge(eT_done, u * FC + i + 1)
                    act.copy(bm["ah"][:], ps[:, 4, :]).then_inc(eah_ready, 1)

                unit_split(0)
                unit_split(1)
                for j, (kind, i) in enumerate(unit_chunks):
                    if j + 2 < CPU:
                        unit_split(j + 2)
                    if kind == "g":
                        act.wait_ge(w_used, u * CPU + C_MOE + j + 1)
                        if i:
                            act.wait_ge(eprod_ready, u * FC + i)
                        act.activation(bm["sil"][:], ps[:, 0, :], ACT.Silu).then_inc(esil_ready, 1)
                    if (kind, i) == ("u", 0):
                        turned_high(0)
                    if kind == "d" and i + 1 < FC:
                        turned_high(i + 1)
                        if i + 1 == 3:
                            act.wait_ge(payT_done, u + 1)
                            act.copy(bm["payT"][:], ps[:, 7, 0:SEQ]).then_inc(payT_ev, 1)
                        if i + 1 == FC - 1:
                            act.wait_ge(gathered, u + 2)
                            gathered_high(u + 1)
                act.wait_ge(w_used, u * CPU + C_MOE + CPU)
                act.copy(bm["y"][:, 0:BANK], ps[:, 2, :]).then_inc(y0_ev, 1)

            for t in range(QT):
                act.wait_ge(acc_done, units * 4 + 1)
                act.activation(bm["tok"][:, t, :], bm["acc"][:, t, :], ACT.Square,
                               accum_out=small[:, 4 + t:5 + t]).then_inc(fin_sq, 1)
            act.wait_ge(fin_sq, QT)
            act.activation(small[:, 6:8], small[:, 4:6], ACT.Sqrt, bias=eps[:, 0:1], scale=1.0 / D).then_inc(fin_root, 1)

        @block.vector
        def _(dve):
            steps = [0]

            def step(ins):
                steps[0] += 1
                ins.then_inc(dve_step, 1)
                dve.wait_ge(dve_step, steps[0])

            def split_low(c):
                dve.wait_ge(wh_ready, c + 1)
                if c >= 2:
                    dve.wait_ge(w_used, c - 1)
                n = size[c]
                dve.tensor_tensor(wl[:, c % 2, 0:n], raw[:, c % 3, 0:n], raw_f(wh[:, c % 2, 0:n]),
                                  ALU.subtract).then_inc(wl_ready, 1)

            def scaled(n):
                dve.wait_ge(rooted, n + 1)
                step(dve.reciprocal(rs[:], rs[:]))
                for k in range(KD):
                    dve.scalar_tensor_tensor(out=xn3[:, k, :], in0=hT[:, k, :], scalar=vecs[:, n * KD + k:n * KD + k + 1],
                                             in1=rs[:], op0=ALU.mult, op1=ALU.mult).then_inc(normed, 1)

            def norm(n):
                scaled(n)
                for h in range(2):
                    s = slice(h * 4 * L, (h + 1) * 4 * L)
                    dve.wait_ge(xh_ready, 2 * n + h + 1)
                    dve.tensor_tensor(xl[:, s], xn[:, s], raw_f(xh[:, s]), ALU.subtract).then_inc(xl_ready, 1)

            def add_tile(n, bank, first):
                ins = dve.tensor_tensor(hT[:, n, first:L], hT[:, n, first:L], ps[:, bank, 0:L - first], ALU.add)
                return ins

            step(dve.memset(vec_rows[:], 0.0))
            dve.nop().then_inc(rows_zero, 1)
            dve.memset(eps[:], EPS).then_inc(pads, 1)
            dve.memset(raw_f(xh[:, KD * L:]), 0.0).then_inc(pads, 1)
            dve.memset(raw_f(xl[:, KD * L:]), 0.0).then_inc(pads, 1)
            dve.memset(b0["k"][:, KD * L:], 0.0).then_inc(pads, 1)
            split_low(0)
            split_low(1)
            dve.wait_ge(vec_ev, 1)
            dve.tensor_tensor(small[:, 0:1], vecs[:, 33:34], vecs[:, 34:35], ALU.mult)
            step(dve.tensor_tensor(small[:, 1:2], vecs[:, 35:36], vecs[:, 36:37], ALU.mult))
            dve.tensor_scalar(gsub[:], vecs[:, 32:33], 1.0 - LAMBDA_INIT, None, ALU.mult).then_inc(lam_sum_in, 1)
            dve.wait_ge(lam_exp, 1)
            step(dve.tensor_tensor(neg_lam[:], small[:, 3:4], small[:, 2:3], ALU.subtract))
            step(dve.tensor_scalar(neg_lam[:], neg_lam[:], LAMBDA_INIT, None, ALU.subtract))
            dve.wait_ge(turned_ev, 6)
            dve.nop().then_inc(residual, 1)

            norm(0)
            for c in range(6):
                split_low(c + 2)

            dve.wait_ge(strict_in, 16)
            neg_keep, strict_bias = b0["strict"][:, 0, :], b0["strict"][:, 1, :]
            for n in range(SB_HEADS + 4):
                m = n - 2
                if 0 <= m < SB_HEADS:
                    dve.wait_ge(soft_done, m + 1)
                    if m >= 2:
                        dve.wait_ge(pv_done, m - 1)
                    dve.tensor_tensor(b0["att"][:, m % 2, :], ps[:, m % 4, 0:SCW], strict_bias,
                                      ALU.add).then_inc(expo_ready, 1)
                if n < SB_HEADS:
                    a = b0["soft"][:, n % 2, :]
                    dve.wait_ge(log_done, n + 1)
                    step(dve.scalar_tensor_tensor(out=a, in0=ps[:, n % 4, 0:SCW], scalar=0.0, in1=a,
                                                  op0=ALU.max, op1=ALU.add))
                    if n >= 3:
                        dve.wait_ge(soft_done, n - 2)
                    dve.tensor_tensor(b0["keepers"][:, n % 3, :], a, neg_keep, ALU.mult).then_inc(keep_ready, 1)
                m = n - 4
                if 0 <= m < SB_HEADS and m % 2 == 1:
                    i = m // 2
                    dve.wait_ge(oh_ready, i + 1)
                    s = slice(i * L, (i + 1) * L)
                    dve.tensor_tensor(xl[:, s], ps[:, 4 + i % 2, 0:L], raw_f(xh[:, s]), ALU.subtract).then_inc(ol_ready, 1)

            for c in range(C_SB_O, C_SB_O + 2):
                for n in range(4 * (c - C_SB_O), 4 * (c - C_SB_O) + 4):
                    await_tile(dve, add_done, 3 * (c - C_SB_O), c, n % 4, 4)
                    add_tile(n, n % 4, 0).then_inc(tile_free, 1)
                split_low(c + 2)
            dve.wait_ge(tile_free, KD)
            dve.nop().then_inc(residual, 1)

            norm(1)
            for i in range(N_UP):
                split_low(C_UP + 2 * i + 2)
                for f in range(4 * i, 4 * i + up_tiles(i)):
                    await_tile(dve, u_done, 3 * i, C_UP + 2 * i + 1, f - 4 * i, up_tiles(i))
                    dve.wait_ge(sil_ready, f + 1)
                    dve.tensor_tensor(xn3[:, f % 8, :], xn3[:, f % 8, :], ps[:, 4 + f % 4, 0:L],
                                      ALU.mult).then_inc(prod_ready, 1)
                for f in range(4 * i, 4 * i + up_tiles(i)):
                    dve.wait_ge(ah_ready, f + 1)
                    dve.tensor_tensor(bf["al"][:, f, :], xn3[:, f % 8, :], raw_f(bf["ah"][:, f, :]),
                                      ALU.subtract).then_inc(al_ready, 1)
                split_low(C_UP + 2 * i + 3)
            for i in range(N_DOWN):
                if i == N_DOWN - 1:
                    for n in range(KD):
                        await_tile(dve, add_done, 6, C_DOWN + i, n, KD)
                        add_tile(n, n, 0).then_inc(tile_free, 1)
                split_low(C_DOWN + i + 2)
            dve.wait_ge(tile_free, 2 * KD)
            dve.nop().then_inc(residual, 1)

            norm(2)
            dve.wait_ge(diff_in, 16)
            con = b1["con"]
            causal, swap, cos, sin = con[:, 0:L], con[:, L:L + P], con[:, L + P:2 * L + P], con[:, 2 * L + P:3 * L + P]

            def rotate(tt):
                q = tt < KD
                w, first = (SEQ, META) if q else (L, 0)
                dst = b1["q"][:, tt * SEQ:(tt + 1) * SEQ] if q else b1["k"][:, (tt - KD) * L:(tt - KD + 1) * L]
                src = xn3[:, tt % 8, 0:w]
                dve.wait_ge(tile_ev, 16 + tt + 1)
                dve.wait_ge(swap_done, tt + 1)
                dve.tensor_tensor(dst, ps[:, 4 + tt % 4, 0:w], sin[:, first:L], ALU.mult)
                step(dve.tensor_tensor(src, src, cos[:, first:L], ALU.mult))
                dve.tensor_tensor(dst, dst, src, ALU.add).then_inc(rope_done, 1)

            for c in range(6):
                if c < 4:
                    for tt in range(4 * c, 4 * c + 4):
                        if tt >= 1:
                            rotate(tt - 1)
                if c == 4:
                    rotate(15)
                split_low(C_D_QKV + c + 2)

            for n in range(DIFF_HEADS + 3):
                if n < DIFF_HEADS:
                    st = b1["stat"][:, n % 2, :]
                    if n >= 2:
                        dve.wait_ge(wt_done, n - 1)
                    for comp in range(2):
                        dve.wait_ge(ds_done, 2 * n + comp + 1)
                        for t in range(2):
                            j, c0, w = 2 * t + comp, t * (P + META), P + META if t == 0 else L
                            ins = dve.tensor_tensor_reduce(
                                b1["probs"][:, n % 2, j, 0:w], ps[:, (2 * n + comp) % 4, c0:c0 + w],
                                causal[:, L - w:L], 1.0, -3e38, ALU.add, ALU.max, st[:, j:j + 1])
                        ins.then_inc(ds_free, 1)
                    dve.wait_ge(ds_free, 2 * n + 2)
                    dve.tensor_scalar(st[:, 4:8], st[:, 0:4], -1.0, None, ALU.mult).then_inc(max_ready, 1)
                m = n - 1
                if 0 <= m < DIFF_HEADS:
                    st = b1["stat"][:, m % 2, :]
                    dve.wait_ge(probs_ready, 4 * m + 4)
                    step(dve.reciprocal(st[:, 8:12], st[:, 8:12]))
                    step(dve.tensor_scalar(st[:, 12:14], st[:, 9:12:2], neg_lam[:, 0:1], None, ALU.mult))
                    for t in range(2):
                        w = P + META if t == 0 else L
                        p1, p2 = b1["probs"][:, m % 2, 2 * t, 0:w], b1["probs"][:, m % 2, 2 * t + 1, 0:w]
                        step(dve.tensor_scalar(p1, p1, st[:, 8 + 2 * t:9 + 2 * t], None, ALU.mult))
                        dve.scalar_tensor_tensor(out=p1, in0=p2, scalar=st[:, 12 + t:13 + t], in1=p1,
                                                 op0=ALU.mult, op1=ALU.add).then_inc(mix_ready, 1)
                m = n - 2
                if 0 <= m < DIFF_HEADS:
                    dve.wait_ge(wt_done, m + 1)
                    if m >= 2:
                        dve.wait_ge(do_done, m - 1)
                    dve.tensor_copy(b1["wT"][0:META, m % 2, 3 * P:], ps[0:META, 6, 0:SEQ]).then_inc(wt_ev_m, 1)
            dve.wait_ge(sub_root, 1)
            nd = DIFF_HEADS * SEQ
            step(dve.reciprocal(b1["k"][:, 0:nd], b1["k"][:, 0:nd]))
            dve.scalar_tensor_tensor(out=xn[:, 0:nd], in0=xn[:, 0:nd], scalar=gsub[:, 0:1], in1=b1["k"][:, 0:nd],
                                     op0=ALU.mult, op1=ALU.mult).then_inc(normed, 1)
            dve.wait_ge(oh_ready, KD + 1)
            dve.tensor_tensor(xl[:, 0:nd], xn[:, 0:nd], raw_f(xh[:, 0:nd]), ALU.subtract).then_inc(ol_ready, 1)
            for c in range(C_D_O, C_D_O + 2):
                for n in range(4 * (c - C_D_O), 4 * (c - C_D_O) + 4):
                    await_tile(dve, add_done, 13 + 3 * (c - C_D_O), c, n % 4, 4)
                    add_tile(n, n % 4, META).then_inc(tile_free, 1)
            dve.wait_ge(tile_free, 3 * KD)
            dve.nop().then_inc(residual, 1)

            dve.wait_ge(rooted, 4)
            step(dve.reciprocal(rs[:], rs[:]))
            for k in range(KD):
                dve.scalar_tensor_tensor(out=xn3[:, k, :], in0=hT[:, k, :], scalar=vecs[:, 3 * KD + k:3 * KD + k + 1],
                                         in1=rs[:], op0=ALU.mult, op1=ALU.mult).then_inc(normed, 1)

            r, one, over, unit_f = bm["r"], bm["one"], bm["over"], bm["unit_f"]
            lg, key, top1, lg2, key2, top2, sel, gat, posp, posm = (r[:, i] for i in range(10))
            m1, m2, gap, eg, g1, g2 = one[:, 0], one[:, 1], one[:, 4], one[:, 5], one[:, 6], one[:, 7]
            dve.wait_ge(route_in, 32)
            before, slots, desc = bm["con"][:, 0:P], bm["con"][:, P:2 * P], bm["con"][:, 2 * P:2 * P + E]
            dve.memset(bm["pos"][:], 0.0)
            dve.memset(bm["gate"][:], 0.0)
            dve.wait_ge(logit_done, 1)
            step(dve.tensor_copy(lg, ps[:, 0, 0:QT * E].rearrange("p (t e) -> p t e", e=E)))

            def best(src, key, top, m, km):
                step(dve.tensor_reduce(m, src, AX_X, ALU.max))
                for t in range(QT):
                    ins = dve.scalar_tensor_tensor(out=key[:, t], in0=src[:, t], scalar=m[:, t:t + 1], in1=desc,
                                                   op0=ALU.is_equal, op1=ALU.mult)
                step(ins)
                step(dve.tensor_reduce(km, key, AX_X, ALU.max))
                for t in range(QT):
                    ins = dve.tensor_scalar(top[:, t], key[:, t], km[:, t:t + 1], None, ALU.is_equal)
                step(ins)

            best(lg, key, top1, m1, one[:, 2])
            step(dve.scalar_tensor_tensor(out=lg2, in0=top1, scalar=-3e38, in1=lg, op0=ALU.mult, op1=ALU.add))
            best(lg2, key2, top2, m2, one[:, 3])
            dve.tensor_tensor(sel, top1, top2, ALU.add).then_inc(sel_ready, 1)
            dve.tensor_tensor(gap, m2, m1, ALU.subtract).then_inc(gap_ready, 1)
            dve.wait_ge(gap_exp, 1)
            step(dve.tensor_scalar(g1, eg, 1.0, None, ALU.add))
            step(dve.reciprocal(g1, g1))
            step(dve.tensor_tensor(g2, eg, g1, ALU.mult))
            for t in range(QT):
                ins = dve.tensor_scalar(gat[:, t], top1[:, t], g1[:, t:t + 1], None, ALU.mult)
            step(ins)
            for t in range(QT):
                ins = dve.scalar_tensor_tensor(out=bm["gate"][:, t, 0:E], in0=top2[:, t], scalar=g2[:, t:t + 1],
                                               in1=gat[:, t], op0=ALU.mult, op1=ALU.add)
            step(ins)
            dve.wait_ge(pos_done, 1)
            step(dve.scalar_tensor_tensor(out=bm["pos"][:, :, 0:E],
                                          in0=ps[:, 7, 0:QT * E].rearrange("p (t e) -> p t e", e=E), scalar=1.0,
                                          in1=sel, op0=ALU.add, op1=ALU.mult))
            posp = bm["pos"][:, :, 0:E]

            def pick(u):
                for t in range(QT):
                    ins = dve.tensor_scalar(bm["pick"][:, t, :], slots, bm["pos"][:, t, bass.ds(u, 1)], None, ALU.is_equal)
                ins.then_inc(pick_ready, 1)

            pick(0)
            step(dve.tensor_scalar(posm, posp, float(P), None, ALU.subtract))
            step(dve.tensor_scalar(over[:, 0], ps[:, 7, QT * E:(QT + 1) * E], P + 0.5, None, ALU.is_gt))
            step(dve.tensor_reduce(unit_f[:, 15:16], over[:, 0], AX_X, ALU.add))
            step(dve.tensor_scalar(unit_f[:, 15:16], unit_f[:, 15:16], float(E), None, ALU.add))
            step(dve.tensor_tensor(over[:, 1], over[:, 0], desc, ALU.mult))
            for j in range(MAX_UNITS - E):
                step(dve.tensor_reduce(unit_f[:, 12:13], over[:, 1], AX_X, ALU.max))
                step(dve.tensor_scalar(over[:, 2], over[:, 1], unit_f[:, 12:13], None, ALU.is_equal))
                dve.tensor_scalar(unit_f[:, E + j:E + j + 1], unit_f[:, 12:13], -1.0, float(E), ALU.mult, ALU.add)
                for t in range(QT):
                    step(dve.tensor_tensor_reduce(over[:, 3], over[:, 2], posm[:, t], 1.0, 0.0, ALU.mult, ALU.add,
                                                  bm["pos"][:, t, E + j:E + j + 1]))
                    step(dve.tensor_tensor_reduce(over[:, 3], over[:, 2], bm["gate"][:, t, 0:E], 1.0, 0.0, ALU.mult,
                                                  ALU.add, bm["gate"][:, t, E + j:E + j + 1]))
                step(dve.scalar_tensor_tensor(out=over[:, 1], in0=over[:, 2], scalar=-2.0 * E, in1=over[:, 1],
                                              op0=ALU.mult, op1=ALU.add))
            step(dve.memset(unit_f[:, 0:E], 0.0))
            step(dve.memset(unit_f[:, MAX_UNITS:15], 0.0))
            dve.tensor_copy(bm["unit_i"][:], unit_f[0:1, :]).then_inc(routed, 1)
            dve.wait_ge(routed, 1)
            units = dve.value_load(bm["unit_i"][0:1, 15:16], min_val=E, max_val=MAX_UNITS)

            def gathered_low(k):
                for h in range(2):
                    s = slice(h * BANK, (h + 1) * BANK)
                    dve.wait_ge(gh_ready, k * 2 + h - 1)
                    dve.tensor_tensor(bm["gl"][:, s], ps[:, 5 + h, :], raw_f(bm["gh"][:, s]), ALU.subtract).then_inc(gl_ready, 1)

            gathered_low(1)
            dve.wait_ge(back_ev, 8)
            dve.nop().then_inc(acc_done, 1)
            with dve.Fori(0, units) as u:
                def unit_split(j):
                    slot = (C_MOE + j) % 3
                    dve.wait_ge(wh_ready, u * CPU + C_MOE + j + 1)
                    dve.wait_ge(w_used, u * CPU + C_MOE + j - (1 if j else 0))
                    dve.tensor_tensor(wl[:, j % 2, :], raw[:, slot, :], raw_f(wh[:, j % 2, :]), ALU.subtract).then_inc(wl_ready, 1)

                def turned_low(i):
                    dve.wait_ge(eah_ready, u * FC + i + 1)
                    dve.tensor_tensor(bm["al"][:], ps[:, 4, :], raw_f(bm["ah"][:]), ALU.subtract).then_inc(eal_ready, 1)

                unit_split(0)
                unit_split(1)
                for j, (kind, i) in enumerate(unit_chunks):
                    if kind == "u":
                        dve.wait_ge(esil_ready, u * FC + i + 1)
                        dve.wait_ge(w_used, u * CPU + C_MOE + j + 1)
                        if i:
                            dve.wait_ge(eT_done, u * FC + i)
                        dve.tensor_tensor(bm["act"][:], bm["sil"][:], ps[:, 1, :], ALU.mult).then_inc(eprod_ready, 1)
                    if j + 2 < CPU:
                        unit_split(j + 2)
                    if (kind, i) == ("u", 0):
                        turned_low(0)
                    if kind == "d" and i + 1 < FC:
                        turned_low(i + 1)
                        if i == 1:
                            for t in range(QT):
                                ins = dve.tensor_scalar(bm["pay"][:, t, :], slots, bm["pos"][:, t, bass.ds(u, 1)],
                                                        bm["gate"][:, t, bass.ds(u, 1)], ALU.is_equal, ALU.mult)
                            ins.then_inc(pay_ready, 1)
                        if i == 4:
                            dve.wait_ge(gathered, u + 1)
                            pick(u + 1)
                        if i + 1 == FC - 1:
                            gathered_low(u + 2)
                dve.wait_ge(w_used, u * CPU + C_MOE + CPU)
                dve.tensor_copy(bm["y"][:, BANK:D], ps[:, 3, :]).then_inc(y1_ev, 1)
                for n in range(4):
                    dve.wait_ge(sc_done, u * 4 + n + 1)
                    a = bm["acc"][:, n // 2, n % 2 * BANK:(n % 2 + 1) * BANK]
                    dve.tensor_tensor(a, a, ps[:, (7, 4, 5, 6)[n], :], ALU.add).then_inc(acc_done, 1)

            dve.wait_ge(gain_in, 16)
            dve.wait_ge(fin_root, 1)
            dve.reciprocal(small[:, 8:10], small[:, 6:8]).then_inc(fin_rec, 1)
            dve.wait_ge(fin_rec, 1)
            for t in range(QT):
                dve.scalar_tensor_tensor(out=bm["tok"][:, t, :], in0=bm["acc"][:, t, :], scalar=small[:, 8 + t:9 + t],
                                         in1=xn[:, 0:D], op0=ALU.mult, op1=ALU.mult).then_inc(fin_ready, 1)

        @block.tensor
        def _(pe):
            def feature_product(outp, c, k_tiles, n0, ncols, highs, lows, first=True, last=True):
                high, low = wh[:, c % 2, :], wl[:, c % 2, :]
                for k in range(k_tiles):
                    w = high[:, k * ncols + n0:k * ncols + n0 + P]
                    pe.matmul(outp, w, highs(k), start=first and k == 0, stop=False)
                    last_high = pe.matmul(outp, w, lows(k), start=False, stop=False)
                for k in range(k_tiles):
                    w = low[:, k * ncols + n0:k * ncols + n0 + P]
                    ins = pe.matmul(outp, w, highs(k), start=False, stop=last and k == k_tiles - 1)
                return last_high, ins

            def token_product(outp, c, firsts, stride):
                high, low = wh[:, c % 2, :], wl[:, c % 2, :]
                for k in range(KD):
                    w = high[:, k * WIDE:(k + 1) * WIDE]
                    s = slice(k * stride + firsts, k * stride + firsts + P)
                    pe.matmul(outp, xh[:, s], w, start=(k == 0), stop=False)
                    last_high = pe.matmul(outp, xl[:, s], w, start=False, stop=False)
                for k in range(KD):
                    s = slice(k * stride + firsts, k * stride + firsts + P)
                    ins = pe.matmul(outp, xh[:, s], low[:, k * WIDE:(k + 1) * WIDE], start=False, stop=(k == KD - 1))
                return last_high, ins

            def arrived(c):
                pe.wait_ge(wh_ready, c + 1)
                pe.wait_ge(wl_ready, c + 1)

            def norm_sum(n):
                pe.wait_ge(squared, n + 1)
                for k in range(KD):
                    ins = pe.matmul(ps[:, 7, 0:L], ones, xn3[:, k, :], start=(k == 0), stop=(k == KD - 1))
                ins.then_inc(summed, 1)

            pe.wait_ge(base_in, 16)
            pe.wait_ge(x_in, 64)
            for n in range(6):
                t, g = n // 2, n % 2
                w = P if t < 2 else META
                if n >= 4:
                    pe.wait_ge(turned_ev, n - 3)
                for k in range(4):
                    ins = pe.transpose(ps[:, n % 4, k * w:(k + 1) * w],
                                       tokens_in[0:w, t, (4 * g + k) * P:(4 * g + k + 1) * P], ident[0:w, 0:w])
                ins.then_inc(turned, 1)
            pe.wait_ge(vec_in, 96)
            pe.transpose(ps[:, 4, 0:48], vec_rows[:, :], ident[0:48, 0:48]).then_inc(vec_turned, 1)
            pe.wait_ge(lam_sum_in, 1)
            pe.matmul(ps[:, 5, 0:2], ones, small[:, 0:2], start=True, stop=True).then_inc(lam_sum, 1)

            def part(x_, s, stride):
                return lambda k: x_[:, k * stride + s.start:k * stride + s.stop]

            norm_sum(0)
            pe.wait_ge(pads, 4)
            pe.wait_ge(xl_ready, 2)
            for c in range(4):
                arrived(c)
                for m in range(4):
                    tt = 4 * c + m
                    if tt >= 4:
                        pe.wait_ge(tile_ev, tt - 3)
                    lh, ins = feature_product(ps[:, tt % 4, 0:L], c, KD, m * P, WIDE,
                                              part(xh, slice(0, L), L), part(xl, slice(0, L), L))
                    tile_signal(ins, tile_done, m, 4)
                lh.then_inc(wh_used, 1)
            for c in range(4, 6):
                arrived(c)
                for t in range(3):
                    vi = 3 * (c - 4) + t
                    if vi >= 4:
                        pe.wait_ge(v_ev, vi - 3)
                    lh, ins = token_product(ps[:, 4 + vi % 4, :], c, t * P, L)
                    tile_signal(ins, v_done, t, 3)
                lh.then_inc(wh_used, 1)

            q0, k0, v0 = b0["q"], b0["k"], b0["v"]
            pe.wait_ge(v_ev, 6)
            for n in range(SB_HEADS + 3):
                if n < SB_HEADS:
                    i, rows_ = n // 2, slice(HD * (n % 2), HD * (n % 2) + HD)
                    if n >= 4:
                        pe.wait_ge(expo_ready, n - 3)
                    for first, col, width in KEY_TILES:
                        ins = pe.matmul(ps[:, n % 4, col:col + width], k0[rows_, i * L + first:i * L + first + P],
                                        q0[rows_, i, first:L], start=(first == 0), stop=False, skip_group_check=True)
                    ins.then_inc(score_done, 1)
                m = n - 2
                if 0 <= m < SB_HEADS:
                    pe.wait_ge(keep_ready, m + 1)
                    keep = b0["keepers"][:, m % 3, :]
                    for a, (fa, ca, wa) in enumerate(KEY_TILES):
                        for b, (fb, cb, wb) in enumerate(KEY_TILES[a:]):
                            ins = pe.matmul(ps[:, m % 4, ca + wa - wb:ca + wa], from_here if b == 0 else ones,
                                            keep[:, cb:cb + wb], start=False, stop=(fb == 2 * P),
                                            skip_group_check=True)
                    ins.then_inc(soft_done, 1)
                m = n - 3
                if 0 <= m < SB_HEADS:
                    i, rows_ = m // 2, slice(HD * (m % 2), HD * (m % 2) + HD)
                    pe.wait_ge(att_ready, m + 1)
                    if i >= 2 and m % 2 == 0:
                        pe.wait_ge(ol_ready, i - 1)
                    for t, (first, col, width) in enumerate(KEY_TILES):
                        ins = pe.matmul(ps[rows_, 4 + i % 2, first:L], v0[:, t, m * HD:(m + 1) * HD],
                                        b0["att"][:, m % 2, col:col + width], start=(t == 0), stop=(t == 2),
                                        skip_group_check=True)
                    ins.then_inc(pv_done, 1)

            def out_projection(c0, width, ready):
                pe.wait_ge(ol_ready, ready)
                for c in range(c0, c0 + 2):
                    arrived(c)
                    for m in range(4):
                        n = 4 * (c - c0) + m
                        if n >= 4:
                            pe.wait_ge(tile_free, (0 if c0 == C_SB_O else 2 * KD) + n - 3)
                        lh, ins = feature_product(ps[:, n % 4, 0:width], c, KD, m * P, WIDE,
                                                  part(xh, slice(0, width), width), part(xl, slice(0, width), width))
                        tile_signal(ins, add_done, m, 4)
                    lh.then_inc(wh_used, 1)

            out_projection(C_SB_O, L, KD)

            norm_sum(1)
            pe.wait_ge(xl_ready, 4)
            for i in range(N_UP):
                for kind in range(2):
                    c = C_UP + 2 * i + kind
                    arrived(c)
                    for m in range(up_tiles(i)):
                        f = 4 * i + m
                        if f >= 4:
                            pe.wait_ge(prod_ready if kind else sil_ready, f - 3)
                        lh, ins = feature_product(ps[:, 4 * kind + m, 0:L], c, KD, m * P, up_tiles(i) * P,
                                                  part(xh, slice(0, L), L), part(xl, slice(0, L), L))
                        tile_signal(ins, u_done if kind else g_done, m, up_tiles(i))
                    lh.then_inc(wh_used, 1)
            pe.wait_ge(al_ready, NF)
            for i in range(N_DOWN):
                c = C_DOWN + i
                arrived(c)
                for n in range(KD):
                    lh, ins = feature_product(ps[:, n, 0:L], c, up_tiles(i), n * P, D,
                                              lambda k: bf["ah"][:, 4 * i + k, :], lambda k: bf["al"][:, 4 * i + k, :],
                                              first=(i == 0), last=(i == N_DOWN - 1))
                    if i == N_DOWN - 1 or n == KD - 1:
                        tile_signal(ins, add_done, n, KD)
                lh.then_inc(wh_used, 1)

            norm_sum(2)
            pe.wait_ge(xl_ready, 6)
            pe.wait_ge(diff_in, 16)
            swap = b1["con"][:, L:L + P]

            def swapped(tt):
                w = SEQ if tt < KD else L
                pe.wait_ge(tile_ev, 16 + tt + 1)
                if tt >= 4:
                    pe.wait_ge(rope_done, tt - 3)
                pe.matmul(ps[:, 4 + tt % 4, 0:w], swap, xn3[:, tt % 8, 0:w], start=True, stop=True).then_inc(swap_done, 1)

            for c in range(4):
                arrived(C_D_QKV + c)
                for m in range(4):
                    tt = 4 * c + m
                    if tt >= 4:
                        pe.wait_ge(tile_ev, 16 + tt - 3)
                    s = slice(META, L) if c < 2 else slice(0, L)
                    lh, ins = feature_product(ps[:, tt % 4, 0:s.stop - s.start], C_D_QKV + c, KD, m * P, WIDE,
                                              part(xh, s, L), part(xl, s, L))
                    tile_signal(ins, tile_done, m, 4)
                    if tt >= 1:
                        swapped(tt - 1)
                lh.then_inc(wh_used, 1)
            swapped(15)
            for c in range(4, 6):
                arrived(C_D_QKV + c)
                for t in range(3):
                    vi = 3 * (c - 4) + t
                    if vi >= 4:
                        pe.wait_ge(v_ev, 6 + vi - 3)
                    lh, ins = token_product(ps[:, vi % 4, :], C_D_QKV + c, (0, META, META + P)[t], L)
                    tile_signal(ins, v_done, t, 3)
                lh.then_inc(wh_used, 1)

            q1, k1, v1 = b1["q"], b1["k"], b1["v"]
            pe.wait_ge(rope_done, 16)
            pe.wait_ge(v_ev, 12)
            for n in range(DIFF_HEADS + 3):
                if n < DIFF_HEADS:
                    if n >= 2:
                        pe.wait_ge(ds_free, 2 * n - 2)
                    for t in range(2):
                        c0, w = t * (P + META), P + META if t == 0 else L
                        for comp in range(2):
                            rows_ = slice(HD * comp, HD * comp + HD)
                            ins = pe.matmul(ps[:, (2 * n + comp) % 4, c0:c0 + w],
                                            q1[rows_, n * SEQ + t * P:n * SEQ + (t + 1) * P],
                                            k1[rows_, n * L:n * L + w], start=True, stop=True)
                            if t:
                                ins.then_inc(ds_done, 1)
                m = n - 2
                if 0 <= m < DIFF_HEADS:
                    pr = b1["probs"][:, m % 2]
                    pe.wait_ge(mix_ready, 2 * m + 2)
                    if m >= 2:
                        pe.wait_ge(wt_ev_a, m - 1)
                    pe.transpose(ps[:, 4 + m % 2, 0:P], pr[:, 0, META:META + P], ident)
                    pe.transpose(ps[:, 4 + m % 2, P:2 * P], pr[:, 2, META:META + P], ident)
                    pe.transpose(ps[:, 4 + m % 2, 2 * P:3 * P], pr[:, 2, META + P:L], ident)
                    if m >= 1:
                        pe.wait_ge(wt_ev_m, m)
                    pe.transpose(ps[0:META, 6, 0:P], pr[:, 0, 0:META], ident)
                    pe.transpose(ps[0:META, 6, P:2 * P], pr[:, 2, 0:META], ident).then_inc(wt_done, 1)
                m = n - 3
                if 0 <= m < DIFF_HEADS:
                    wT = b1["wT"][:, m % 2, :]
                    pe.wait_ge(wt_ev_a, m + 1)
                    pe.wait_ge(wt_ev_m, m + 1)
                    if m >= 1:
                        pe.wait_ge(do_ev, m)
                    cs = slice(m * P, (m + 1) * P)
                    pe.matmul(ps[:, 7, 0:SEQ], v1[0:META, 0, cs], wT[0:META, 3 * P:], start=True, stop=False)
                    pe.matmul(ps[:, 7, 0:SEQ], v1[:, 1, cs], wT[:, 0:2 * P], start=False, stop=False)
                    pe.matmul(ps[:, 7, P:SEQ], v1[:, 2, cs], wT[:, 2 * P:3 * P], start=False, stop=True).then_inc(do_done, 1)
            pe.wait_ge(sub_sq, 1)
            for n in range(4):
                pe.matmul(ps[:, n, :], ones, b1["q"][:, n * BANK:(n + 1) * BANK], start=True, stop=True).then_inc(sub_sum, 1)
            out_projection(C_D_O, SEQ, KD + 1)

            norm_sum(3)
            pe.wait_ge(normed, 4 * KD + 1)
            pe.wait_ge(route_in, 32)
            for t in range(QT):
                for k in range(KD):
                    ins = pe.matmul(ps[:, 0, t * E:(t + 1) * E], xn3[:, k, META + t * P:META + (t + 1) * P],
                                    bm["wr"][:, k, :], start=(k == 0), stop=(k == KD - 1))
            ins.then_inc(logit_done, 1)
            for n in range(8):
                if n >= 6:
                    pe.wait_ge(back_ev, n - 5)
                src = xn3 if n < 4 else hT
                t, half = n % 4 // 2, n % 2
                for k in range(4):
                    ins = pe.transpose(ps[:, 1 + n % 6, k * P:(k + 1) * P],
                                       src[:, 4 * half + k, META + t * P:META + (t + 1) * P], ident)
                ins.then_inc(back_done, 1)
            before = bm["con"][:, 0:P]
            sel = bm["r"][:, 6]
            pe.wait_ge(sel_ready, 1)
            pe.matmul(ps[:, 7, 0:E], before, sel[:, 0], start=True, stop=True)
            pe.matmul(ps[:, 7, E:2 * E], ones, sel[:, 0], start=True, stop=False)
            pe.matmul(ps[:, 7, E:2 * E], before, sel[:, 1], start=False, stop=True)
            pe.matmul(ps[:, 7, 2 * E:3 * E], ones, sel[:, 0], start=True, stop=False)
            pe.matmul(ps[:, 7, 2 * E:3 * E], ones, sel[:, 1], start=False, stop=True).then_inc(pos_done, 1)

            def gather(k):
                pe.wait_ge(pick_ready, k + 1)
                for f in range(KD):
                    for t in range(QT):
                        ins = pe.matmul(ps[:, 5 + f // 4, f % 4 * P:(f % 4 + 1) * P], bm["tok"][:, t, f * P:(f + 1) * P],
                                        bm["pick"][:, t, :], start=(t == 0), stop=(t == QT - 1))
                ins.then_inc(gathered, 1)

            pe.wait_ge(back_ev, 8)
            gather(0)
            pe.wait_ge(routed, 1)
            units = pe.value_load(bm["unit_i"][0:1, 15:16], min_val=E, max_val=MAX_UNITS)
            with pe.Fori(0, units) as u:
                gh, gl = bm["gh"], bm["gl"]

                def up(i, kind):
                    j, bank = at[kind, i], 0 if kind == "g" else 1
                    high, low = wh[:, j % 2, :], wl[:, j % 2, :]
                    if i:
                        pe.wait_ge(esil_ready if kind == "g" else eprod_ready, u * FC + i)
                    pe.wait_ge(wh_ready, u * CPU + C_MOE + j + 1)
                    for k in range(KD):
                        w, s = high[:, k * WIDE:(k + 1) * WIDE], slice(k * P, (k + 1) * P)
                        pe.matmul(ps[:, bank, :], gh[:, s], w, start=(k == 0), stop=False)
                        ins = pe.matmul(ps[:, bank, :], gl[:, s], w, start=False, stop=False)
                    ins.then_inc(wh_used, 1)
                    pe.wait_ge(wl_ready, u * CPU + C_MOE + j + 1)
                    for k in range(KD):
                        s = slice(k * P, (k + 1) * P)
                        ins = pe.matmul(ps[:, bank, :], gh[:, s], low[:, k * WIDE:(k + 1) * WIDE], start=False, stop=(k == KD - 1))
                    ins.then_inc(w_used, 1)

                def down(i):
                    j = at["d", i]
                    high, low = wh[:, j % 2, :], wl[:, j % 2, :]
                    ah, al = bm["ah"], bm["al"]
                    pe.wait_ge(eal_ready, u * FC + i + 1)
                    pe.wait_ge(wh_ready, u * CPU + C_MOE + j + 1)
                    for k in range(4):
                        s = slice(k * P, (k + 1) * P)
                        for h in range(2):
                            w = high[:, k * D + h * BANK:k * D + (h + 1) * BANK]
                            pe.matmul(ps[:, 2 + h, :], ah[:, s], w, start=(i == 0 and k == 0), stop=False)
                            ins = pe.matmul(ps[:, 2 + h, :], al[:, s], w, start=False, stop=False)
                    ins.then_inc(wh_used, 1)
                    pe.wait_ge(wl_ready, u * CPU + C_MOE + j + 1)
                    for k in range(4):
                        s = slice(k * P, (k + 1) * P)
                        for h in range(2):
                            w = low[:, k * D + h * BANK:k * D + (h + 1) * BANK]
                            ins = pe.matmul(ps[:, 2 + h, :], ah[:, s], w, start=False, stop=(i == FC - 1 and k == 3))
                    ins.then_inc(w_used, 1)

                pe.wait_ge(gl_ready, u * 2 + 2)
                for i in range(FC):
                    up(i, "g")
                    up(i, "u")
                    if i >= 1:
                        down(i - 1)
                    pe.wait_ge(eprod_ready, u * FC + i + 1)
                    if i:
                        pe.wait_ge(eal_ready, u * FC + i)
                    else:
                        pe.wait_ge(acc_done, u * 4 + 1)
                    for k in range(4):
                        s = slice(k * P, (k + 1) * P)
                        ins = pe.transpose(ps[:, 4, s], bm["act"][:, s], ident)
                    ins.then_inc(eT_done, 1)
                    if i == 3:
                        pe.wait_ge(pay_ready, u + 1)
                        for t in range(QT):
                            ins = pe.transpose(ps[:, 7, t * P:(t + 1) * P], bm["pay"][:, t, :], ident)
                        ins.then_inc(payT_done, 1)
                gather(u + 1)
                down(FC - 1)
                pe.wait_ge(payT_ev, u + 1)
                pe.wait_ge(y0_ev, u + 1)
                pe.wait_ge(y1_ev, u + 1)
                pe.wait_ge(gl_ready, u * 2 + 4)
                for n in range(4):
                    t, half = n // 2, n % 2
                    pe.matmul(ps[:, (7, 4, 5, 6)[n], :], bm["payT"][:, t * P:(t + 1) * P],
                              bm["y"][:, half * BANK:(half + 1) * BANK], start=True, stop=True).then_inc(sc_done, 1)


_INS = ["x", "meta_tokens", "norm_gains", "sb_w_qkv", "sb_w_o", "diff_w_qkv", "diff_w_o", "diff_subln",
        "diff_lambda_q1", "diff_lambda_k1", "diff_lambda_q2", "diff_lambda_k2", "ffn_w_gate", "ffn_w_up",
        "ffn_w_down", "moe_router", "moe_w_gate", "moe_w_up", "moe_w_down", "final_norm"]


def kernel(**inputs):
    import concourse.bacc as bacc
    from concourse.bass_utils import run_bass_kernel_spmd

    nc = bacc.Bacc("TRN2", target_bir_lowering=False, num_devices=1)
    arrays, args = {}, []
    for name, a in [(n, inputs[n]) for n in _INS] + list(constants().items()):
        a = np.ascontiguousarray(a)
        arrays[f"in_{name}"] = a
        args.append(nc.dram_tensor(f"in_{name}", a.shape, mybir.dt.from_np(a.dtype), kind="ExternalInput").ap())
    args.append(nc.dram_tensor("out", (1, SEQ, D), F32, kind="ExternalOutput").ap())
    build(nc, *args)
    r = run_bass_kernel_spmd(nc, [arrays], core_ids=[0])
    return np.asarray(r.results[0]["out"])
```

```python
import math
from contextlib import ExitStack

import numpy as np

import concourse.bass as bass
from concourse import mybir

F32 = mybir.dt.float32
F32R = mybir.dt.float32r
I32 = mybir.dt.int32
ALU = mybir.AluOpType
ACT = mybir.ActivationFunctionType
AX_X = mybir.AxisListType.X

P = 128
D = 1024
KD = D // P
META = 16
SEQ = 256
L = META + SEQ
HD = 64
SB_HEADS = D // HD
DIFF_HEADS = D // (2 * HD)
FF = 2816
NF = FF // P
E = 8
FE = 3584
EPS = 1e-6
LAMBDA_INIT = 0.8 - 0.6 * math.exp(-0.3)
SCALE = HD ** -0.5
MASKED = -1e30

CHUNK = 4096
WIDE = CHUNK // KD
HALF = WIDE // P * P
QT = SEQ // P
BANK = 512

KT2 = (2 * P, 0, L - 2 * P)
KT0 = (0, KT2[1] + KT2[2], L)
KT1 = (P, KT0[1] + KT0[2], L - P)
KEY_TILES = (KT0, KT1, KT2)
SCW = KT1[1] + KT1[2]
KEEP2 = SCW + P
KEEPW = KEEP2 + KT2[2]

C_SB_QKV = 0
C_SB_O = 6
C_UP = 8
N_UP = -(-FF // WIDE)
C_DOWN = C_UP + 2 * N_UP
N_DOWN = -(-NF // 4)
C_D_QKV = C_DOWN + N_DOWN
C_D_O = C_D_QKV + 6
C_MOE = C_D_O + 2
FC = FE // WIDE
CPU = 3 * FC
PIECES = CPU + 1
MAX_UNITS = E + 3

LOG_EXP = "natural_log_exp_and_others"
SILU = "silu_and_others"


def up_tiles(i):
    return min(4, NF - 4 * i)


def constants():
    r = np.arange(P)
    ident = np.eye(P, dtype=np.float32)
    from_here = (r[:, None] >= r[None, :]).astype(np.float32)
    ones = np.ones((P, P), np.float32)
    before = (r[:, None] < r[None, :]).astype(np.float32)
    keep = np.zeros((P, SCW), np.float32)
    for first, col, width in KEY_TILES:
        key = first + r[:, None]
        query = first + np.arange(width)[None, :]
        keep[:, col:col + width] = key < query
    neg_keep = -keep
    strict_bias = np.where(keep > 0, np.float32(0), np.float32(MASKED)).astype(np.float32)
    causal_bias = np.zeros((P, L), np.float32)
    causal_bias[:, L - P:] = np.where(r[None, :] <= r[:, None], 0.0, MASKED)
    swap = np.zeros((P, P), np.float32)
    swap[r, r ^ 32] = 1.0
    inv = (np.float32(10000.0) ** (-np.arange(0, HD, 2, dtype=np.float32) / np.float32(HD))).astype(np.float32)
    ang = np.arange(L, dtype=np.float32)[None, :] * inv[r % 32][:, None]
    cos = np.cos(ang).astype(np.float32)
    sin = (np.sin(ang) * np.where(r % HD < 32, -1.0, 1.0)[:, None]).astype(np.float32)
    slots = np.broadcast_to(np.arange(1, P + 1, dtype=np.float32), (P, P))
    desc = np.broadcast_to(np.arange(E, 0, -1, dtype=np.float32), (P, E))
    return {
        "c_base": np.concatenate([ident, from_here, ones], 1),
        "c_neg_keep": neg_keep.astype(np.float32),
        "c_bias": strict_bias,
        "c_diff": np.concatenate([causal_bias, swap, cos, sin], 1).astype(np.float32),
        "c_route": np.concatenate([before, slots, desc, E - desc], 1).astype(np.float32),
    }


def build(nc, x, meta, gains, sb_qkv, sb_o, d_qkv, d_o, subln, lq1, lk1, lq2, lk2,
          ffn_gate, ffn_up, ffn_down, router, moe_gate, moe_up, moe_down, final_norm,
          c_base, c_neg_keep, c_bias, c_diff, c_route, out):
    ctx = ExitStack()
    with ctx:
        def sb(name, shape, dt=F32, where=ctx):
            return where.enter_context(nc.sbuf_tensor(name, shape, dt))

        def sem(name):
            return ctx.enter_context(nc.semaphore(name))

        ps = ctx.enter_context(nc.psum_tensor("ps", [P, 8, BANK], F32))

        raw = sb("raw", [P, 3, CHUNK])
        wh = sb("wh", [P, 2, CHUNK], F32R)
        wl = sb("wl", [P, 2, CHUNK], F32R)
        hT = sb("hT", [P, KD, L])
        xn = sb("xn", [P, KD * L])
        base = sb("base", [P, 3 * P])
        ident, from_here, ones = (base[:, i * P:(i + 1) * P] for i in range(3))
        sums_r = sb("sums_r", [P, 2 * P], F32R)
        rs = sb("rs", [P, L])
        var = sb("var", [P, L])
        rsT = sb("rsT", [P, 3])
        vecs = sb("vecs", [P, 48])
        eps = sb("eps", [P, 1])
        small = sb("small", [P, 16])
        neg_lam = sb("neg_lam", [P, 1])
        gsub = sb("gsub", [P, 1])
        xn3 = xn[:].rearrange("p (k t) -> p k t", t=L)
        nd = DIFF_HEADS * SEQ

        def phase(make):
            with ExitStack() as own:
                return make(own)

        def parts(own):
            return (sb("xh", [P, KD * L + P - META], F32R, where=own),
                    sb("xl", [P, KD * L + P - META], F32R, where=own))

        def heads0(own):
            return {"soft": sb("soft", [P, 2, SCW], where=own), "keep_h": sb("keep_h", [P, 2, KEEPW], F32R, where=own), "keep_l": sb("keep_l", [P, 2, KEEPW], F32R, where=own),
                    "att": sb("att", [P, 2, SCW], where=own), "bias": sb("bias", [P, SCW], where=own)}

        def heads1(own):
            return {"probs": sb("probs", [P, 2, 4, L], where=own), "wT": sb("wT", [P, 2, 3 * P + SEQ], where=own),
                    "sq": sb("head_sq", [P, 2, SEQ], where=own), "o": sb("head_o", [P, 2, SEQ], where=own)}

        def layer0(own):
            return {"q": sb("q0", [P, KD, L], where=own), "k": sb("k0", [P, KD * L + P - META], where=own),
                    "v": sb("v0", [P, 3, D], where=own),
                    "oh": sb("oh0", [P, KD * L], F32R, where=own), "ol": sb("ol0", [P, KD * L], F32R, where=own),
                    "neg_keep": sb("neg_keep", [P, SCW], where=own), "vec_rows": sb("vec_rows", [48, P], where=own)}

        def feed_forward(own):
            return {"ah": sb("ah", [P, NF, L], F32R, where=own), "al": sb("al", [P, NF, L], F32R, where=own)}

        def layer1(own):
            return {"q": sb("q1", [P, nd], where=own), "k": sb("k1", [P, KD * L], where=own),
                    "v": sb("v1", [P, 3, D], where=own),
                    "oh": sb("oh1", [P, nd], F32R, where=own), "ol": sb("ol1", [P, nd], F32R, where=own),
                    "con": sb("con", [P, L + P + 2 * L], where=own), "stat": sb("stat", [P, 2, 16], where=own)}

        def experts(own):
            b = {}
            for name, shape in (("tok", [P, QT, D]), ("acc", [P, QT, D]), ("pick", [P, QT, P]), ("pay", [P, QT, P]),
                                ("payT", [P, SEQ]), ("sil", [P, BANK]), ("act", [P, BANK]), ("y", [P, D]),
                                ("rcon", [P, 2 * P + 2 * E]), ("wr", [P, KD, E]), ("r", [P, 10, QT, E]),
                                ("one", [P, 8, QT]), ("pos", [P, QT, 12]), ("gate", [P, QT, 12]),
                                ("over", [P, 20, E]), ("unit_f", [P, 16])):
                b[name] = sb(name, shape, where=own)
            for name, width in (("gh", KD * P), ("gl", KD * P), ("eah", BANK), ("eal", BANK)):
                b[name] = sb(name, [P, width], F32R, where=own)
            b["unit_i"] = sb("unit_i", [1, 16], I32, where=own)
            return b

        xh, xl = phase(parts)
        h0, h1 = phase(heads0), phase(heads1)
        sq3 = phase(lambda own: sb("sq3", [P, KD, L], where=own))
        sb("overlay", [P, 2 * (KD * L + P - META)])
        b0, bf, b1, bm = phase(layer0), phase(feed_forward), phase(layer1), phase(experts)
        tokens_in, vec_rows = b0["v"], b0["vec_rows"]

        raw_landed = [sem(f"raw_landed{i}") for i in range(3)]
        wh_ready, wl_ready = sem("wh_ready"), sem("wl_ready")
        wh_used, w_used = sem("wh_used"), sem("w_used")
        base_in, keep_in, bias_in = sem("base_in"), sem("keep_in"), sem("bias_in")
        diff_in, route_in = sem("diff_in"), sem("route_in")
        x_in, vec_in, gain_in, rows_zero, stores = sem("x_in"), sem("vec_in"), sem("gain_in"), sem("rows_zero"), sem("stores")
        pads, turned, turned_act, turned_dve = sem("pads"), sem("turned"), sem("turned_act"), sem("turned_dve")
        vec_turned, vec_ev, lam_sum, lam_exp = sem("vec_turned"), sem("vec_ev"), sem("lam_sum"), sem("lam_exp")
        dve_step, act_step = sem("dve_step"), sem("act_step")
        residual, squared, summed, rooted = sem("residual"), sem("squared"), sem("summed"), sem("rooted")
        rs_ready, rs_turned, rsT_ready = sem("rs_ready"), sem("rs_turned"), sem("rsT_ready")
        xh_ready, xl_ready, gained = sem("xh_ready"), sem("xl_ready"), sem("gained")
        tile_done, tile_ev = sem("tile_done"), sem("tile_ev")
        v_done, v_ev = sem("v_done"), sem("v_ev")
        add_done = sem("add_done")
        lam_sum_in, pv_done, ds_free, fin_rec = sem("lam_sum_in"), sem("pv_done"), sem("ds_free"), sem("fin_rec")
        score_done, abs_done, soft_done, keep_ready = sem("score_done"), sem("abs_done"), sem("soft_done"), sem("keep_ready")
        sums_ready, masked, kh_ready, gap_zero = sem("sums_ready"), sem("masked"), sem("kh_ready"), sem("gap_zero")
        log_done, expo_ready, att_ready = sem("log_done"), sem("expo_ready"), sem("att_ready")
        oh_ready, ol_ready = sem("oh_ready"), sem("ol_ready")
        g_done, sil_ready, u_done, prod_ready = sem("g_done"), sem("sil_ready"), sem("u_done"), sem("prod_ready")
        ah_ready, al_ready, g_free, sil_scaled = sem("ah_ready"), sem("al_ready"), sem("g_free"), sem("sil_scaled")
        swap_done, rope_done = sem("swap_done"), sem("rope_done")
        ds_done, max_ready, probs_ready, mix_ready = sem("ds_done"), sem("max_ready"), sem("probs_ready"), sem("mix_ready")
        wt_done, wt_ev_a, wt_ev_m, do_done, do_ev = sem("wt_done"), sem("wt_ev_a"), sem("wt_ev_m"), sem("do_done"), sem("do_ev")
        sub_sum, sub_root, sub_ready = sem("sub_sum"), sem("sub_root"), sem("sub_ready")
        logit_done, back_done, back_ev = sem("logit_done"), sem("back_done"), sem("back_ev")
        gap_ready, gap_exp, sel_ready, pos_done, routed = sem("gap_ready"), sem("gap_exp"), sem("sel_ready"), sem("pos_done"), sem("routed")
        pick_ready, gathered, gh_ready, gl_ready = sem("pick_ready"), sem("gathered"), sem("gh_ready"), sem("gl_ready")
        esil_ready, eprod_ready = sem("esil_ready"), sem("eprod_ready")
        eT_done, eah_ready, eal_ready = sem("eT_done"), sem("eah_ready"), sem("eal_ready")
        pay_ready, payT_done, payT_ev = sem("pay_ready"), sem("payT_done"), sem("payT_ev")
        y_ev, sc_done, acc_done = sem("y_ev"), sem("sc_done"), sem("acc_done")
        fin_sq, fin_root, fin_ready = sem("fin_sq"), sem("fin_root"), sem("fin_ready")

        def cols(w, i):
            return w[:, WIDE * i:min(WIDE * (i + 1), w.shape[1])].rearrange("(k p) n -> p k n", p=P)

        def rows(w, i):
            return w[WIDE * i:min(WIDE * (i + 1), w.shape[0]), :].rearrange("(k p) n -> p k n", p=P)

        sources = [cols(sb_qkv[0], i) for i in range(6)] + [cols(sb_o[0], i) for i in range(2)]
        for i in range(N_UP):
            sources += [cols(ffn_gate[0], i), cols(ffn_up[0], i)]
        sources += [rows(ffn_down[0], i) for i in range(N_DOWN)]
        sources += [cols(d_qkv[0], i) for i in range(6)] + [cols(d_o[0], i) for i in range(2)]
        assert len(sources) == C_MOE
        size = [s.shape[1] * s.shape[2] for s in sources] + [CHUNK] * 4
        weights_of = {"g": moe_gate.rearrange("a e k n -> (a e k) n"), "u": moe_up.rearrange("a e k n -> (a e k) n"),
                      "d": moe_down.rearrange("a e k n -> (a e k) n")}
        unit_chunks = [("g", 0), ("u", 0)]
        for i in range(1, FC):
            unit_chunks += [("g", i), ("u", i), ("d", i - 1)]
        unit_chunks += [("d", FC - 1)]
        at = {c: j for j, c in enumerate(unit_chunks)}

        def piece(p):
            if p < CPU - 1:
                return (C_MOE + p) % 3, 0, CHUNK
            return (C_MOE + CPU - 1) % 3, (p - CPU + 1) * (CHUNK // 2), CHUNK // 2

        def raw_f(w):
            return w.bitcast(F32)

        def await_tile(eng, done, before, c, m, tiles):
            if m == tiles - 1:
                eng.wait_ge(w_used, c + 1)
            else:
                eng.wait_ge(done, before + m + 1)

        def tile_signal(ins, done, m, tiles):
            ins.then_inc(w_used if m == tiles - 1 else done, 1)

        block = ctx.enter_context(nc.Block())

        @block.sync
        def _(sp):
            sp.dma_start(tokens_in[0:META, 0, :], meta).then_inc(x_in, 16)
            sp.dma_start(tokens_in[META:P, 0, :], x[0, 0:P - META]).then_inc(x_in, 16)
            sp.dma_start(tokens_in[:, 1, :], x[0, P - META:2 * P - META]).then_inc(x_in, 16)
            sp.dma_start(tokens_in[0:META, 2, :], x[0, 2 * P - META:SEQ]).then_inc(x_in, 16)

            for c, src in enumerate(sources):
                if c >= 3:
                    sp.wait_ge(wl_ready, c - 2)
                dst = raw[:, c % 3, 0:size[c]].rearrange("p (k n) -> p k n", n=src.shape[2])
                sp.dma_start(dst, src).then_inc(raw_landed[c % 3], 16)

            def load_unit(u, e, first=False):
                for j, (kind, i) in enumerate(unit_chunks):
                    slot = (C_MOE + j) % 3
                    sp.wait_ge(wl_ready, u * PIECES + C_MOE + j - (2 if first or j >= 2 else 3))
                    w = weights_of[kind]
                    if kind == "d":
                        src = w[bass.ds(e * FE + WIDE * i, WIDE), :]
                    else:
                        src = w[bass.ds(e * D, D), WIDE * i:WIDE * (i + 1)]
                    src = src.rearrange("(k p) n -> p k n", p=P)
                    dst = raw[:, slot, :].rearrange("p (k n) -> p k n", n=src.shape[2])
                    sp.dma_start(dst, src).then_inc(raw_landed[slot], 16)

            load_unit(0, 0, first=True)
            with sp.Fori(1, E) as u:
                load_unit(u, u)
            sp.wait_ge(routed, 1)
            units = sp.value_load(bm["unit_i"][0:1, 15:16], min_val=E, max_val=MAX_UNITS)
            with sp.If(units > E):
                with sp.Fori(E, units) as u:
                    e = sp.value_load(bm["unit_i"][0:1, bass.ds(u, 1)], min_val=0, max_val=E - 1)
                    load_unit(u, e)

            for t in range(QT):
                sp.wait_ge(fin_ready, t + 1)
                sp.dma_start(out[0, t * P:(t + 1) * P], bm["tok"][:, t, :]).then_inc(stores, 16)
            sp.wait_ge(stores, 16 * QT)

        @block.gpsimd
        def _(pool):
            pool.dma_start(base[:], c_base).then_inc(base_in, 16)
            pool.wait_ge(rows_zero, 1)
            pool.dma_start(vec_rows[0:32, :], gains.rearrange("a b (k p) -> (a b k) p", p=P)).then_inc(vec_in, 16)
            pool.dma_start(vec_rows[32:33, :], subln).then_inc(vec_in, 16)
            for n, v in enumerate((lq1, lk1, lq2, lk2)):
                pool.dma_start(vec_rows[33 + n:34 + n, 0:HD], v).then_inc(vec_in, 16)
            pool.dma_start(b0["neg_keep"][:], c_neg_keep).then_inc(keep_in, 16)
            pool.wait_ge(w_used, C_SB_O)
            pool.dma_start(h0["bias"][:], c_bias).then_inc(bias_in, 16)
            pool.wait_ge(w_used, C_D_QKV)
            pool.dma_start(b1["con"][:], c_diff).then_inc(diff_in, 16)
            pool.wait_ge(w_used, C_MOE)
            pool.dma_start(bm["rcon"][:], c_route).then_inc(route_in, 16)
            pool.dma_start(bm["wr"][:], router[0].rearrange("(k p) e -> p k e", p=P)).then_inc(route_in, 16)
            pool.wait_ge(logit_done, 1)
            pool.wait_ge(back_done, 4)
            pool.dma_start(xn[:, 0:D], final_norm[None, :].to_broadcast([P, D])).then_inc(gain_in, 16)

        @block.scalar
        def _(act):
            def split_high(c):
                act.wait_ge(raw_landed[c % 3], 16 * (c // 3 + 1))
                if c >= 2:
                    act.wait_ge(wh_used, c - 1)
                    act.wait_ge(wl_ready, c - 1)
                n = size[c]
                act.copy(wh[:, c % 2, 0:n], raw[:, c % 3, 0:n]).then_inc(wh_ready, 1)

            def a_step(ins):
                act_steps[0] += 1
                ins.then_inc(act_step, 1)
                act.wait_ge(act_step, act_steps[0])

            act_steps = [0]

            def gained_high(n, k):
                act.activation(xh[:, k * L:(k + 1) * L], hT[:, k, :], ACT.Identity,
                               scale=vecs[:, n * KD + k:n * KD + k + 1]).then_inc(xh_ready, 1)

            def square(n, k):
                act.activation(sq3[:, k, :] if n == 3 else xn3[:, k, :], hT[:, k, :], ACT.Square).then_inc(squared, 1)

            def root(n):
                act.wait_ge(summed, n + 1)
                a_step(act.activation(var[:], ps[:, 7, 0:L], ACT.Identity, bias=eps[:, 0:1], scale=1.0 / D))
                a_step(act.activation(rs[:], var[:], ACT.Ln))
                act.activation(rs[:], rs[:], ACT.Exp, scale=-0.5).then_inc(rooted, 1)

            def turn_root(n):
                act.wait_ge(rs_turned, n)
                for t in range(3 if n < 3 else 2):
                    w = META if (n, t) == (1, 2) else P
                    ins = act.copy(rsT[0:w, t:t + 1], ps[0:w, 6, 32 * t:32 * t + 1])
                ins.then_inc(rsT_ready, 1)
                act.wait_ge(rsT_ready, n)

            act.preload_act_table_set(LOG_EXP)
            act.wait_ge(base_in, 16)
            act.copy(sums_r[:], base[:, P:3 * P]).then_inc(sums_ready, 1)
            for n in (0, 2, 3, 5):
                g, t = n // 3, n % 3
                w = P if t < 2 else META
                act.wait_ge(turned, n + 1)
                src = ps[:, n, 0:4 * w].rearrange("p (k t) -> p k t", t=w)
                act.copy(hT[:, 4 * g:4 * g + 4, t * P:t * P + w], src).then_inc(turned_act, 1)
            act.wait_ge(vec_turned, 1)
            act.copy(vecs[:], ps[:, 6, 0:48]).then_inc(vec_ev, 1)
            act.wait_ge(vec_ev, 1)
            for k in range(KD):
                if k % 4 == 0:
                    act.wait_ge(turned_act, 2 + k // 2)
                    act.wait_ge(turned_dve, 1 + k // 4)
                gained_high(0, k)
            split_high(0)
            for k in range(KD):
                square(0, k)
            split_high(1)
            root(0)
            act.wait_ge(lam_sum, 1)
            act.activation(small[:, 2:4], ps[:, 5, 0:2], ACT.Exp).then_inc(lam_exp, 1)
            for c in range(4):
                if c == 2:
                    turn_root(1)
                split_high(c + 2)
            for c in range(4, 6):
                for t in range(3):
                    vi = 3 * (c - 4) + t
                    await_tile(act, v_done, 2 * (c - 4), c, t, 3)
                    act.mul(b0["v"][:, t, (c - 4) * BANK:(c - 3) * BANK], ps[:, 4 + vi % 4, :],
                            rsT[:, t:t + 1]).then_inc(v_ev, 1)
                split_high(c + 2)

            for n in range(SB_HEADS + 4):
                m = n - 1
                if 0 <= m < SB_HEADS:
                    act.wait_ge(masked, m + 1)
                    if m >= 2:
                        act.wait_ge(soft_done, m - 1)
                    a, kh = h0["soft"][:, m % 2, :], h0["keep_h"][:, m % 2, :]
                    act.copy(kh[:, 0:SCW], a)
                    act.copy(kh[:, KEEP2:KEEPW], a[:, 0:KT2[2]]).then_inc(kh_ready, 1)
                if n < SB_HEADS:
                    a = h0["soft"][:, n % 2, :]
                    act.wait_ge(score_done, n + 1)
                    if n >= 2:
                        act.wait_ge(keep_ready, n - 1)
                    act.activation(a, ps[:, n % 4, 0:SCW], ACT.Abs).then_inc(abs_done, 1)
                    act.wait_ge(abs_done, 2 * n + 1)
                    act.activation(a, a, ACT.Exp, scale=-1.0).then_inc(abs_done, 1)
                    act.wait_ge(abs_done, 2 * n + 2)
                    act.activation(a, a, ACT.Ln, bias=1.0).then_inc(log_done, 1)
                m = n - 2
                if 0 <= m < SB_HEADS:
                    act.wait_ge(expo_ready, m + 1)
                    a = h0["att"][:, m % 2, :]
                    act.activation(a, a, ACT.Exp).then_inc(att_ready, 1)
                m = n - 4
                if 0 <= m < SB_HEADS and m % 2 == 1:
                    i = m // 2
                    act.wait_ge(pv_done, 2 * i + 2)
                    act.copy(b0["oh"][:, i * L:(i + 1) * L], ps[:, 4 + i % 2, 0:L]).then_inc(oh_ready, 1)

            def residual_tile(n, k):
                act.wait_ge(residual, KD * (n - 1) + k + 1)
                gained_high(n, k)
                square(n, k)

            for c in range(C_SB_O, C_SB_O + 2):
                for k in range(4 * (c - C_SB_O), 4 * (c - C_SB_O) + 4):
                    residual_tile(1, k)
                split_high(c + 2)

            root(1)
            for i in range(N_UP):
                for f in range(4 * i, 4 * i + up_tiles(i)):
                    act.wait_ge(g_free, f + 1)
                    act.activation(xn3[:, f % 8, :], xn3[:, f % 8, :], ACT.Silu).then_inc(sil_ready, 1)
                split_high(C_UP + 2 * i + 2)
                for f in range(4 * i, 4 * i + up_tiles(i)):
                    act.wait_ge(prod_ready, f + 1)
                    act.copy(bf["ah"][:, f, :], xn3[:, f % 8, :]).then_inc(ah_ready, 1)
                split_high(C_UP + 2 * i + 3)
            act.preload_act_table_set(LOG_EXP)
            for i in range(N_DOWN):
                if i == N_DOWN - 1:
                    for k in range(KD):
                        residual_tile(2, k)
                split_high(C_DOWN + i + 2)

            root(2)
            for c in range(4):
                if c == 2:
                    turn_root(2)
                split_high(C_D_QKV + c + 2)
            for c in range(4, 6):
                for t in range(3):
                    vi = 3 * (c - 4) + t
                    await_tile(act, v_done, 4 + 2 * (c - 4), C_D_QKV + c, t, 3)
                    act.mul(b1["v"][:, t, (c - 4) * BANK:(c - 3) * BANK], ps[:, vi % 4, :],
                            rsT[:, t:t + 1]).then_inc(v_ev, 1)
                split_high(C_D_QKV + c + 2)

            for n in range(DIFF_HEADS + 4):
                if n < DIFF_HEADS:
                    act.wait_ge(max_ready, n + 1)
                    st = b1["stat"][:, n % 2, :]
                    for j in range(4):
                        w = P + META if j < 2 else L
                        pr = h1["probs"][:, n % 2, j, 0:w]
                        act.activation(pr, pr, ACT.Exp, bias=st[:, 4 + j:5 + j],
                                       accum_out=st[:, 8 + j:9 + j]).then_inc(probs_ready, 1)
                m = n - 2
                if 0 <= m < DIFF_HEADS:
                    act.wait_ge(wt_done, m + 1)
                    if m >= 2:
                        act.wait_ge(do_done, m - 1)
                    act.copy(h1["wT"][:, m % 2, 0:3 * P], ps[:, 4, 0:3 * P]).then_inc(wt_ev_a, 1)
                m = n - 4
                if 0 <= m < DIFF_HEADS:
                    r_ = h1["sq"][:, m % 2, :]
                    act.wait_ge(sub_sum, m + 1)
                    a_step(act.activation(r_, ps[:, 5, 0:SEQ], ACT.Ln, bias=eps[:, 0:1], scale=1.0 / (2 * HD)))
                    act.activation(r_, r_, ACT.Exp, scale=-0.5).then_inc(sub_root, 1)
                m = n - 3
                if 0 <= m < DIFF_HEADS:
                    act.wait_ge(do_done, m + 1)
                    if m >= 2:
                        act.wait_ge(ol_ready, KD + m - 1)
                    act.copy(h1["o"][:, m % 2, :], ps[:, 7, 0:SEQ]).then_inc(do_ev, 1)
                    act.activation(h1["sq"][:, m % 2, :], ps[:, 7, 0:SEQ], ACT.Square).then_inc(do_ev, 1)
                m = n - 4
                if 0 <= m < DIFF_HEADS:
                    act.wait_ge(sub_ready, m + 1)
                    act.copy(b1["oh"][:, m * SEQ:(m + 1) * SEQ], h1["o"][:, m % 2, :]).then_inc(oh_ready, 1)

            for c in range(C_D_O, C_D_O + 2):
                for k in range(4 * (c - C_D_O), 4 * (c - C_D_O) + 4):
                    act.wait_ge(residual, 2 * KD + k + 1)
                    act.activation(xn3[:, k, :], hT[:, k, :], ACT.Identity,
                                   scale=vecs[:, 3 * KD + k:3 * KD + k + 1]).then_inc(gained, 1)
                    square(3, k)
            root(3)

            def unit_split(u, p):
                j = min(p, CPU - 1)
                slot, s, to = piece(p)
                act.wait_ge(raw_landed[slot], u * (16 * FC) + 16 * ((C_MOE + j) // 3 + 1))
                act.wait_ge(wh_used, u * PIECES + C_MOE + p - 1)
                act.wait_ge(wl_ready, u * PIECES + C_MOE + p - 1)
                act.copy(wh[:, p % 2, 0:to], raw[:, slot, s:s + to]).then_inc(wh_ready, 1)

            unit_split(0, 0)
            turn_root(3)
            for n in range(4):
                act.wait_ge(back_done, n + 1)
                act.mul(bm["tok"][:, n // 2, n % 2 * BANK:(n % 2 + 1) * BANK], ps[:, 1 + n, :],
                        rsT[:, n // 2:n // 2 + 1]).then_inc(back_ev, 1)
            act.wait_ge(gap_ready, 1)
            act.activation(bm["one"][:, 5, :], bm["one"][:, 4, :], ACT.Exp).then_inc(gap_exp, 1)
            for n in range(4, 8):
                act.wait_ge(back_done, n + 1)
                act.copy(bm["acc"][:, n % 4 // 2, n % 2 * BANK:(n % 2 + 1) * BANK], ps[:, 1 + n % 4, :]).then_inc(back_ev, 1)
            act.preload_act_table_set(SILU)
            unit_split(0, 1)

            def gathered_high():
                for h in range(2):
                    s = slice(h * BANK, (h + 1) * BANK)
                    act.copy(bm["gh"][:, s], ps[:, 5 + h, :]).then_inc(gh_ready, 1)

            act.wait_ge(gathered, 1)
            gathered_high()
            act.wait_ge(routed, 1)
            units = act.value_load(bm["unit_i"][0:1, 15:16], min_val=E, max_val=MAX_UNITS)

            with act.Fori(0, units) as u:
                def turned_high(i):
                    act.wait_ge(eT_done, u * FC + i + 1)
                    act.copy(bm["eah"][:], ps[:, 4, :]).then_inc(eah_ready, 1)

                with act.If(u > 0):
                    unit_split(u, 0)
                    unit_split(u, 1)
                for j, (kind, i) in enumerate(unit_chunks):
                    if j + 2 < PIECES:
                        unit_split(u, j + 2)
                    if kind == "g":
                        act.wait_ge(w_used, u * PIECES + C_MOE + j + 1)
                        if i:
                            act.wait_ge(eprod_ready, u * FC + i)
                        act.activation(bm["sil"][:], ps[:, 0, :], ACT.Silu).then_inc(esil_ready, 1)
                    if (kind, i) == ("u", 0):
                        turned_high(0)
                    if kind == "d" and i + 1 < FC:
                        turned_high(i + 1)
                        if i + 1 == 3:
                            act.wait_ge(payT_done, u + 1)
                            act.copy(bm["payT"][:], ps[:, 7, 0:SEQ]).then_inc(payT_ev, 1)
                        if i + 1 == FC - 1:
                            act.wait_ge(gathered, u + 2)
                            gathered_high()

            for t in range(QT):
                act.wait_ge(acc_done, units * 4 + 1)
                act.activation(bm["tok"][:, t, :], bm["acc"][:, t, :], ACT.Square,
                               accum_out=small[:, 4 + t:5 + t]).then_inc(fin_sq, 1)
            act.wait_ge(fin_sq, QT)
            act.activation(small[:, 6:8], small[:, 4:6], ACT.Sqrt, bias=eps[:, 0:1], scale=1.0 / D).then_inc(fin_root, 1)

        @block.vector
        def _(dve):
            steps = [0]

            def step(ins):
                steps[0] += 1
                ins.then_inc(dve_step, 1)
                dve.wait_ge(dve_step, steps[0])

            def split_low(c):
                dve.wait_ge(wh_ready, c + 1)
                if c >= 2:
                    dve.wait_ge(w_used, c - 1)
                n = size[c]
                dve.tensor_tensor(wl[:, c % 2, 0:n], raw[:, c % 3, 0:n], raw_f(wh[:, c % 2, 0:n]),
                                  ALU.subtract).then_inc(wl_ready, 1)

            def gained_low(n, k):
                dve.wait_ge(xh_ready, KD * n + k + 1)
                s = slice(k * L, (k + 1) * L)
                dve.scalar_tensor_tensor(out=xl[:, s], in0=hT[:, k, :], scalar=vecs[:, n * KD + k:n * KD + k + 1],
                                         in1=raw_f(xh[:, s]), op0=ALU.mult, op1=ALU.subtract).then_inc(xl_ready, 1)

            def polish(n):
                dve.wait_ge(rooted, n + 1)
                step(dve.scalar_tensor_tensor(out=var[:], in0=var[:], scalar=-0.5, in1=rs[:], op0=ALU.mult, op1=ALU.mult))
                step(dve.tensor_tensor(var[:], var[:], rs[:], ALU.mult))
                dve.scalar_tensor_tensor(out=rs[:], in0=var[:], scalar=1.5, in1=rs[:], op0=ALU.add,
                                         op1=ALU.mult).then_inc(rs_ready, 1)
                dve.wait_ge(rs_ready, n + 1)

            def feed_low(f):
                dve.wait_ge(ah_ready, f + 1)
                dve.tensor_tensor(bf["al"][:, f, :], xn3[:, f % 8, :], raw_f(bf["ah"][:, f, :]),
                                  ALU.subtract).then_inc(al_ready, 1)

            def add_tile(n, bank, first):
                dve.tensor_tensor(hT[:, n, first:L], hT[:, n, first:L], ps[:, bank, 0:L - first], ALU.add).then_inc(residual, 1)

            step(dve.memset(vec_rows[:], 0.0))
            dve.nop().then_inc(rows_zero, 1)
            dve.memset(eps[:], EPS).then_inc(pads, 1)
            dve.memset(rsT[:], 1.0).then_inc(pads, 1)
            dve.memset(raw_f(xh[:, KD * L:]), 0.0).then_inc(pads, 1)
            dve.memset(raw_f(xl[:, KD * L:]), 0.0).then_inc(pads, 1)
            dve.memset(b0["k"][:, KD * L:], 0.0).then_inc(pads, 1)
            for n in (1, 4):
                dve.wait_ge(turned, n + 1)
                src = ps[:, n, :].rearrange("p (k t) -> p k t", t=P)
                dve.tensor_copy(hT[:, 4 * (n // 3):4 * (n // 3) + 4, P:2 * P], src).then_inc(turned_dve, 1)
            dve.wait_ge(turned_dve, 2)
            dve.wait_ge(vec_ev, 1)
            for k in range(KD):
                gained_low(0, k)
            split_low(0)
            dve.tensor_tensor(small[:, 0:1], vecs[:, 33:34], vecs[:, 34:35], ALU.mult)
            step(dve.tensor_tensor(small[:, 1:2], vecs[:, 35:36], vecs[:, 36:37], ALU.mult))
            dve.tensor_scalar(gsub[:], vecs[:, 32:33], 1.0 - LAMBDA_INIT, None, ALU.mult).then_inc(lam_sum_in, 1)
            split_low(1)
            polish(0)
            dve.wait_ge(lam_exp, 1)
            step(dve.tensor_tensor(neg_lam[:], small[:, 3:4], small[:, 2:3], ALU.subtract))
            step(dve.tensor_scalar(neg_lam[:], neg_lam[:], LAMBDA_INIT, None, ALU.subtract))

            for c in range(6):
                for m in range(4 if c < 4 else 0):
                    tt = 4 * c + m
                    await_tile(dve, tile_done, 3 * c, c, m, 4)
                    if c < 2:
                        dve.scalar_tensor_tensor(out=b0["q"][:, tt, :], in0=ps[:, tt % 4, 0:L], scalar=SCALE, in1=rs[:],
                                                 op0=ALU.mult, op1=ALU.mult).then_inc(tile_ev, 1)
                    else:
                        dve.tensor_tensor(b0["k"][:, (tt - KD) * L:(tt - KD + 1) * L], ps[:, tt % 4, 0:L], rs[:],
                                          ALU.mult).then_inc(tile_ev, 1)
                split_low(c + 2)

            dve.wait_ge(keep_in, 16)
            dve.wait_ge(bias_in, 16)
            neg_keep, strict_bias = b0["neg_keep"][:], h0["bias"][:]
            for parts_ in (h0["keep_h"], h0["keep_l"]):
                for slot in range(2):
                    ins = dve.memset(raw_f(parts_[:, slot, SCW:KEEP2]), 0.0)
            ins.then_inc(gap_zero, 1)
            for n in range(SB_HEADS + 4):
                m = n - 1
                if 0 <= m < SB_HEADS:
                    dve.wait_ge(kh_ready, m + 1)
                    a, kh, kl = (h0[b_][:, m % 2, :] for b_ in ("soft", "keep_h", "keep_l"))
                    dve.tensor_tensor(kl[:, 0:SCW], a, raw_f(kh[:, 0:SCW]), ALU.subtract)
                    dve.tensor_tensor(kl[:, KEEP2:KEEPW], a[:, 0:KT2[2]], raw_f(kh[:, KEEP2:KEEPW]),
                                      ALU.subtract).then_inc(keep_ready, 1)
                m = n - 2
                if 0 <= m < SB_HEADS:
                    dve.wait_ge(soft_done, m + 1)
                    if m >= 2:
                        dve.wait_ge(pv_done, m - 1)
                    dve.tensor_tensor(h0["att"][:, m % 2, :], ps[:, m % 4, 0:SCW], strict_bias,
                                      ALU.add).then_inc(expo_ready, 1)
                if n < SB_HEADS:
                    a = h0["soft"][:, n % 2, :]
                    dve.wait_ge(log_done, n + 1)
                    step(dve.scalar_tensor_tensor(out=a, in0=ps[:, n % 4, 0:SCW], scalar=0.0, in1=a,
                                                  op0=ALU.max, op1=ALU.add))
                    dve.tensor_tensor(a, a, neg_keep, ALU.mult).then_inc(masked, 1)
                m = n - 4
                if 0 <= m < SB_HEADS and m % 2 == 1:
                    i = m // 2
                    dve.wait_ge(oh_ready, i + 1)
                    s = slice(i * L, (i + 1) * L)
                    dve.tensor_tensor(b0["ol"][:, s], ps[:, 4 + i % 2, 0:L], raw_f(b0["oh"][:, s]), ALU.subtract).then_inc(ol_ready, 1)

            for c in range(C_SB_O, C_SB_O + 2):
                for n in range(4 * (c - C_SB_O), 4 * (c - C_SB_O) + 4):
                    await_tile(dve, add_done, 3 * (c - C_SB_O), c, n % 4, 4)
                    add_tile(n, n % 4, 0)
                    if n:
                        gained_low(1, n - 1)
                if c > C_SB_O:
                    gained_low(1, KD - 1)
                split_low(c + 2)

            polish(1)
            for i in range(N_UP):
                for f in range(4 * i, 4 * i + up_tiles(i)):
                    await_tile(dve, g_done, 3 * i, C_UP + 2 * i, f - 4 * i, up_tiles(i))
                    if f >= 8:
                        dve.wait_ge(al_ready, f - 7)
                    dve.tensor_tensor(xn3[:, f % 8, :], ps[:, f % 4, 0:L], rs[:], ALU.mult).then_inc(g_free, 1)
                split_low(C_UP + 2 * i + 2)
                for f in range(4 * i, 4 * i + up_tiles(i)):
                    dve.wait_ge(sil_ready, f + 1)
                    dve.tensor_tensor(xn3[:, f % 8, :], xn3[:, f % 8, :], rs[:], ALU.mult).then_inc(sil_scaled, 1)
                for f in range(4 * i, 4 * i + up_tiles(i)):
                    await_tile(dve, u_done, 3 * i, C_UP + 2 * i + 1, f - 4 * i, up_tiles(i))
                    dve.wait_ge(sil_scaled, f + 1)
                    dve.tensor_tensor(xn3[:, f % 8, :], xn3[:, f % 8, :], ps[:, 4 + f % 4, 0:L],
                                      ALU.mult).then_inc(prod_ready, 1)
                    if f > 4 * i:
                        feed_low(f - 1)
                feed_low(f)
                split_low(C_UP + 2 * i + 3)
            for i in range(N_DOWN):
                if i == N_DOWN - 1:
                    for n in range(KD):
                        await_tile(dve, add_done, 6, C_DOWN + i, n, KD)
                        add_tile(n, n, 0)
                        if n:
                            gained_low(2, n - 1)
                    gained_low(2, KD - 1)
                split_low(C_DOWN + i + 2)

            polish(2)
            dve.wait_ge(diff_in, 16)
            con = b1["con"]
            causal, swap, cos, sin = con[:, 0:L], con[:, L:L + P], con[:, L + P:2 * L + P], con[:, 2 * L + P:3 * L + P]

            def rotate(tt):
                q = tt < KD
                w, first = (SEQ, META) if q else (L, 0)
                dst = b1["q"][:, tt * SEQ:(tt + 1) * SEQ] if q else b1["k"][:, (tt - KD) * L:(tt - KD + 1) * L]
                src = xn3[:, tt % 8, 0:w]
                dve.wait_ge(swap_done, tt + 1)
                dve.tensor_tensor(dst, ps[:, 4 + tt % 2, 0:w], sin[:, first:L], ALU.mult)
                step(dve.tensor_tensor(src, src, cos[:, first:L], ALU.mult))
                dve.tensor_tensor(dst, dst, src, ALU.add).then_inc(rope_done, 1)

            for c in range(6):
                for m in range(4 if c < 4 else 0):
                    tt = 4 * c + m
                    await_tile(dve, tile_done, 12 + 3 * c, C_D_QKV + c, m, 4)
                    if tt >= 8:
                        dve.wait_ge(rope_done, tt - 7)
                    if c < 2:
                        dve.scalar_tensor_tensor(out=xn3[:, tt % 8, 0:SEQ], in0=ps[:, tt % 4, 0:SEQ], scalar=SCALE,
                                                 in1=rs[:, META:L], op0=ALU.mult, op1=ALU.mult).then_inc(tile_ev, 1)
                    else:
                        dve.tensor_tensor(xn3[:, tt % 8, :], ps[:, tt % 4, 0:L], rs[:], ALU.mult).then_inc(tile_ev, 1)
                    if tt >= 1:
                        rotate(tt - 1)
                if c == 4:
                    rotate(15)
                split_low(C_D_QKV + c + 2)

            for n in range(DIFF_HEADS + 5):
                if n < DIFF_HEADS:
                    st = b1["stat"][:, n % 2, :]
                    if n >= 2:
                        dve.wait_ge(wt_done, n - 1)
                    for comp in range(2):
                        dve.wait_ge(ds_done, 2 * n + comp + 1)
                        for t in range(2):
                            j, c0, w = 2 * t + comp, t * (P + META), P + META if t == 0 else L
                            ins = dve.tensor_tensor_reduce(
                                h1["probs"][:, n % 2, j, 0:w], ps[:, (2 * n + comp) % 4, c0:c0 + w],
                                causal[:, L - w:L], 1.0, -3e38, ALU.add, ALU.max, st[:, j:j + 1])
                        ins.then_inc(ds_free, 1)
                    dve.wait_ge(ds_free, 2 * n + 2)
                    dve.tensor_scalar(st[:, 4:8], st[:, 0:4], -1.0, None, ALU.mult).then_inc(max_ready, 1)
                m = n - 1
                if 0 <= m < DIFF_HEADS:
                    st = b1["stat"][:, m % 2, :]
                    dve.wait_ge(probs_ready, 4 * m + 4)
                    step(dve.reciprocal(st[:, 8:12], st[:, 8:12]))
                    step(dve.tensor_scalar(st[:, 12:14], st[:, 9:12:2], neg_lam[:, 0:1], None, ALU.mult))
                    for t in range(2):
                        w = P + META if t == 0 else L
                        p1, p2 = h1["probs"][:, m % 2, 2 * t, 0:w], h1["probs"][:, m % 2, 2 * t + 1, 0:w]
                        step(dve.tensor_scalar(p1, p1, st[:, 8 + 2 * t:9 + 2 * t], None, ALU.mult))
                        dve.scalar_tensor_tensor(out=p1, in0=p2, scalar=st[:, 12 + t:13 + t], in1=p1,
                                                 op0=ALU.mult, op1=ALU.add).then_inc(mix_ready, 1)
                m = n - 2
                if 0 <= m < DIFF_HEADS:
                    dve.wait_ge(wt_done, m + 1)
                    if m >= 2:
                        dve.wait_ge(do_done, m - 1)
                    dve.tensor_copy(h1["wT"][0:META, m % 2, 3 * P:], ps[0:META, 6, 0:SEQ]).then_inc(wt_ev_m, 1)
                m = n - 4
                if 0 <= m < DIFF_HEADS:
                    o_ = h1["o"][:, m % 2, :]
                    dve.wait_ge(sub_root, m + 1)
                    dve.scalar_tensor_tensor(out=o_, in0=o_, scalar=gsub[:, 0:1], in1=h1["sq"][:, m % 2, :],
                                             op0=ALU.mult, op1=ALU.mult).then_inc(sub_ready, 1)
                    s = slice(m * SEQ, (m + 1) * SEQ)
                    dve.wait_ge(oh_ready, KD + m + 1)
                    dve.tensor_tensor(b1["ol"][:, s], o_, raw_f(b1["oh"][:, s]), ALU.subtract).then_inc(ol_ready, 1)
            for c in range(C_D_O, C_D_O + 2):
                for n in range(4 * (c - C_D_O), 4 * (c - C_D_O) + 4):
                    await_tile(dve, add_done, 13 + 3 * (c - C_D_O), c, n % 4, 4)
                    add_tile(n, n % 4, META)
            polish(3)

            def unit_split(u, p):
                slot, s, to = piece(p)
                dve.wait_ge(wh_ready, u * PIECES + C_MOE + p + 1)
                dve.wait_ge(w_used, u * PIECES + C_MOE + p - 1)
                dve.tensor_tensor(wl[:, p % 2, 0:to], raw[:, slot, s:s + to], raw_f(wh[:, p % 2, 0:to]),
                                  ALU.subtract).then_inc(wl_ready, 1)

            r, one, over, unit_f = bm["r"], bm["one"], bm["over"], bm["unit_f"]
            lg, key, top1, lg2, key2, top2, sel, gat, posp, posm = (r[:, i] for i in range(10))
            m1, m2, gap, eg, g1, g2 = one[:, 0], one[:, 1], one[:, 4], one[:, 5], one[:, 6], one[:, 7]
            dve.wait_ge(route_in, 32)
            before, slots, desc = bm["rcon"][:, 0:P], bm["rcon"][:, P:2 * P], bm["rcon"][:, 2 * P:2 * P + E]
            dve.memset(bm["pos"][:], 0.0)
            dve.memset(bm["gate"][:], 0.0)
            dve.wait_ge(logit_done, 1)
            step(dve.tensor_copy(lg, ps[:, 0, 0:QT * E].rearrange("p (t e) -> p t e", e=E)))

            def best(src, key, top, m, km):
                step(dve.tensor_reduce(m, src, AX_X, ALU.max))
                for t in range(QT):
                    ins = dve.scalar_tensor_tensor(out=key[:, t], in0=src[:, t], scalar=m[:, t:t + 1], in1=desc,
                                                   op0=ALU.is_equal, op1=ALU.mult)
                step(ins)
                step(dve.tensor_reduce(km, key, AX_X, ALU.max))
                for t in range(QT):
                    ins = dve.tensor_scalar(top[:, t], key[:, t], km[:, t:t + 1], None, ALU.is_equal)
                step(ins)

            best(lg, key, top1, m1, one[:, 2])
            step(dve.scalar_tensor_tensor(out=lg2, in0=top1, scalar=-3e38, in1=lg, op0=ALU.mult, op1=ALU.add))
            best(lg2, key2, top2, m2, one[:, 3])
            dve.tensor_tensor(sel, top1, top2, ALU.add).then_inc(sel_ready, 1)
            step(dve.tensor_tensor(gap, m2, m1, ALU.subtract))
            dve.wait_ge(rsT_ready, 3)
            dve.tensor_tensor(gap, gap, rsT[:, 0:QT], ALU.mult).then_inc(gap_ready, 1)
            unit_split(0, 0)
            dve.wait_ge(gap_exp, 1)
            step(dve.tensor_scalar(g1, eg, 1.0, None, ALU.add))
            step(dve.reciprocal(g1, g1))
            step(dve.tensor_tensor(g2, eg, g1, ALU.mult))
            for t in range(QT):
                ins = dve.tensor_scalar(gat[:, t], top1[:, t], g1[:, t:t + 1], None, ALU.mult)
            step(ins)
            for t in range(QT):
                ins = dve.scalar_tensor_tensor(out=bm["gate"][:, t, 0:E], in0=top2[:, t], scalar=g2[:, t:t + 1],
                                               in1=gat[:, t], op0=ALU.mult, op1=ALU.add)
            step(ins)
            dve.wait_ge(pos_done, 1)
            step(dve.scalar_tensor_tensor(out=bm["pos"][:, :, 0:E],
                                          in0=ps[:, 7, 0:QT * E].rearrange("p (t e) -> p t e", e=E), scalar=1.0,
                                          in1=sel, op0=ALU.add, op1=ALU.mult))
            posp = bm["pos"][:, :, 0:E]

            def pick(u):
                for t in range(QT):
                    ins = dve.tensor_scalar(bm["pick"][:, t, :], slots, bm["pos"][:, t, bass.ds(u, 1)], None, ALU.is_equal)
                ins.then_inc(pick_ready, 1)

            pick(0)
            numbers = bm["rcon"][:, 2 * P + E:2 * P + 2 * E]
            more = over[:, 0]
            dve.tensor_scalar(posm, posp, float(P), None, ALU.subtract)
            dve.memset(unit_f[:], 0.0)
            step(dve.tensor_scalar(more, ps[:, 7, QT * E:(QT + 1) * E], P + 0.5, None, ALU.is_gt))
            step(dve.tensor_tensor_scan(over[:, 1], more, more, 0.0, ALU.add, ALU.max))
            step(dve.tensor_tensor(over[:, 1], over[:, 1], more, ALU.mult))
            for j in range(MAX_UNITS - E):
                ins = dve.tensor_scalar(over[:, 2 + j], over[:, 1], float(j + 1), None, ALU.is_equal)
            step(ins)
            for j in range(MAX_UNITS - E):
                dve.tensor_tensor_reduce(over[:, 5 + 5 * j], over[:, 2 + j], numbers, 1.0, 0.0, ALU.mult, ALU.add,
                                         unit_f[:, E + j:E + j + 1])
                for t in range(QT):
                    dve.tensor_tensor_reduce(over[:, 6 + 5 * j + 2 * t], over[:, 2 + j], posm[:, t], 1.0, 0.0, ALU.mult, ALU.add,
                                             bm["pos"][:, t, E + j:E + j + 1])
                    dve.tensor_tensor_reduce(over[:, 7 + 5 * j + 2 * t], over[:, 2 + j], bm["gate"][:, t, 0:E], 1.0, 0.0, ALU.mult,
                                             ALU.add, bm["gate"][:, t, E + j:E + j + 1])
            step(dve.tensor_reduce(unit_f[:, 15:16], more, AX_X, ALU.add))
            step(dve.tensor_scalar(unit_f[:, 15:16], unit_f[:, 15:16], float(E), None, ALU.add))
            dve.tensor_copy(bm["unit_i"][:], unit_f[0:1, :]).then_inc(routed, 1)

            def gathered_low(k):
                for h in range(2):
                    s = slice(h * BANK, (h + 1) * BANK)
                    dve.wait_ge(gh_ready, k * 2 + h - 1)
                    dve.tensor_tensor(bm["gl"][:, s], ps[:, 5 + h, :], raw_f(bm["gh"][:, s]), ALU.subtract).then_inc(gl_ready, 1)

            gathered_low(1)
            unit_split(0, 1)
            dve.wait_ge(routed, 1)
            units = dve.value_load(bm["unit_i"][0:1, 15:16], min_val=E, max_val=MAX_UNITS)
            dve.wait_ge(back_ev, 8)
            dve.nop().then_inc(acc_done, 1)

            def add_unit(u):
                for n in range(4):
                    dve.wait_ge(sc_done, u * 4 + n + 1)
                    a = bm["acc"][:, n % 2, n // 2 * BANK:(n // 2 + 1) * BANK]
                    dve.tensor_tensor(a, a, ps[:, (7, 4, 5, 6)[n], :], ALU.add).then_inc(acc_done, 1)

            with dve.Fori(0, units) as u:
                def turned_low(i):
                    dve.wait_ge(eah_ready, u * FC + i + 1)
                    dve.tensor_tensor(bm["eal"][:], ps[:, 4, :], raw_f(bm["eah"][:]), ALU.subtract).then_inc(eal_ready, 1)

                with dve.If(u > 0):
                    unit_split(u, 0)
                    unit_split(u, 1)
                    add_unit(u)
                for j, (kind, i) in enumerate(unit_chunks):
                    if kind == "u":
                        dve.wait_ge(esil_ready, u * FC + i + 1)
                        dve.wait_ge(w_used, u * PIECES + C_MOE + j + 1)
                        if i:
                            dve.wait_ge(eT_done, u * FC + i)
                        dve.tensor_tensor(bm["act"][:], bm["sil"][:], ps[:, 1, :], ALU.mult).then_inc(eprod_ready, 1)
                    if j + 2 < PIECES:
                        unit_split(u, j + 2)
                    if (kind, i) == ("u", 0):
                        turned_low(0)
                    if kind == "d" and i + 1 < FC:
                        turned_low(i + 1)
                        if i == 1:
                            for t in range(QT):
                                ins = dve.tensor_scalar(bm["pay"][:, t, :], slots, bm["pos"][:, t, bass.ds(u, 1)],
                                                        bm["gate"][:, t, bass.ds(u, 1)], ALU.is_equal, ALU.mult)
                            ins.then_inc(pay_ready, 1)
                        if i == 4:
                            dve.wait_ge(gathered, u + 1)
                            pick(u + 1)
                        if i + 1 == FC - 1:
                            gathered_low(u + 2)
                dve.wait_ge(w_used, u * PIECES + C_MOE + PIECES)
                dve.tensor_copy(bm["y"][:, 0:BANK], ps[:, 2, :]).then_inc(y_ev, 1)
                dve.tensor_copy(bm["y"][:, BANK:D], ps[:, 3, :]).then_inc(y_ev, 1)
            add_unit(units)

            dve.wait_ge(gain_in, 16)
            dve.wait_ge(fin_root, 1)
            dve.reciprocal(small[:, 8:10], small[:, 6:8]).then_inc(fin_rec, 1)
            dve.wait_ge(fin_rec, 1)
            for t in range(QT):
                dve.scalar_tensor_tensor(out=bm["tok"][:, t, :], in0=bm["acc"][:, t, :], scalar=small[:, 8 + t:9 + t],
                                         in1=xn[:, 0:D], op0=ALU.mult, op1=ALU.mult).then_inc(fin_ready, 1)

        @block.tensor
        def _(pe):
            def feature_product(outp, c, k_tiles, n0, ncols, highs, lows, first=True, last=True, await_k=None):
                high, low = wh[:, c % 2, :], wl[:, c % 2, :]
                if n0 == 0:
                    pe.wait_ge(wh_ready, c + 1)
                for k in range(k_tiles):
                    if await_k:
                        await_k(k)
                    w = high[:, k * ncols + n0:k * ncols + n0 + P]
                    pe.matmul(outp, w, highs(k), start=first and k == 0, stop=False)
                    last_high = pe.matmul(outp, w, lows(k), start=False, stop=False)
                if n0 == 0:
                    pe.wait_ge(wl_ready, c + 1)
                for k in range(k_tiles):
                    w = low[:, k * ncols + n0:k * ncols + n0 + P]
                    ins = pe.matmul(outp, w, highs(k), start=False, stop=last and k == k_tiles - 1)
                return last_high, ins

            def token_product(outp, c, firsts, stride):
                high, low = wh[:, c % 2, :], wl[:, c % 2, :]
                pe.wait_ge(wh_ready, c + 1)
                for k in range(KD):
                    w = high[:, k * WIDE:(k + 1) * WIDE]
                    s = slice(k * stride + firsts, k * stride + firsts + P)
                    pe.matmul(outp, xh[:, s], w, start=(k == 0), stop=False)
                    last_high = pe.matmul(outp, xl[:, s], w, start=False, stop=False)
                pe.wait_ge(wl_ready, c + 1)
                for k in range(KD):
                    s = slice(k * stride + firsts, k * stride + firsts + P)
                    ins = pe.matmul(outp, xh[:, s], low[:, k * WIDE:(k + 1) * WIDE], start=False, stop=(k == KD - 1))
                return last_high, ins

            def norm_sum(n):
                src = sq3 if n == 3 else xn3
                for k in range(KD):
                    pe.wait_ge(squared, KD * n + k + 1)
                    ins = pe.matmul(ps[:, 7, 0:L], ones, src[:, k, :], start=(k == 0), stop=(k == KD - 1))
                ins.then_inc(summed, 1)

            def turn_rs(n, firsts):
                pe.wait_ge(rs_ready, n)
                for t, first in enumerate(firsts):
                    w = min(P, L - first)
                    ins = pe.transpose(ps[0:w, 6, 32 * t:32 * t + 32], rs[0:32, first:first + w], ident[0:32, 0:32])
                ins.then_inc(rs_turned, 1)

            def gained_parts(n):
                return lambda k: pe.wait_ge(xl_ready, KD * n + k + 1)

            pe.wait_ge(base_in, 16)
            pe.wait_ge(x_in, 64)
            for n in range(6):
                g, t = n // 3, n % 3
                w = P if t < 2 else META
                for k in range(4):
                    ins = pe.transpose(ps[:, n, k * w:(k + 1) * w],
                                       tokens_in[0:w, t, (4 * g + k) * P:(4 * g + k + 1) * P], ident[0:w, 0:w])
                ins.then_inc(turned, 1)
            pe.wait_ge(vec_in, 96)
            pe.transpose(ps[:, 6, 0:48], vec_rows[:, :], ident[0:48, 0:48]).then_inc(vec_turned, 1)

            def part(x_, s, stride):
                return lambda k: x_[:, k * stride + s.start:k * stride + s.stop]

            pe.wait_ge(pads, 5)
            for c in range(4):
                for m in range(4):
                    tt = 4 * c + m
                    if tt >= 4:
                        pe.wait_ge(tile_ev, tt - 3)
                    lh, ins = feature_product(ps[:, tt % 4, 0:L], c, KD, m * P, WIDE,
                                              part(xh, slice(0, L), L), part(xl, slice(0, L), L),
                                              await_k=gained_parts(0) if tt == 0 else None)
                    tile_signal(ins, tile_done, m, 4)
                    if tt == 0:
                        norm_sum(0)
                    if tt == 1:
                        pe.wait_ge(lam_sum_in, 1)
                        pe.matmul(ps[:, 5, 0:2], ones, small[:, 0:2], start=True, stop=True).then_inc(lam_sum, 1)
                    if tt == 4:
                        turn_rs(1, (0, P, 2 * P))
                lh.then_inc(wh_used, 1)
            for c in range(4, 6):
                for t in range(3):
                    vi = 3 * (c - 4) + t
                    if vi >= 4:
                        pe.wait_ge(v_ev, vi - 3)
                    lh, ins = token_product(ps[:, 4 + vi % 4, :], c, t * P, L)
                    tile_signal(ins, v_done, t, 3)
                lh.then_inc(wh_used, 1)

            q0, k0, v0 = b0["q"], b0["k"], b0["v"]
            pe.wait_ge(v_ev, 6)
            for n in range(SB_HEADS + 3):
                if n < SB_HEADS:
                    i, rows_ = n // 2, slice(HD * (n % 2), HD * (n % 2) + HD)
                    if n >= 4:
                        pe.wait_ge(expo_ready, n - 3)
                    for first, col, width in KEY_TILES:
                        ins = pe.matmul(ps[:, n % 4, col:col + width], k0[rows_, i * L + first:i * L + first + P],
                                        q0[rows_, i, first:L], start=(first == 0), stop=False, skip_group_check=True)
                    ins.then_inc(score_done, 1)
                m = n - 2
                if 0 <= m < SB_HEADS:
                    pe.wait_ge(keep_ready, m + 1)
                    if m == 0:
                        pe.wait_ge(gap_zero, 1)
                        pe.wait_ge(sums_ready, 1)
                    after0 = KT0[1] + KT0[2]
                    for name in ("keep_h", "keep_l"):
                        keep = h0[name][:, m % 2, :]
                        pe.matmul(ps[:, m % 4, 0:SCW], sums_r[:, 0:P], keep[:, 0:SCW],
                                  start=False, stop=False, skip_group_check=True)
                        pe.matmul(ps[:, m % 4, KT0[1] + P:SCW], sums_r[:, P:2 * P], keep[:, KT1[1]:KEEPW],
                                  start=False, stop=False, skip_group_check=True)
                        ins = pe.matmul(ps[:, m % 4, after0 - KT2[2]:after0], sums_r[:, P:2 * P], keep[:, 0:KT2[2]],
                                        start=False, stop=(name == "keep_l"), skip_group_check=True)
                    ins.then_inc(soft_done, 1)
                m = n - 3
                if 0 <= m < SB_HEADS:
                    i, rows_ = m // 2, slice(HD * (m % 2), HD * (m % 2) + HD)
                    pe.wait_ge(att_ready, m + 1)
                    if i >= 2 and m % 2 == 0:
                        pe.wait_ge(ol_ready, i - 1)
                    for t, (first, col, width) in enumerate(KEY_TILES):
                        ins = pe.matmul(ps[rows_, 4 + i % 2, first:L], v0[:, t, m * HD:(m + 1) * HD],
                                        h0["att"][:, m % 2, col:col + width], start=(t == 0), stop=(t == 2),
                                        skip_group_check=True)
                    ins.then_inc(pv_done, 1)

            def out_projection(c0, width, ready, oh, ol, freed):
                pe.wait_ge(ol_ready, ready)
                for c in range(c0, c0 + 2):
                    for m in range(4):
                        n = 4 * (c - c0) + m
                        if n >= 4:
                            pe.wait_ge(residual, freed + n - 3)
                        lh, ins = feature_product(ps[:, n % 4, 0:width], c, KD, m * P, WIDE,
                                                  part(oh, slice(0, width), width), part(ol, slice(0, width), width))
                        tile_signal(ins, add_done, m, 4)
                    lh.then_inc(wh_used, 1)

            out_projection(C_SB_O, L, KD, b0["oh"], b0["ol"], 0)

            for i in range(N_UP):
                for kind in range(2):
                    c = C_UP + 2 * i + kind
                    for m in range(up_tiles(i)):
                        f = 4 * i + m
                        if f >= 4:
                            pe.wait_ge(prod_ready if kind else g_free, f - 3)
                        elif kind == 0:
                            pe.wait_ge(residual, 5 + f)
                        elif f == 3:
                            pe.wait_ge(rooted, 2)
                        lh, ins = feature_product(ps[:, 4 * kind + m, 0:L], c, KD, m * P, up_tiles(i) * P,
                                                  part(xh, slice(0, L), L), part(xl, slice(0, L), L),
                                                  await_k=gained_parts(1) if c == C_UP and m == 0 else None)
                        tile_signal(ins, u_done if kind else g_done, m, up_tiles(i))
                        if c == C_UP and m == 0:
                            norm_sum(1)
                    lh.then_inc(wh_used, 1)
            pe.wait_ge(al_ready, NF)
            for i in range(N_DOWN):
                c = C_DOWN + i
                for n in range(KD):
                    lh, ins = feature_product(ps[:, n, 0:L], c, up_tiles(i), n * P, D,
                                              lambda k: bf["ah"][:, 4 * i + k, :], lambda k: bf["al"][:, 4 * i + k, :],
                                              first=(i == 0), last=(i == N_DOWN - 1))
                    if i == N_DOWN - 1 or n == KD - 1:
                        tile_signal(ins, add_done, n, KD)
                lh.then_inc(wh_used, 1)

            swap = b1["con"][:, L:L + P]

            def swapped(tt):
                w = SEQ if tt < KD else L
                pe.wait_ge(tile_ev, 16 + tt + 1)
                if tt == 0:
                    pe.wait_ge(diff_in, 16)
                if tt >= 2:
                    pe.wait_ge(rope_done, tt - 1)
                pe.matmul(ps[:, 4 + tt % 2, 0:w], swap, xn3[:, tt % 8, 0:w], start=True, stop=True).then_inc(swap_done, 1)

            for c in range(4):
                for m in range(4):
                    tt = 4 * c + m
                    if tt >= 4:
                        pe.wait_ge(tile_ev, 16 + tt - 3)
                    else:
                        pe.wait_ge(residual, KD + tt + 1)
                    s = slice(META, L) if c < 2 else slice(0, L)
                    lh, ins = feature_product(ps[:, tt % 4, 0:s.stop - s.start], C_D_QKV + c, KD, m * P, WIDE,
                                              part(xh, s, L), part(xl, s, L),
                                              await_k=gained_parts(2) if tt == 0 else None)
                    tile_signal(ins, tile_done, m, 4)
                    if tt == 0:
                        pe.wait_ge(residual, 2 * KD)
                        norm_sum(2)
                    if tt >= 1:
                        swapped(tt - 1)
                    if tt == 4:
                        turn_rs(2 + 1, (0, META, META + P))
                lh.then_inc(wh_used, 1)
            swapped(15)
            for c in range(4, 6):
                for t in range(3):
                    vi = 3 * (c - 4) + t
                    if vi >= 4:
                        pe.wait_ge(v_ev, 6 + vi - 3)
                    lh, ins = token_product(ps[:, vi % 4, :], C_D_QKV + c, (0, META, META + P)[t], L)
                    tile_signal(ins, v_done, t, 3)
                lh.then_inc(wh_used, 1)

            q1, k1, v1 = b1["q"], b1["k"], b1["v"]
            pe.wait_ge(rope_done, 16)
            pe.wait_ge(v_ev, 12)
            for n in range(DIFF_HEADS + 4):
                if n < DIFF_HEADS:
                    if n >= 2:
                        pe.wait_ge(ds_free, 2 * n - 2)
                    for t in range(2):
                        c0, w = t * (P + META), P + META if t == 0 else L
                        for comp in range(2):
                            rows_ = slice(HD * comp, HD * comp + HD)
                            ins = pe.matmul(ps[:, (2 * n + comp) % 4, c0:c0 + w],
                                            q1[rows_, n * SEQ + t * P:n * SEQ + (t + 1) * P],
                                            k1[rows_, n * L:n * L + w], start=True, stop=True)
                            if t:
                                ins.then_inc(ds_done, 1)
                m = n - 2
                if 0 <= m < DIFF_HEADS:
                    pr = h1["probs"][:, m % 2]
                    pe.wait_ge(mix_ready, 2 * m + 2)
                    if m >= 1:
                        pe.wait_ge(wt_ev_a, m)
                    pe.transpose(ps[:, 4, 0:P], pr[:, 0, META:META + P], ident)
                    pe.transpose(ps[:, 4, P:2 * P], pr[:, 2, META:META + P], ident)
                    pe.transpose(ps[:, 4, 2 * P:3 * P], pr[:, 2, META + P:L], ident)
                    if m >= 1:
                        pe.wait_ge(wt_ev_m, m)
                    pe.transpose(ps[0:META, 6, 0:P], pr[:, 0, 0:META], ident)
                    pe.transpose(ps[0:META, 6, P:2 * P], pr[:, 2, 0:META], ident).then_inc(wt_done, 1)
                m = n - 4
                if 0 <= m < DIFF_HEADS:
                    pe.wait_ge(do_ev, 2 * m + 2)
                    if m >= 1:
                        pe.wait_ge(sub_root, m)
                    pe.matmul(ps[:, 5, 0:SEQ], ones, h1["sq"][:, m % 2, :], start=True, stop=True).then_inc(sub_sum, 1)
                m = n - 3
                if 0 <= m < DIFF_HEADS:
                    wT = h1["wT"][:, m % 2, :]
                    pe.wait_ge(wt_ev_a, m + 1)
                    pe.wait_ge(wt_ev_m, m + 1)
                    if m >= 1:
                        pe.wait_ge(do_ev, 2 * m)
                    cs = slice(m * P, (m + 1) * P)
                    pe.matmul(ps[:, 7, 0:SEQ], v1[0:META, 0, cs], wT[0:META, 3 * P:], start=True, stop=False)
                    pe.matmul(ps[:, 7, 0:SEQ], v1[:, 1, cs], wT[:, 0:2 * P], start=False, stop=False)
                    pe.matmul(ps[:, 7, P:SEQ], v1[:, 2, cs], wT[:, 2 * P:3 * P], start=False, stop=True).then_inc(do_done, 1)
            out_projection(C_D_O, SEQ, 2 * KD, b1["oh"], b1["ol"], 2 * KD)

            norm_sum(3)
            pe.wait_ge(gained, KD)
            pe.wait_ge(route_in, 32)
            pe.wait_ge(residual, 3 * KD)
            for t in range(QT):
                for k in range(KD):
                    ins = pe.matmul(ps[:, 0, t * E:(t + 1) * E], xn3[:, k, META + t * P:META + (t + 1) * P],
                                    bm["wr"][:, k, :], start=(k == 0), stop=(k == KD - 1))
            ins.then_inc(logit_done, 1)
            for n in range(8):
                if n == 4:
                    turn_rs(4, (META, META + P))
                if n >= 4:
                    pe.wait_ge(back_ev, n - 3)
                src = xn3 if n < 4 else hT
                t, half = n % 4 // 2, n % 2
                for k in range(4):
                    ins = pe.transpose(ps[:, 1 + n % 4, k * P:(k + 1) * P],
                                       src[:, 4 * half + k, META + t * P:META + (t + 1) * P], ident)
                ins.then_inc(back_done, 1)
            before = bm["rcon"][:, 0:P]
            sel = bm["r"][:, 6]
            pe.wait_ge(sel_ready, 1)
            pe.matmul(ps[:, 7, 0:E], before, sel[:, 0], start=True, stop=True)
            pe.matmul(ps[:, 7, E:2 * E], ones, sel[:, 0], start=True, stop=False)
            pe.matmul(ps[:, 7, E:2 * E], before, sel[:, 1], start=False, stop=True)
            pe.matmul(ps[:, 7, 2 * E:3 * E], ones, sel[:, 0], start=True, stop=False)
            pe.matmul(ps[:, 7, 2 * E:3 * E], ones, sel[:, 1], start=False, stop=True).then_inc(pos_done, 1)

            def gather(k):
                pe.wait_ge(pick_ready, k + 1)
                for f in range(KD):
                    for t in range(QT):
                        ins = pe.matmul(ps[:, 5 + f // 4, f % 4 * P:(f % 4 + 1) * P], bm["tok"][:, t, f * P:(f + 1) * P],
                                        bm["pick"][:, t, :], start=(t == 0), stop=(t == QT - 1))
                ins.then_inc(gathered, 1)

            pe.wait_ge(back_ev, 8)
            gather(0)
            pe.nop().then_inc(sc_done, 4)
            pe.wait_ge(routed, 1)
            units = pe.value_load(bm["unit_i"][0:1, 15:16], min_val=E, max_val=MAX_UNITS)
            with pe.Fori(0, units) as u:
                gh, gl = bm["gh"], bm["gl"]

                def up(i, kind):
                    j, bank = at[kind, i], 0 if kind == "g" else 1
                    high, low = wh[:, j % 2, :], wl[:, j % 2, :]
                    if i:
                        pe.wait_ge(esil_ready if kind == "g" else eprod_ready, u * FC + i)
                    pe.wait_ge(wh_ready, u * PIECES + C_MOE + j + 1)
                    for k in range(KD):
                        w, s = high[:, k * WIDE:(k + 1) * WIDE], slice(k * P, (k + 1) * P)
                        pe.matmul(ps[:, bank, :], gh[:, s], w, start=(k == 0), stop=False)
                        ins = pe.matmul(ps[:, bank, :], gl[:, s], w, start=False, stop=False)
                    ins.then_inc(wh_used, 1)
                    pe.wait_ge(wl_ready, u * PIECES + C_MOE + j + 1)
                    for k in range(KD):
                        s = slice(k * P, (k + 1) * P)
                        ins = pe.matmul(ps[:, bank, :], gh[:, s], low[:, k * WIDE:(k + 1) * WIDE], start=False, stop=(k == KD - 1))
                    ins.then_inc(w_used, 1)

                def down(i, k0=0, n=4):
                    p = at["d", i] + k0 // 2
                    high, low = wh[:, p % 2, :], wl[:, p % 2, :]
                    ah, al = bm["eah"], bm["eal"]
                    pe.wait_ge(eal_ready, u * FC + i + 1)
                    pe.wait_ge(wh_ready, u * PIECES + C_MOE + p + 1)
                    for k in range(n):
                        s = slice((k0 + k) * P, (k0 + k + 1) * P)
                        for h in range(2):
                            w = high[:, k * D + h * BANK:k * D + (h + 1) * BANK]
                            pe.matmul(ps[:, 2 + h, :], ah[:, s], w, start=(i == 0 and k == 0), stop=False)
                            ins = pe.matmul(ps[:, 2 + h, :], al[:, s], w, start=False, stop=False)
                    ins.then_inc(wh_used, 1)
                    pe.wait_ge(wl_ready, u * PIECES + C_MOE + p + 1)
                    for k in range(n):
                        s = slice((k0 + k) * P, (k0 + k + 1) * P)
                        for h in range(2):
                            w = low[:, k * D + h * BANK:k * D + (h + 1) * BANK]
                            ins = pe.matmul(ps[:, 2 + h, :], ah[:, s], w, start=False,
                                            stop=(i == FC - 1 and k0 + k == 3))
                    ins.then_inc(w_used, 1)

                pe.wait_ge(gl_ready, u * 2 + 2)
                for i in range(FC):
                    up(i, "g")
                    up(i, "u")
                    if i >= 1:
                        down(i - 1)
                    pe.wait_ge(eprod_ready, u * FC + i + 1)
                    if i:
                        pe.wait_ge(eal_ready, u * FC + i)
                    else:
                        pe.wait_ge(acc_done, u * 4 + 1)
                    for k in range(4):
                        s = slice(k * P, (k + 1) * P)
                        ins = pe.transpose(ps[:, 4, s], bm["act"][:, s], ident)
                    ins.then_inc(eT_done, 1)
                    if i == 3:
                        pe.wait_ge(pay_ready, u + 1)
                        for t in range(QT):
                            ins = pe.transpose(ps[:, 7, t * P:(t + 1) * P], bm["pay"][:, t, :], ident)
                        ins.then_inc(payT_done, 1)
                gather(u + 1)
                down(FC - 1, 0, 2)
                down(FC - 1, 2, 2)
                pe.wait_ge(payT_ev, u + 1)
                pe.wait_ge(gl_ready, u * 2 + 4)
                for n in range(4):
                    half, t = n // 2, n % 2
                    if t == 0:
                        pe.wait_ge(y_ev, u * 2 + half + 1)
                    pe.matmul(ps[:, (7, 4, 5, 6)[n], :], bm["payT"][:, t * P:(t + 1) * P],
                              bm["y"][:, half * BANK:(half + 1) * BANK], start=True, stop=True).then_inc(sc_done, 1)


_INS = ["x", "meta_tokens", "norm_gains", "sb_w_qkv", "sb_w_o", "diff_w_qkv", "diff_w_o", "diff_subln",
        "diff_lambda_q1", "diff_lambda_k1", "diff_lambda_q2", "diff_lambda_k2", "ffn_w_gate", "ffn_w_up",
        "ffn_w_down", "moe_router", "moe_w_gate", "moe_w_up", "moe_w_down", "final_norm"]


def kernel(**inputs):
    import concourse.bacc as bacc
    from concourse.bass_utils import run_bass_kernel_spmd

    nc = bacc.Bacc("TRN2", target_bir_lowering=False, num_devices=1)
    arrays, args = {}, []
    for name, a in [(n, inputs[n]) for n in _INS] + list(constants().items()):
        a = np.ascontiguousarray(a)
        arrays[f"in_{name}"] = a
        args.append(nc.dram_tensor(f"in_{name}", a.shape, mybir.dt.from_np(a.dtype), kind="ExternalInput").ap())
    args.append(nc.dram_tensor("out", (1, SEQ, D), F32, kind="ExternalOutput").ap())
    build(nc, *args)
    r = run_bass_kernel_spmd(nc, [arrays], core_ids=[0])
    return np.asarray(r.results[0]["out"])
```

```python
import math
from contextlib import ExitStack

import numpy as np

import concourse.bass as bass
from concourse import mybir

F32 = mybir.dt.float32
F32R = mybir.dt.float32r
I32 = mybir.dt.int32
ALU = mybir.AluOpType
ACT = mybir.ActivationFunctionType
AX_X = mybir.AxisListType.X

P = 128
D = 1024
KD = D // P
META = 16
SEQ = 256
L = META + SEQ
HD = 64
SB_HEADS = D // HD
DIFF_HEADS = D // (2 * HD)
FF = 2816
NF = FF // P
E = 8
FE = 3584
EPS = 1e-6
LAMBDA_INIT = 0.8 - 0.6 * math.exp(-0.3)
SCALE = HD ** -0.5
MASKED = -1e30

CHUNK = 4096
WIDE = CHUNK // KD
HALF = WIDE // P * P
QT = SEQ // P
BANK = 512

KT2 = (2 * P, 0, L - 2 * P)
KT0 = (0, KT2[1] + KT2[2], L)
KT1 = (P, KT0[1] + KT0[2], L - P)
KEY_TILES = (KT0, KT1, KT2)
SCW = KT1[1] + KT1[2]
KEEP2 = SCW + P
KEEPW = KEEP2 + KT2[2]

C_SB_QKV = 0
C_SB_O = 6
C_UP = 8
N_UP = -(-FF // WIDE)
C_DOWN = C_UP + 2 * N_UP
N_DOWN = -(-NF // 4)
C_D_QKV = C_DOWN + N_DOWN
C_D_O = C_D_QKV + 6
C_MOE = C_D_O + 2
FC = FE // WIDE
CPU = 3 * FC
PIECES = CPU + 1
MAX_UNITS = E + 3

SUMS = (4, 7, 5, 6)

BACKS = (4, 5, 6, 7, 1, 2, 3, 4)

LOG_EXP = "natural_log_exp_and_others"
SILU = "silu_and_others"


TOKENS0 = (0, P, 2 * P)
TOKENS1 = (0, META, META + P)


def tile_rows(firsts, t):
    return (firsts + (L,))[t + 1] - firsts[t]


def up_tiles(i):
    return min(4, NF - 4 * i)


def constants():
    r = np.arange(P)
    ident = np.eye(P, dtype=np.float32)
    from_here = (r[:, None] >= r[None, :]).astype(np.float32)
    ones = np.ones((P, P), np.float32)
    before = (r[:, None] < r[None, :]).astype(np.float32)
    keep = np.zeros((P, SCW), np.float32)
    for first, col, width in KEY_TILES:
        key = first + r[:, None]
        query = first + np.arange(width)[None, :]
        keep[:, col:col + width] = key < query
    neg_keep = -keep
    strict_bias = np.where(keep > 0, np.float32(0), np.float32(MASKED)).astype(np.float32)
    causal_bias = np.zeros((P, L), np.float32)
    causal_bias[:, L - P:] = np.where(r[None, :] <= r[:, None], 0.0, MASKED)
    swap = np.zeros((P, P), np.float32)
    swap[r, r ^ 32] = 1.0
    inv = (np.float32(10000.0) ** (-np.arange(0, HD, 2, dtype=np.float32) / np.float32(HD))).astype(np.float32)
    ang = np.arange(L, dtype=np.float32)[None, :] * inv[r % 32][:, None]
    cos = np.cos(ang).astype(np.float32)
    sin = (np.sin(ang) * np.where(r % HD < 32, -1.0, 1.0)[:, None]).astype(np.float32)
    slots = np.broadcast_to(np.arange(1, P + 1, dtype=np.float32), (P, P))
    desc = np.broadcast_to(np.arange(E, 0, -1, dtype=np.float32), (P, E))
    return {
        "c_base": np.concatenate([ident, from_here, ones], 1),
        "c_neg_keep": neg_keep.astype(np.float32),
        "c_bias": strict_bias,
        "c_diff": np.concatenate([causal_bias, swap, cos, sin], 1).astype(np.float32),
        "c_route": np.concatenate([before, slots, desc, E - desc], 1).astype(np.float32),
    }


def build(nc, x, meta, gains, sb_qkv, sb_o, d_qkv, d_o, subln, lq1, lk1, lq2, lk2,
          ffn_gate, ffn_up, ffn_down, router, moe_gate, moe_up, moe_down, final_norm,
          c_base, c_neg_keep, c_bias, c_diff, c_route, out):
    ctx = ExitStack()
    with ctx:
        def sb(name, shape, dt=F32, where=ctx):
            return where.enter_context(nc.sbuf_tensor(name, shape, dt))

        def sem(name):
            return ctx.enter_context(nc.semaphore(name))

        ps = ctx.enter_context(nc.psum_tensor("ps", [P, 8, BANK], F32))

        raw = sb("raw", [P, 3, CHUNK])
        wh = sb("wh", [P, 2, CHUNK], F32R)
        wl = sb("wl", [P, 2, CHUNK], F32R)
        hT = sb("hT", [P, KD, L])
        xn = sb("xn", [P, KD * L])
        base = sb("base", [P, 3 * P])
        ident, from_here, ones = (base[:, i * P:(i + 1) * P] for i in range(3))
        sums_r = sb("sums_r", [P, 2 * P], F32R)
        rs = sb("rs", [P, L])
        var = sb("var", [P, L])
        rsT = sb("rsT", [P, QT])
        vecs = sb("vecs", [P, 48])
        eps = sb("eps", [P, 1])
        small = sb("small", [P, 20])
        neg_lam = sb("neg_lam", [P, 1])
        gsub = sb("gsub", [P, 1])
        rcon = sb("rcon", [P, 2 * P + 2 * E])
        wr = sb("wr", [P, KD, E])
        xn3 = xn[:].rearrange("p (k t) -> p k t", t=L)
        nd = DIFF_HEADS * SEQ

        def phase(make):
            with ExitStack() as own:
                return make(own)

        def parts(own):
            return (sb("xh", [P, KD * L + P - META], F32R, where=own),
                    sb("xl", [P, KD * L + P - META], F32R, where=own))

        def heads0(own):
            return {"soft": sb("soft", [P, 2, SCW], where=own), "keep_h": sb("keep_h", [P, 2, KEEPW], F32R, where=own), "keep_l": sb("keep_l", [P, 2, KEEPW], F32R, where=own),
                    "att": sb("att", [P, 2, SCW], where=own), "bias": sb("bias", [P, SCW], where=own)}

        def heads1(own):
            return {"probs": sb("probs", [P, 2, 4, L], where=own), "wT": sb("wT", [P, 2, 3 * P + SEQ], where=own),
                    "sq": sb("head_sq", [P, 2, SEQ], where=own), "o": sb("head_o", [P, 2, SEQ], where=own)}

        def layer0(own):
            return {"q": sb("q0", [P, KD, L], where=own), "k": sb("k0", [P, KD * L + P - META], where=own),
                    "v": sb("v0", [P, 3, D], where=own),
                    "oh": sb("oh0", [P, KD * L], F32R, where=own), "ol": sb("ol0", [P, KD * L], F32R, where=own),
                    "neg_keep": sb("neg_keep", [P, SCW], where=own), "vec_rows": sb("vec_rows", [48, P], where=own)}

        def feed_forward(own):
            return {"ah": sb("ah", [P, NF, L], F32R, where=own), "al": sb("al", [P, NF, L], F32R, where=own)}

        def layer1(own):
            return {"q": sb("q1", [P, nd], where=own), "k": sb("k1", [P, KD * L], where=own),
                    "v": sb("v1", [P, 3, D], where=own),
                    "oh": sb("oh1", [P, nd], F32R, where=own), "ol": sb("ol1", [P, nd], F32R, where=own),
                    "con": sb("con", [P, L + P + 2 * L], where=own), "stat": sb("stat", [P, 2, 16], where=own)}

        def experts(own):
            b = {}
            for name, shape in (("tok", [P, QT, D]), ("acc", [P, QT, D]), ("pick", [P, QT, P]), ("pay", [P, QT, P]),
                                ("payT", [P, SEQ]), ("sil", [P, BANK]), ("act", [P, BANK]), ("y", [P, D]),
                                ("r", [P, 10, QT, E]),
                                ("one", [P, 8, QT]), ("pos", [P, QT, 12]), ("gate", [P, QT, 12]),
                                ("over", [P, 20, E]), ("unit_f", [P, 16])):
                b[name] = sb(name, shape, where=own)
            for name, width in (("gh", KD * P), ("gl", KD * P), ("eah", BANK), ("eal", BANK)):
                b[name] = sb(name, [P, width], F32R, where=own)
            b["unit_i"] = sb("unit_i", [1, 16], I32, where=own)
            return b

        xh, xl = phase(parts)
        h0, h1 = phase(heads0), phase(heads1)
        sq3 = phase(lambda own: sb("sq3", [P, 4 * BANK], where=own))
        sb("overlay", [P, 2 * (KD * L + P - META)])
        b0, bf, b1, bm = phase(layer0), phase(feed_forward), phase(layer1), phase(experts)
        tokens_in, vec_rows = b0["v"], b0["vec_rows"]

        raw_landed = [sem(f"raw_landed{i}") for i in range(3)]
        wh_ready, wl_ready = sem("wh_ready"), sem("wl_ready")
        wh_used, w_used = sem("wh_used"), sem("w_used")
        base_in, keep_in, bias_in = sem("base_in"), sem("keep_in"), sem("bias_in")
        diff_in, route_in = sem("diff_in"), sem("route_in")
        x_in, vec_in, gain_in, rows_zero, stores = sem("x_in"), sem("vec_in"), sem("gain_in"), sem("rows_zero"), sem("stores")
        pads, turned, turned_act, turned_dve = sem("pads"), sem("turned"), sem("turned_act"), sem("turned_dve")
        vec_turned, vec_ev, lam_sum, lam_exp = sem("vec_turned"), sem("vec_ev"), sem("lam_sum"), sem("lam_exp")
        dve_step, act_step = sem("dve_step"), sem("act_step")
        residual, squared, summed, rooted = sem("residual"), sem("squared"), sem("summed"), sem("rooted")
        rs_ready = sem("rs_ready")
        xh_ready, xl_ready, gained = sem("xh_ready"), sem("xl_ready"), sem("gained")
        tile_done, tile_ev = sem("tile_done"), sem("tile_ev")
        v_turned, v_ev, v_zero = sem("v_turned"), sem("v_ev"), sem("v_zero")
        add_done = sem("add_done")
        lam_sum_in, pv_done, ds_free, fin_rec = sem("lam_sum_in"), sem("pv_done"), sem("ds_free"), sem("fin_rec")
        score_done, abs_done, soft_done, keep_ready = sem("score_done"), sem("abs_done"), sem("soft_done"), sem("keep_ready")
        sums_ready, masked, kh_ready, gap_zero = sem("sums_ready"), sem("masked"), sem("kh_ready"), sem("gap_zero")
        log_done, expo_ready, att_ready = sem("log_done"), sem("expo_ready"), sem("att_ready")
        oh_ready, ol_ready = sem("oh_ready"), sem("ol_ready")
        g_done, sil_ready, u_done, prod_ready = sem("g_done"), sem("sil_ready"), sem("u_done"), sem("prod_ready")
        ah_ready, al_ready, g_free, sil_scaled = sem("ah_ready"), sem("al_ready"), sem("g_free"), sem("sil_scaled")
        swap_done, rope_done = sem("swap_done"), sem("rope_done")
        ds_done, max_ready, probs_ready, mix_ready = sem("ds_done"), sem("max_ready"), sem("probs_ready"), sem("mix_ready")
        wt_done, wt_ev_a, wt_ev_m, do_done, do_ev = sem("wt_done"), sem("wt_ev_a"), sem("wt_ev_m"), sem("do_done"), sem("do_ev")
        sub_sum, sub_root, sub_ready = sem("sub_sum"), sem("sub_root"), sem("sub_ready")
        logit_done, back_done, back_ev = sem("logit_done"), sem("back_done"), sem("back_ev")
        gap_ready, gap_exp, sel_ready, pos_done, routed = sem("gap_ready"), sem("gap_exp"), sem("sel_ready"), sem("pos_done"), sem("routed")
        tok_squared, tok_summed, rsT_scaled, acc_ev = sem("tok_squared"), sem("tok_summed"), sem("rsT_scaled"), sem("acc_ev")
        pick_ready, gathered, gh_ready, gl_ready = sem("pick_ready"), sem("gathered"), sem("gh_ready"), sem("gl_ready")
        esil_ready, eprod_ready = sem("esil_ready"), sem("eprod_ready")
        eT_done, eah_ready, eal_ready = sem("eT_done"), sem("eah_ready"), sem("eal_ready")
        pay_ready, payT_done, payT_ev = sem("pay_ready"), sem("payT_done"), sem("payT_ev")
        y_ev, sc_done, acc_done = sem("y_ev"), sem("sc_done"), sem("acc_done")
        fin_sq, fin_root, fin_ready = sem("fin_sq"), sem("fin_root"), sem("fin_ready")

        def cols(w, i):
            return w[:, WIDE * i:min(WIDE * (i + 1), w.shape[1])].rearrange("(k p) n -> p k n", p=P)

        def rows(w, i):
            return w[WIDE * i:min(WIDE * (i + 1), w.shape[0]), :].rearrange("(k p) n -> p k n", p=P)

        sources = [cols(sb_qkv[0], i) for i in range(6)] + [cols(sb_o[0], i) for i in range(2)]
        for i in range(N_UP):
            sources += [cols(ffn_gate[0], i), cols(ffn_up[0], i)]
        sources += [rows(ffn_down[0], i) for i in range(N_DOWN)]
        sources += [cols(d_qkv[0], i) for i in range(6)] + [cols(d_o[0], i) for i in range(2)]
        assert len(sources) == C_MOE
        size = [s.shape[1] * s.shape[2] for s in sources] + [CHUNK] * 4
        weights_of = {"g": moe_gate.rearrange("a e k n -> (a e k) n"), "u": moe_up.rearrange("a e k n -> (a e k) n"),
                      "d": moe_down.rearrange("a e k n -> (a e k) n")}
        unit_chunks = [("g", 0), ("u", 0)]
        for i in range(1, FC):
            unit_chunks += [("g", i), ("u", i), ("d", i - 1)]
        unit_chunks += [("d", FC - 1)]
        at = {c: j for j, c in enumerate(unit_chunks)}

        def piece(p):
            if p < CPU - 1:
                return (C_MOE + p) % 3, 0, CHUNK
            return (C_MOE + CPU - 1) % 3, (p - CPU + 1) * (CHUNK // 2), CHUNK // 2

        def raw_f(w):
            return w.bitcast(F32)

        def await_tile(eng, done, before, c, m, tiles):
            if m == tiles - 1:
                eng.wait_ge(w_used, c + 1)
            else:
                eng.wait_ge(done, before + m + 1)

        def tile_signal(ins, done, m, tiles):
            ins.then_inc(w_used if m == tiles - 1 else done, 1)

        block = ctx.enter_context(nc.Block())

        @block.sync
        def _(sp):
            sp.dma_start(base[:], c_base).then_inc(base_in, 16)
            sp.dma_start(tokens_in[0:META, 0, :], meta).then_inc(x_in, 16)
            sp.dma_start(tokens_in[META:P, 0, :], x[0, 0:P - META]).then_inc(x_in, 16)
            sp.dma_start(tokens_in[:, 1, :], x[0, P - META:2 * P - META]).then_inc(x_in, 16)
            sp.dma_start(tokens_in[0:META, 2, :], x[0, 2 * P - META:SEQ]).then_inc(x_in, 16)
            sp.wait_ge(vec_in, 96)

            for c, src in enumerate(sources):
                if c >= 3:
                    sp.wait_ge(wl_ready, c - 2)
                dst = raw[:, c % 3, 0:size[c]].rearrange("p (k n) -> p k n", n=src.shape[2])
                sp.dma_start(dst, src).then_inc(raw_landed[c % 3], 16)

            def load_unit(u, e, first=False):
                for j, (kind, i) in enumerate(unit_chunks):
                    slot = (C_MOE + j) % 3
                    sp.wait_ge(wl_ready, u * PIECES + C_MOE + j - (2 if first or j >= 2 else 3))
                    w = weights_of[kind]
                    if kind == "d":
                        src = w[bass.ds(e * FE + WIDE * i, WIDE), :]
                    else:
                        src = w[bass.ds(e * D, D), WIDE * i:WIDE * (i + 1)]
                    src = src.rearrange("(k p) n -> p k n", p=P)
                    dst = raw[:, slot, :].rearrange("p (k n) -> p k n", n=src.shape[2])
                    sp.dma_start(dst, src).then_inc(raw_landed[slot], 16)

            load_unit(0, 0, first=True)
            with sp.Fori(1, E) as u:
                load_unit(u, u)
            sp.wait_ge(routed, 1)
            units = sp.value_load(bm["unit_i"][0:1, 15:16], min_val=E, max_val=MAX_UNITS)
            with sp.If(units > E):
                with sp.Fori(E, units) as u:
                    e = sp.value_load(bm["unit_i"][0:1, bass.ds(u, 1)], min_val=0, max_val=E - 1)
                    load_unit(u, e)

            for t in range(QT):
                sp.wait_ge(fin_ready, t + 1)
                sp.dma_start(out[0, t * P:(t + 1) * P], bm["tok"][:, t, :]).then_inc(stores, 16)
            sp.wait_ge(stores, 16 * QT)

        @block.gpsimd
        def _(pool):
            pool.dma_start(b0["neg_keep"][:], c_neg_keep).then_inc(keep_in, 16)
            pool.dma_start(rcon[:], c_route).then_inc(route_in, 16)
            pool.dma_start(wr[:], router[0].rearrange("(k p) e -> p k e", p=P)).then_inc(route_in, 16)
            pool.wait_ge(w_used, C_SB_O)
            pool.dma_start(h0["bias"][:], c_bias).then_inc(bias_in, 16)
            pool.wait_ge(w_used, C_D_QKV)
            pool.dma_start(b1["con"][:], c_diff).then_inc(diff_in, 16)
            pool.wait_ge(logit_done, 1)
            pool.wait_ge(back_done, 8)
            pool.dma_start(xn[:, 0:D], final_norm[None, :].to_broadcast([P, D])).then_inc(gain_in, 16)

        @block.scalar
        def _(act):
            def split_high(c):
                act.wait_ge(raw_landed[c % 3], 16 * (c // 3 + 1))
                if c >= 2:
                    act.wait_ge(wh_used, c - 1)
                    act.wait_ge(wl_ready, c - 1)
                n = size[c]
                act.copy(wh[:, c % 2, 0:n], raw[:, c % 3, 0:n]).then_inc(wh_ready, 1)

            def a_step(ins):
                act_steps[0] += 1
                ins.then_inc(act_step, 1)
                act.wait_ge(act_step, act_steps[0])

            act_steps = [0]

            def gained_high(n, k):
                act.activation(xh[:, k * L:(k + 1) * L], hT[:, k, :], ACT.Identity,
                               scale=vecs[:, n * KD + k:n * KD + k + 1]).then_inc(xh_ready, 1)

            def square(n, k):
                act.activation(xn3[:, k, :], hT[:, k, :], ACT.Square).then_inc(squared, 1)

            def root(n):
                act.wait_ge(summed, n + 1)
                a_step(act.activation(var[:], ps[:, 7, 0:L], ACT.Identity, bias=eps[:, 0:1], scale=1.0 / D))
                a_step(act.activation(rs[:], var[:], ACT.Ln))
                act.activation(rs[:], rs[:], ACT.Exp, scale=-0.5).then_inc(rooted, 1)

            def value_rows(v, base, cc, firsts):
                for t, first in enumerate(firsts):
                    w = tile_rows(firsts, t)
                    act.wait_ge(v_turned, base + 3 * cc + t + 1)
                    act.copy(v[0:w, t, cc * BANK:(cc + 1) * BANK], ps[0:w, 4 + (3 * cc + t) % 4, :]).then_inc(v_ev, 1)

            act.wait_ge(rows_zero, 1)
            act.dma_start(vec_rows[0:32, :], gains.rearrange("a b (k p) -> (a b k) p", p=P)).then_inc(vec_in, 16)
            act.dma_start(vec_rows[32:33, :], subln).then_inc(vec_in, 16)
            for n, v in enumerate((lq1, lk1, lq2, lk2)):
                act.dma_start(vec_rows[33 + n:34 + n, 0:HD], v).then_inc(vec_in, 16)
            act.preload_act_table_set(LOG_EXP)
            act.wait_ge(base_in, 16)
            act.copy(sums_r[:], base[:, P:3 * P]).then_inc(sums_ready, 1)
            for n in (0, 2, 3, 5):
                g, t = n // 3, n % 3
                w = P if t < 2 else META
                act.wait_ge(turned, n + 1)
                src = ps[:, n, 0:4 * w].rearrange("p (k t) -> p k t", t=w)
                act.copy(hT[:, 4 * g:4 * g + 4, t * P:t * P + w], src).then_inc(turned_act, 1)
            act.wait_ge(vec_turned, 1)
            act.copy(vecs[:], ps[:, 6, 0:48]).then_inc(vec_ev, 1)
            act.wait_ge(vec_ev, 1)
            for k in range(KD):
                if k % 4 == 0:
                    act.wait_ge(turned_act, 2 + k // 2)
                    act.wait_ge(turned_dve, 1 + k // 4)
                gained_high(0, k)
            split_high(0)
            for k in range(KD):
                square(0, k)
            split_high(1)
            root(0)
            act.wait_ge(lam_sum, 1)
            act.activation(small[:, 2:4], ps[:, 5, 0:2], ACT.Exp).then_inc(lam_exp, 1)
            for c in range(5):
                split_high(c + 2)
            act.wait_ge(v_zero, 1)
            for cc in range(2):
                value_rows(b0["v"], 0, cc, TOKENS0)

            for n in range(SB_HEADS + 4):
                if n < SB_HEADS:
                    a = h0["soft"][:, n % 2, :]
                    act.wait_ge(score_done, n + 1)
                    if n >= 2:
                        act.wait_ge(keep_ready, n - 1)
                    act.activation(a, ps[:, n % 4, 0:SCW], ACT.Abs).then_inc(abs_done, 1)
                    act.wait_ge(abs_done, 2 * n + 1)
                    act.activation(a, a, ACT.Exp, scale=-1.0).then_inc(abs_done, 1)
                    act.wait_ge(abs_done, 2 * n + 2)
                    act.activation(a, a, ACT.Ln, bias=1.0).then_inc(log_done, 1)
                m = n - 1
                if 0 <= m < SB_HEADS:
                    act.wait_ge(masked, m + 1)
                    if m >= 2:
                        act.wait_ge(soft_done, m - 1)
                    a, kh = h0["soft"][:, m % 2, :], h0["keep_h"][:, m % 2, :]
                    act.copy(kh[:, 0:SCW], a)
                    act.copy(kh[:, KEEP2:KEEPW], a[:, 0:KT2[2]]).then_inc(kh_ready, 1)
                m = n - 2
                if 0 <= m < SB_HEADS:
                    act.wait_ge(expo_ready, m + 1)
                    a = h0["att"][:, m % 2, :]
                    act.activation(a, a, ACT.Exp).then_inc(att_ready, 1)
                m = n - 4
                if 0 <= m < SB_HEADS and m % 2 == 1:
                    i = m // 2
                    act.wait_ge(pv_done, 2 * i + 2)
                    act.copy(b0["oh"][:, i * L:(i + 1) * L], ps[:, 4 + i % 2, 0:L]).then_inc(oh_ready, 1)

            def residual_tile(n, k):
                act.wait_ge(residual, KD * (n - 1) + k + 1)
                gained_high(n, k)
                square(n, k)

            split_high(C_SB_O + 1)
            for c in range(C_SB_O, C_SB_O + 2):
                for k in range(4 * (c - C_SB_O), 4 * (c - C_SB_O) + 4):
                    residual_tile(1, k)
                split_high(c + 2)

            root(1)
            for i in range(N_UP):
                for f in range(4 * i, 4 * i + up_tiles(i)):
                    act.wait_ge(g_free, f + 1)
                    act.activation(xn3[:, f % 8, :], xn3[:, f % 8, :], ACT.Silu).then_inc(sil_ready, 1)
                split_high(C_UP + 2 * i + 2)
                for f in range(4 * i, 4 * i + up_tiles(i)):
                    act.wait_ge(prod_ready, f + 1)
                    act.copy(bf["ah"][:, f, :], xn3[:, f % 8, :]).then_inc(ah_ready, 1)
                split_high(C_UP + 2 * i + 3)
            act.preload_act_table_set(LOG_EXP)
            for i in range(N_DOWN):
                if i == N_DOWN - 1:
                    for k in range(KD):
                        residual_tile(2, k)
                split_high(C_DOWN + i + 2)

            root(2)
            for c in range(5):
                split_high(C_D_QKV + c + 2)
            for cc in range(2):
                value_rows(b1["v"], 6, cc, TOKENS1)

            for n in range(DIFF_HEADS + 4):
                m = n - 4
                if 0 <= m < DIFF_HEADS:
                    r_ = h1["sq"][:, m % 2, :]
                    act.wait_ge(sub_sum, m + 1)
                    a_step(act.activation(r_, ps[:, 5, 0:SEQ], ACT.Ln, bias=eps[:, 0:1], scale=1.0 / (2 * HD)))
                    act.activation(r_, r_, ACT.Exp, scale=-0.5).then_inc(sub_root, 1)
                if n < DIFF_HEADS:
                    act.wait_ge(max_ready, n + 1)
                    st = b1["stat"][:, n % 2, :]
                    for j in range(4):
                        w = P + META if j < 2 else L
                        pr = h1["probs"][:, n % 2, j, 0:w]
                        act.activation(pr, pr, ACT.Exp, bias=st[:, 4 + j:5 + j],
                                       accum_out=st[:, 8 + j:9 + j]).then_inc(probs_ready, 1)
                m = n - 4
                if 0 <= m < DIFF_HEADS:
                    act.wait_ge(sub_ready, m + 1)
                    act.copy(b1["oh"][:, m * SEQ:(m + 1) * SEQ], h1["o"][:, m % 2, :]).then_inc(oh_ready, 1)
                m = n - 2
                if 0 <= m < DIFF_HEADS:
                    act.wait_ge(wt_done, m + 1)
                    if m >= 2:
                        act.wait_ge(do_done, m - 1)
                    act.copy(h1["wT"][:, m % 2, 0:3 * P], ps[:, 4, 0:3 * P]).then_inc(wt_ev_a, 1)
                m = n - 3
                if 0 <= m < DIFF_HEADS:
                    act.wait_ge(do_done, m + 1)
                    if m >= 2:
                        act.wait_ge(ol_ready, KD + m - 1)
                    act.copy(h1["o"][:, m % 2, :], ps[:, 7, 0:SEQ]).then_inc(do_ev, 1)
                    act.activation(h1["sq"][:, m % 2, :], ps[:, 7, 0:SEQ], ACT.Square).then_inc(do_ev, 1)

            split_high(C_D_O + 1)
            for c in range(C_D_O, C_D_O + 2):
                for k in range(4 * (c - C_D_O), 4 * (c - C_D_O) + 4):
                    act.wait_ge(residual, 2 * KD + k + 1)
                    act.activation(xn3[:, k, :], hT[:, k, :], ACT.Identity,
                                   scale=vecs[:, 3 * KD + k:3 * KD + k + 1]).then_inc(gained, 1)
            for n in range(4):
                act.wait_ge(back_done, n + 1)
                act.activation(sq3[:, n * BANK:(n + 1) * BANK], ps[:, BACKS[n], :], ACT.Square,
                               accum_out=small[:, 10 + n:11 + n]).then_inc(tok_squared, 1)
            act.wait_ge(tok_summed, 1)
            a_step(act.activation(small[:, 14:16], small[:, 14:16], ACT.Identity, bias=eps[:, 0:1], scale=1.0 / D))
            a_step(act.activation(small[:, 16:18], small[:, 14:16], ACT.Ln))
            act.activation(small[:, 16:18], small[:, 16:18], ACT.Exp, scale=-0.5).then_inc(rooted, 1)

            def unit_split(u, p):
                j = min(p, CPU - 1)
                slot, s, to = piece(p)
                act.wait_ge(raw_landed[slot], u * (16 * FC) + 16 * ((C_MOE + j) // 3 + 1))
                act.wait_ge(wh_used, u * PIECES + C_MOE + p - 1)
                act.wait_ge(wl_ready, u * PIECES + C_MOE + p - 1)
                act.copy(wh[:, p % 2, 0:to], raw[:, slot, s:s + to]).then_inc(wh_ready, 1)

            unit_split(0, 0)
            act.wait_ge(rsT_scaled, 1)
            for n in range(4, 8):
                act.wait_ge(back_done, n + 1)
                act.mul(bm["tok"][:, n % 2, (n - 4) // 2 * BANK:((n - 4) // 2 + 1) * BANK], ps[:, BACKS[n], :],
                        rsT[:, n % 2:n % 2 + 1]).then_inc(back_ev, 1)
            unit_split(0, 1)

            def gathered_high(k):
                for h in range(2):
                    act.wait_ge(gathered, k * 2 + h - 1)
                    s = slice(h * BANK, (h + 1) * BANK)
                    act.copy(bm["gh"][:, s], ps[:, 5 + h, :]).then_inc(gh_ready, 1)

            gathered_high(1)
            act.wait_ge(gap_ready, 1)
            act.activation(bm["one"][:, 5, :], bm["one"][:, 4, :], ACT.Exp).then_inc(gap_exp, 1)
            act.preload_act_table_set(SILU)
            act.wait_ge(routed, 1)
            units = act.value_load(bm["unit_i"][0:1, 15:16], min_val=E, max_val=MAX_UNITS)


            def output_out(u):
                act.wait_ge(w_used, u * PIECES + C_MOE)
                for h in range(2):
                    act.copy(bm["y"][:, h * BANK:(h + 1) * BANK], ps[:, 2 + h, :]).then_inc(y_ev, 1)

            with act.Fori(0, units) as u:
                def turned_high(i):
                    act.wait_ge(eT_done, u * FC + i + 1)
                    act.copy(bm["eah"][:], ps[:, 4, :]).then_inc(eah_ready, 1)

                with act.If(u > 0):
                    unit_split(u, 0)
                    output_out(u)
                    unit_split(u, 1)
                for j, (kind, i) in enumerate(unit_chunks):
                    if j + 2 < CPU:
                        unit_split(u, j + 2)
                    if (kind, i) == ("g", 1):
                        turned_high(0)
                    if kind == "g":
                        act.wait_ge(w_used, u * PIECES + C_MOE + j + 1)
                        if i:
                            act.wait_ge(eprod_ready, u * FC + i)
                        act.activation(bm["sil"][:], ps[:, 0, :], ACT.Silu).then_inc(esil_ready, 1)
                    if kind == "d" and i + 1 < FC:
                        turned_high(i + 1)
                        if i + 1 == FC - 1:
                            unit_split(u, PIECES - 1)
                        if i + 1 == 3:
                            act.wait_ge(payT_done, u + 1)
                            act.copy(bm["payT"][:], ps[:, 7, 0:SEQ]).then_inc(payT_ev, 1)
                        if i + 1 == FC - 1:
                            gathered_high(u + 2)

            output_out(units)

            for t in range(QT):
                act.wait_ge(acc_done, units * 4 + 3 + t)
                act.activation(bm["tok"][:, t, :], bm["acc"][:, t, :], ACT.Square,
                               accum_out=small[:, 4 + t:5 + t]).then_inc(fin_sq, 1)
            act.wait_ge(fin_sq, QT)
            act.activation(small[:, 6:8], small[:, 4:6], ACT.Sqrt, bias=eps[:, 0:1], scale=1.0 / D).then_inc(fin_root, 1)

        @block.vector
        def _(dve):
            steps = [0]

            def step(ins):
                steps[0] += 1
                ins.then_inc(dve_step, 1)
                dve.wait_ge(dve_step, steps[0])

            def split_low(c):
                dve.wait_ge(wh_ready, c + 1)
                if c >= 2:
                    dve.wait_ge(w_used, c - 1)
                n = size[c]
                dve.tensor_tensor(wl[:, c % 2, 0:n], raw[:, c % 3, 0:n], raw_f(wh[:, c % 2, 0:n]),
                                  ALU.subtract).then_inc(wl_ready, 1)

            def gained_low(n, k):
                dve.wait_ge(xh_ready, KD * n + k + 1)
                s = slice(k * L, (k + 1) * L)
                dve.scalar_tensor_tensor(out=xl[:, s], in0=hT[:, k, :], scalar=vecs[:, n * KD + k:n * KD + k + 1],
                                         in1=raw_f(xh[:, s]), op0=ALU.mult, op1=ALU.subtract).then_inc(xl_ready, 1)

            def polish(n):
                dve.wait_ge(rooted, n + 1)
                step(dve.scalar_tensor_tensor(out=var[:], in0=var[:], scalar=-0.5, in1=rs[:], op0=ALU.mult, op1=ALU.mult))
                step(dve.tensor_tensor(var[:], var[:], rs[:], ALU.mult))
                dve.scalar_tensor_tensor(out=rs[:], in0=var[:], scalar=1.5, in1=rs[:], op0=ALU.add,
                                         op1=ALU.mult).then_inc(rs_ready, 1)
                dve.wait_ge(rs_ready, n + 1)

            def feed_low(f):
                dve.wait_ge(ah_ready, f + 1)
                dve.tensor_tensor(bf["al"][:, f, :], xn3[:, f % 8, :], raw_f(bf["ah"][:, f, :]),
                                  ALU.subtract).then_inc(al_ready, 1)

            def add_tile(n, bank, first):
                dve.tensor_tensor(hT[:, n, first:L], hT[:, n, first:L], ps[:, bank, 0:L - first], ALU.add).then_inc(residual, 1)

            step(dve.memset(vec_rows[:], 0.0))
            dve.nop().then_inc(rows_zero, 1)
            dve.memset(eps[:], EPS).then_inc(pads, 1)
            dve.memset(b0["k"][:, KD * L:], 0.0).then_inc(pads, 1)
            for n in (1, 4):
                dve.wait_ge(turned, n + 1)
                src = ps[:, n, :].rearrange("p (k t) -> p k t", t=P)
                dve.tensor_copy(hT[:, 4 * (n // 3):4 * (n // 3) + 4, P:2 * P], src).then_inc(turned_dve, 1)
            dve.wait_ge(turned_dve, 2)
            dve.wait_ge(vec_ev, 1)
            for k in range(KD):
                gained_low(0, k)
            split_low(0)
            dve.tensor_tensor(small[:, 0:1], vecs[:, 33:34], vecs[:, 34:35], ALU.mult)
            step(dve.tensor_tensor(small[:, 1:2], vecs[:, 35:36], vecs[:, 36:37], ALU.mult))
            dve.tensor_scalar(gsub[:], vecs[:, 32:33], 1.0 - LAMBDA_INIT, None, ALU.mult).then_inc(lam_sum_in, 1)
            split_low(1)
            polish(0)
            dve.wait_ge(lam_exp, 1)
            step(dve.tensor_tensor(neg_lam[:], small[:, 3:4], small[:, 2:3], ALU.subtract))
            step(dve.tensor_scalar(neg_lam[:], neg_lam[:], LAMBDA_INIT, None, ALU.subtract))

            for c in range(6):
                if c == 4:
                    dve.wait_ge(turned, 6)
                    dve.memset(b0["v"][:, 2, :], 0.0).then_inc(v_zero, 1)
                for m in range(4):
                    tt = 4 * c + m
                    await_tile(dve, tile_done, 3 * c, c, m, 4)
                    if c < 2:
                        dve.scalar_tensor_tensor(out=b0["q"][:, tt, :], in0=ps[:, tt % 4, 0:L], scalar=SCALE, in1=rs[:],
                                                 op0=ALU.mult, op1=ALU.mult).then_inc(tile_ev, 1)
                    else:
                        dst = b0["k"][:, (tt - KD) * L:(tt - KD + 1) * L] if c < 4 else xn3[:, tt - 2 * KD, :]
                        dve.tensor_tensor(dst, ps[:, tt % 4, 0:L], rs[:], ALU.mult).then_inc(tile_ev, 1)
                if c < 5:
                    split_low(c + 2)

            dve.wait_ge(keep_in, 16)
            dve.wait_ge(w_used, C_SB_O)
            neg_keep, strict_bias = b0["neg_keep"][:], h0["bias"][:]
            for parts_ in (h0["keep_h"], h0["keep_l"]):
                for slot in range(2):
                    ins = dve.memset(raw_f(parts_[:, slot, SCW:KEEP2]), 0.0)
            ins.then_inc(gap_zero, 1)
            for n in range(SB_HEADS + 4):
                m = n - 1
                if 0 <= m < SB_HEADS:
                    dve.wait_ge(kh_ready, m + 1)
                    a, kh, kl = (h0[b_][:, m % 2, :] for b_ in ("soft", "keep_h", "keep_l"))
                    dve.tensor_tensor(kl[:, 0:SCW], a, raw_f(kh[:, 0:SCW]), ALU.subtract)
                    dve.tensor_tensor(kl[:, KEEP2:KEEPW], a[:, 0:KT2[2]], raw_f(kh[:, KEEP2:KEEPW]),
                                      ALU.subtract).then_inc(keep_ready, 1)
                m = n - 2
                if 0 <= m < SB_HEADS:
                    if m == 0:
                        dve.wait_ge(bias_in, 16)
                    dve.wait_ge(soft_done, m + 1)
                    if m >= 2:
                        dve.wait_ge(pv_done, m - 1)
                    dve.tensor_tensor(h0["att"][:, m % 2, :], ps[:, m % 4, 0:SCW], strict_bias,
                                      ALU.add).then_inc(expo_ready, 1)
                if n < SB_HEADS:
                    a = h0["soft"][:, n % 2, :]
                    dve.wait_ge(log_done, n + 1)
                    step(dve.scalar_tensor_tensor(out=a, in0=ps[:, n % 4, 0:SCW], scalar=0.0, in1=a,
                                                  op0=ALU.max, op1=ALU.add))
                    dve.tensor_tensor(a, a, neg_keep, ALU.mult).then_inc(masked, 1)
                m = n - 4
                if 0 <= m < SB_HEADS and m % 2 == 1:
                    i = m // 2
                    dve.wait_ge(oh_ready, i + 1)
                    s = slice(i * L, (i + 1) * L)
                    dve.tensor_tensor(b0["ol"][:, s], ps[:, 4 + i % 2, 0:L], raw_f(b0["oh"][:, s]), ALU.subtract).then_inc(ol_ready, 1)

            split_low(C_SB_O + 1)
            for c in range(C_SB_O, C_SB_O + 2):
                for n in range(4 * (c - C_SB_O), 4 * (c - C_SB_O) + 4):
                    await_tile(dve, add_done, 3 * (c - C_SB_O), c, n % 4, 4)
                    add_tile(n, n % 4, 0)
                    if n:
                        gained_low(1, n - 1)
                if c > C_SB_O:
                    gained_low(1, KD - 1)
                split_low(c + 2)

            polish(1)
            for i in range(N_UP):
                for f in range(4 * i, 4 * i + up_tiles(i)):
                    await_tile(dve, g_done, 3 * i, C_UP + 2 * i, f - 4 * i, up_tiles(i))
                    if f >= 8:
                        dve.wait_ge(al_ready, f - 7)
                    dve.tensor_tensor(xn3[:, f % 8, :], ps[:, f % 4, 0:L], rs[:], ALU.mult).then_inc(g_free, 1)
                split_low(C_UP + 2 * i + 2)
                for f in range(4 * i, 4 * i + up_tiles(i)):
                    dve.wait_ge(sil_ready, f + 1)
                    dve.tensor_tensor(xn3[:, f % 8, :], xn3[:, f % 8, :], rs[:], ALU.mult).then_inc(sil_scaled, 1)
                for f in range(4 * i, 4 * i + up_tiles(i)):
                    await_tile(dve, u_done, 3 * i, C_UP + 2 * i + 1, f - 4 * i, up_tiles(i))
                    dve.wait_ge(sil_scaled, f + 1)
                    dve.tensor_tensor(xn3[:, f % 8, :], xn3[:, f % 8, :], ps[:, 4 + f % 4, 0:L],
                                      ALU.mult).then_inc(prod_ready, 1)
                    if f > 4 * i:
                        feed_low(f - 1)
                feed_low(f)
                split_low(C_UP + 2 * i + 3)
            for i in range(N_DOWN):
                if i == N_DOWN - 1:
                    for n in range(KD):
                        await_tile(dve, add_done, 6, C_DOWN + i, n, KD)
                        add_tile(n, n, 0)
                        if n:
                            gained_low(2, n - 1)
                    gained_low(2, KD - 1)
                    split_low(C_DOWN + i + 1)
                if i != N_DOWN - 2:
                    split_low(C_DOWN + i + 2)

            polish(2)
            dve.wait_ge(diff_in, 16)
            con = b1["con"]
            causal, swap, cos, sin = con[:, 0:L], con[:, L:L + P], con[:, L + P:2 * L + P], con[:, 2 * L + P:3 * L + P]

            def rotate(tt):
                q = tt < KD
                w, first = (SEQ, META) if q else (L, 0)
                dst = b1["q"][:, tt * SEQ:(tt + 1) * SEQ] if q else b1["k"][:, (tt - KD) * L:(tt - KD + 1) * L]
                src = xn3[:, tt % 8, 0:w]
                dve.wait_ge(swap_done, tt + 1)
                dve.tensor_tensor(dst, ps[:, 4 + tt % 2, 0:w], sin[:, first:L], ALU.mult)
                step(dve.tensor_tensor(src, src, cos[:, first:L], ALU.mult))
                dve.tensor_tensor(dst, dst, src, ALU.add).then_inc(rope_done, 1)

            for c in range(6):
                for m in range(4):
                    tt = 4 * c + m
                    await_tile(dve, tile_done, 18 + 3 * c, C_D_QKV + c, m, 4)
                    if tt >= 8:
                        dve.wait_ge(rope_done, tt - 7)
                    if c < 2:
                        dve.scalar_tensor_tensor(out=xn3[:, tt % 8, 0:SEQ], in0=ps[:, tt % 4, 0:SEQ], scalar=SCALE,
                                                 in1=rs[:, META:L], op0=ALU.mult, op1=ALU.mult).then_inc(tile_ev, 1)
                    else:
                        dve.tensor_tensor(xn3[:, tt % 8, :], ps[:, tt % 4, 0:L], rs[:], ALU.mult).then_inc(tile_ev, 1)
                    if 1 <= tt <= 2 * KD:
                        rotate(tt - 1)
                if c < 5:
                    split_low(C_D_QKV + c + 2)

            for n in range(DIFF_HEADS + 5):
                if n < DIFF_HEADS:
                    st = b1["stat"][:, n % 2, :]
                    if n >= 2:
                        dve.wait_ge(wt_done, n - 1)
                    for comp in range(2):
                        dve.wait_ge(ds_done, 2 * n + comp + 1)
                        for t in range(2):
                            j, c0, w = 2 * t + comp, t * (P + META), P + META if t == 0 else L
                            ins = dve.tensor_tensor_reduce(
                                h1["probs"][:, n % 2, j, 0:w], ps[:, (2 * n + comp) % 4, c0:c0 + w],
                                causal[:, L - w:L], 1.0, -3e38, ALU.add, ALU.max, st[:, j:j + 1])
                        ins.then_inc(ds_free, 1)
                    dve.wait_ge(ds_free, 2 * n + 2)
                    dve.tensor_scalar(st[:, 4:8], st[:, 0:4], -1.0, None, ALU.mult).then_inc(max_ready, 1)
                m = n - 4
                if 0 <= m < DIFF_HEADS:
                    o_ = h1["o"][:, m % 2, :]
                    dve.wait_ge(sub_root, m + 1)
                    dve.scalar_tensor_tensor(out=o_, in0=o_, scalar=gsub[:, 0:1], in1=h1["sq"][:, m % 2, :],
                                             op0=ALU.mult, op1=ALU.mult).then_inc(sub_ready, 1)
                m = n - 1
                if 0 <= m < DIFF_HEADS:
                    st = b1["stat"][:, m % 2, :]
                    dve.wait_ge(probs_ready, 4 * m + 4)
                    step(dve.reciprocal(st[:, 8:12], st[:, 8:12]))
                    step(dve.tensor_scalar(st[:, 12:14], st[:, 9:12:2], neg_lam[:, 0:1], None, ALU.mult))
                    for t in range(2):
                        w = P + META if t == 0 else L
                        p1, p2 = h1["probs"][:, m % 2, 2 * t, 0:w], h1["probs"][:, m % 2, 2 * t + 1, 0:w]
                        step(dve.tensor_scalar(p1, p1, st[:, 8 + 2 * t:9 + 2 * t], None, ALU.mult))
                        dve.scalar_tensor_tensor(out=p1, in0=p2, scalar=st[:, 12 + t:13 + t], in1=p1,
                                                 op0=ALU.mult, op1=ALU.add).then_inc(mix_ready, 1)
                m = n - 2
                if 0 <= m < DIFF_HEADS:
                    dve.wait_ge(wt_done, m + 1)
                    if m >= 2:
                        dve.wait_ge(do_done, m - 1)
                    dve.tensor_copy(h1["wT"][0:META, m % 2, 3 * P:], ps[0:META, 6, 0:SEQ]).then_inc(wt_ev_m, 1)
                m = n - 4
                if 0 <= m < DIFF_HEADS:
                    s, o_ = slice(m * SEQ, (m + 1) * SEQ), h1["o"][:, m % 2, :]
                    dve.wait_ge(oh_ready, KD + m + 1)
                    dve.tensor_tensor(b1["ol"][:, s], o_, raw_f(b1["oh"][:, s]), ALU.subtract).then_inc(ol_ready, 1)
            split_low(C_D_O + 1)
            for c in range(C_D_O, C_D_O + 2):
                for n in range(4 * (c - C_D_O), 4 * (c - C_D_O) + 4):
                    await_tile(dve, add_done, 13 + 3 * (c - C_D_O), c, n % 4, 4)
                    add_tile(n, n % 4, META)

            def unit_split(u, p):
                slot, s, to = piece(p)
                dve.wait_ge(wh_ready, u * PIECES + C_MOE + p + 1)
                dve.wait_ge(w_used, u * PIECES + C_MOE + p - 1)
                dve.tensor_tensor(wl[:, p % 2, 0:to], raw[:, slot, s:s + to], raw_f(wh[:, p % 2, 0:to]),
                                  ALU.subtract).then_inc(wl_ready, 1)

            r, one, over, unit_f = bm["r"], bm["one"], bm["over"], bm["unit_f"]
            lg, key, top1, lg2, key2, top2, sel, gat, posp, posm = (r[:, i] for i in range(10))
            m1, m2, gap, eg, g1, g2 = one[:, 0], one[:, 1], one[:, 4], one[:, 5], one[:, 6], one[:, 7]
            for n in range(4):
                dve.wait_ge(tok_squared, n + 1)
                if n == 3:
                    dve.tensor_tensor(small[:, 14:16], small[:, 10:12], small[:, 12:14], ALU.add).then_inc(tok_summed, 1)
                dve.tensor_copy(bm["acc"][:, n % 2, n // 2 * BANK:(n // 2 + 1) * BANK], ps[:, BACKS[n], :]).then_inc(acc_ev, 1)
            dve.wait_ge(rooted, 4)
            step(dve.tensor_tensor(small[:, 18:20], small[:, 14:16], small[:, 16:18], ALU.mult))
            step(dve.tensor_tensor(small[:, 18:20], small[:, 18:20], small[:, 16:18], ALU.mult))
            step(dve.tensor_scalar(small[:, 18:20], small[:, 18:20], -0.5, 1.5, ALU.mult, ALU.add))
            dve.tensor_tensor(rsT[:, 0:QT], small[:, 18:20], small[:, 16:18], ALU.mult).then_inc(rsT_scaled, 1)
            dve.wait_ge(route_in, 32)
            before, slots, desc = rcon[:, 0:P], rcon[:, P:2 * P], rcon[:, 2 * P:2 * P + E]
            dve.memset(bm["pos"][:], 0.0)
            dve.memset(bm["gate"][:], 0.0)
            dve.wait_ge(logit_done, 1)
            step(dve.tensor_copy(lg, ps[:, 0, 0:QT * E].rearrange("p (t e) -> p t e", e=E)))

            def best(src, key, top, m, km):
                step(dve.tensor_reduce(m, src, AX_X, ALU.max))
                for t in range(QT):
                    ins = dve.scalar_tensor_tensor(out=key[:, t], in0=src[:, t], scalar=m[:, t:t + 1], in1=desc,
                                                   op0=ALU.is_equal, op1=ALU.mult)
                step(ins)
                step(dve.tensor_reduce(km, key, AX_X, ALU.max))
                for t in range(QT):
                    ins = dve.tensor_scalar(top[:, t], key[:, t], km[:, t:t + 1], None, ALU.is_equal)
                step(ins)

            best(lg, key, top1, m1, one[:, 2])
            step(dve.scalar_tensor_tensor(out=lg2, in0=top1, scalar=-3e38, in1=lg, op0=ALU.mult, op1=ALU.add))
            best(lg2, key2, top2, m2, one[:, 3])
            dve.tensor_tensor(sel, top1, top2, ALU.add).then_inc(sel_ready, 1)
            dve.wait_ge(pos_done, 1)
            step(dve.scalar_tensor_tensor(out=bm["pos"][:, :, 0:E],
                                          in0=ps[:, 7, 0:QT * E].rearrange("p (t e) -> p t e", e=E), scalar=1.0,
                                          in1=sel, op0=ALU.add, op1=ALU.mult))
            posp = bm["pos"][:, :, 0:E]

            def pick(u):
                for t in range(QT):
                    ins = dve.tensor_scalar(bm["pick"][:, t, :], slots, bm["pos"][:, t, bass.ds(u, 1)], None, ALU.is_equal)
                ins.then_inc(pick_ready, 1)

            pick(0)
            unit_split(0, 0)
            numbers = rcon[:, 2 * P + E:2 * P + 2 * E]
            more = over[:, 0]
            dve.tensor_scalar(posm, posp, float(P), None, ALU.subtract)
            dve.memset(unit_f[:], 0.0)
            step(dve.tensor_scalar(more, ps[:, 7, QT * E:(QT + 1) * E], P + 0.5, None, ALU.is_gt))
            step(dve.tensor_tensor_scan(over[:, 1], more, more, 0.0, ALU.add, ALU.max))
            step(dve.tensor_tensor(over[:, 1], over[:, 1], more, ALU.mult))
            for j in range(MAX_UNITS - E):
                ins = dve.tensor_scalar(over[:, 2 + j], over[:, 1], float(j + 1), None, ALU.is_equal)
            step(ins)
            for j in range(MAX_UNITS - E):
                dve.tensor_tensor_reduce(over[:, 5 + 5 * j], over[:, 2 + j], numbers, 1.0, 0.0, ALU.mult, ALU.add,
                                         unit_f[:, E + j:E + j + 1])
                for t in range(QT):
                    dve.tensor_tensor_reduce(over[:, 6 + 5 * j + 2 * t], over[:, 2 + j], posm[:, t], 1.0, 0.0, ALU.mult, ALU.add,
                                             bm["pos"][:, t, E + j:E + j + 1])
            step(dve.tensor_reduce(unit_f[:, 15:16], more, AX_X, ALU.add))
            step(dve.tensor_scalar(unit_f[:, 15:16], unit_f[:, 15:16], float(E), None, ALU.add))
            dve.tensor_copy(bm["unit_i"][:], unit_f[0:1, :]).then_inc(routed, 1)

            def gathered_low(k):
                for h in range(2):
                    s = slice(h * BANK, (h + 1) * BANK)
                    dve.wait_ge(gh_ready, k * 2 + h - 1)
                    dve.tensor_tensor(bm["gl"][:, s], ps[:, 5 + h, :], raw_f(bm["gh"][:, s]), ALU.subtract).then_inc(gl_ready, 1)

            step(dve.tensor_tensor(gap, m2, m1, ALU.subtract))
            dve.wait_ge(rsT_scaled, 1)
            dve.tensor_tensor(gap, gap, rsT[:, 0:QT], ALU.mult).then_inc(gap_ready, 1)
            gathered_low(1)
            unit_split(0, 1)
            dve.wait_ge(gap_exp, 1)
            step(dve.tensor_scalar(g1, eg, 1.0, None, ALU.add))
            step(dve.reciprocal(g1, g1))
            step(dve.tensor_tensor(g2, eg, g1, ALU.mult))
            for t in range(QT):
                ins = dve.tensor_scalar(gat[:, t], top1[:, t], g1[:, t:t + 1], None, ALU.mult)
            step(ins)
            for t in range(QT):
                ins = dve.scalar_tensor_tensor(out=bm["gate"][:, t, 0:E], in0=top2[:, t], scalar=g2[:, t:t + 1],
                                               in1=gat[:, t], op0=ALU.mult, op1=ALU.add)
            step(ins)
            for j in range(MAX_UNITS - E):
                for t in range(QT):
                    ins = dve.tensor_tensor_reduce(over[:, 7 + 5 * j + 2 * t], over[:, 2 + j], bm["gate"][:, t, 0:E],
                                                   1.0, 0.0, ALU.mult, ALU.add, bm["gate"][:, t, E + j:E + j + 1])
            step(ins)
            dve.wait_ge(routed, 1)
            units = dve.value_load(bm["unit_i"][0:1, 15:16], min_val=E, max_val=MAX_UNITS)
            dve.wait_ge(acc_ev, 4)
            dve.nop().then_inc(acc_done, 4)

            def add_unit(u, first, end):
                for n in range(first, end):
                    dve.wait_ge(sc_done, u * 4 + n + 1)
                    a = bm["acc"][:, n % 2, n // 2 * BANK:(n // 2 + 1) * BANK]
                    dve.tensor_tensor(a, a, ps[:, SUMS[n], :], ALU.add).then_inc(acc_done, 1)

            with dve.Fori(0, units) as u:
                def turned_low(i):
                    dve.wait_ge(eah_ready, u * FC + i + 1)
                    dve.tensor_tensor(bm["eal"][:], ps[:, 4, :], raw_f(bm["eah"][:]), ALU.subtract).then_inc(eal_ready, 1)

                with dve.If(u > 0):
                    unit_split(u, 0)
                    add_unit(u, 0, 1)
                    unit_split(u, 1)
                for j, (kind, i) in enumerate(unit_chunks):
                    if kind == "u":
                        dve.wait_ge(esil_ready, u * FC + i + 1)
                        dve.wait_ge(w_used, u * PIECES + C_MOE + j + 1)
                        if i:
                            dve.wait_ge(eT_done, u * FC + i)
                        dve.tensor_tensor(bm["act"][:], bm["sil"][:], ps[:, 1, :], ALU.mult).then_inc(eprod_ready, 1)
                    if (kind, i) == ("g", 1):
                        turned_low(0)
                    if j + 2 < CPU:
                        unit_split(u, j + 2)
                    if (kind, i) == ("u", 0):
                        with dve.If(u > 0):
                            add_unit(u, 1, 4)
                    if kind == "d" and i + 1 < FC:
                        turned_low(i + 1)
                        if i + 1 == FC - 1:
                            unit_split(u, PIECES - 1)
                        if i == 1:
                            for t in range(QT):
                                ins = dve.tensor_scalar(bm["pay"][:, t, :], slots, bm["pos"][:, t, bass.ds(u, 1)],
                                                        bm["gate"][:, t, bass.ds(u, 1)], ALU.is_equal, ALU.mult)
                            ins.then_inc(pay_ready, 1)
                        if i == 2:
                            dve.wait_ge(gathered, u * 2 + 2)
                            pick(u + 1)
                        if i + 1 == FC - 1:
                            gathered_low(u + 2)
            add_unit(units, 0, 4)

            dve.wait_ge(gain_in, 16)
            dve.wait_ge(fin_root, 1)
            dve.reciprocal(small[:, 8:10], small[:, 6:8]).then_inc(fin_rec, 1)
            dve.wait_ge(fin_rec, 1)
            for t in range(QT):
                dve.scalar_tensor_tensor(out=bm["tok"][:, t, :], in0=bm["acc"][:, t, :], scalar=small[:, 8 + t:9 + t],
                                         in1=xn[:, 0:D], op0=ALU.mult, op1=ALU.mult).then_inc(fin_ready, 1)

        @block.tensor
        def _(pe):
            def chunk_products(c, tiles, k_tiles, ncols, outp, highs, lows, tile_free, last_done,
                               await_k=None, after_high=None, first=True, last=True):
                high, low = wh[:, c % 2, :], wl[:, c % 2, :]
                pe.wait_ge(wh_ready, c + 1)
                for m in range(tiles):
                    tile_free(m)
                    for k in range(k_tiles):
                        if await_k and m == 0:
                            await_k(k)
                        w = high[:, k * ncols + m * P:k * ncols + (m + 1) * P]
                        pe.matmul(outp(m), w, highs(k), start=first and k == 0, stop=False, skip_group_check=True)
                        ins = pe.matmul(outp(m), w, lows(k), start=False, stop=False, skip_group_check=True)
                    if m == tiles - 1:
                        ins.then_inc(wh_used, 1)
                    if after_high:
                        after_high(m)
                pe.wait_ge(wl_ready, c + 1)
                for m in range(tiles):
                    for k in range(k_tiles):
                        w = low[:, k * ncols + m * P:k * ncols + (m + 1) * P]
                        ins = pe.matmul(outp(m), w, highs(k), start=False, stop=last and k == k_tiles - 1,
                                        skip_group_check=True)
                    if last_done:
                        tile_signal(ins, last_done, m, tiles)
                    elif m == tiles - 1:
                        ins.then_inc(w_used, 1)

            def norm_sum(n):
                for k in range(KD):
                    pe.wait_ge(squared, KD * n + k + 1)
                    ins = pe.matmul(ps[:, 7, 0:L], ones, xn3[:, k, :], start=(k == 0), stop=(k == KD - 1))
                ins.then_inc(summed, 1)

            def gained_parts(n):
                return lambda k: pe.wait_ge(xl_ready, KD * n + k + 1)

            pe.wait_ge(base_in, 16)
            pe.wait_ge(x_in, 64)
            for n in range(6):
                g, t = n // 3, n % 3
                w = P if t < 2 else META
                for k in range(4):
                    ins = pe.transpose(ps[:, n, k * w:(k + 1) * w],
                                       tokens_in[0:w, t, (4 * g + k) * P:(4 * g + k + 1) * P], ident[0:w, 0:w])
                ins.then_inc(turned, 1)
            pe.wait_ge(vec_in, 96)
            pe.transpose(ps[:, 6, 0:48], vec_rows[:, :], ident[0:48, 0:48]).then_inc(vec_turned, 1)

            def part(x_, s, stride):
                return lambda k: x_[:, k * stride + s.start:k * stride + s.stop]

            pe.wait_ge(pads, 2)
            def turn_values(base, cc, t, firsts):
                vi, w = 3 * cc + t, tile_rows(firsts, t)
                pe.wait_ge(tile_ev, 4 * base + 2 * KD + 4 * cc + 4)
                if vi >= 4:
                    pe.wait_ge(v_ev, base + vi - 3)
                for m in range(4):
                    ins = pe.transpose(ps[0:w, 4 + vi % 4, m * P:(m + 1) * P], xn3[:, 4 * cc + m, firsts[t]:firsts[t] + w],
                                       ident)
                ins.then_inc(v_turned, 1)

            for c in range(6):
                def tile_free(m):
                    if c:
                        pe.wait_ge(tile_ev, 4 * c + m - 3)

                def after_high(m):
                    if (c, m) == (0, 0):
                        norm_sum(0)
                    if (c, m) == (0, 3):
                        pe.wait_ge(lam_sum_in, 1)
                        pe.matmul(ps[:, 5, 0:2], ones, small[:, 0:2], start=True, stop=True).then_inc(lam_sum, 1)
                    if (c, m) == (5, 0):
                        pe.wait_ge(lam_exp, 1)
                    if c == 5 and m < 3:
                        turn_values(0, 0, m, TOKENS0)

                chunk_products(c, 4, KD, WIDE, lambda m: ps[:, m, 0:L], part(xh, slice(0, L), L),
                               part(xl, slice(0, L), L), tile_free, tile_done,
                               await_k=gained_parts(0) if c == 0 else None, after_high=after_high)
            for t in range(3):
                turn_values(0, 1, t, TOKENS0)

            q0, k0, v0 = b0["q"], b0["k"], b0["v"]
            for n in range(SB_HEADS + 3):
                if n < SB_HEADS:
                    i, rows_ = n // 2, slice(HD * (n % 2), HD * (n % 2) + HD)
                    if n >= 4:
                        pe.wait_ge(expo_ready, n - 3)
                    for first, col, width in KEY_TILES:
                        ins = pe.matmul(ps[:, n % 4, col:col + width], k0[rows_, i * L + first:i * L + first + P],
                                        q0[rows_, i, first:L], start=(first == 0), stop=False, skip_group_check=True)
                    ins.then_inc(score_done, 1)
                m = n - 2
                if 0 <= m < SB_HEADS:
                    pe.wait_ge(keep_ready, m + 1)
                    if m == 0:
                        pe.wait_ge(gap_zero, 1)
                        pe.wait_ge(sums_ready, 1)
                    after0 = KT0[1] + KT0[2]
                    for name in ("keep_h", "keep_l"):
                        keep = h0[name][:, m % 2, :]
                        pe.matmul(ps[:, m % 4, 0:SCW], sums_r[:, 0:P], keep[:, 0:SCW],
                                  start=False, stop=False, skip_group_check=True)
                        pe.matmul(ps[:, m % 4, KT0[1] + P:SCW], sums_r[:, P:2 * P], keep[:, KT1[1]:KEEPW],
                                  start=False, stop=False, skip_group_check=True)
                        ins = pe.matmul(ps[:, m % 4, after0 - KT2[2]:after0], sums_r[:, P:2 * P], keep[:, 0:KT2[2]],
                                        start=False, stop=(name == "keep_l"), skip_group_check=True)
                    ins.then_inc(soft_done, 1)
                m = n - 3
                if 0 <= m < SB_HEADS:
                    i, rows_ = m // 2, slice(HD * (m % 2), HD * (m % 2) + HD)
                    pe.wait_ge(att_ready, m + 1)
                    if m == 0:
                        pe.wait_ge(v_ev, 6)
                    if i >= 2 and m % 2 == 0:
                        pe.wait_ge(ol_ready, i - 1)
                    for t, (first, col, width) in enumerate(KEY_TILES):
                        ins = pe.matmul(ps[rows_, 4 + i % 2, first:L], v0[:, t, m * HD:(m + 1) * HD],
                                        h0["att"][:, m % 2, col:col + width], start=(t == 0), stop=(t == 2),
                                        skip_group_check=True)
                    ins.then_inc(pv_done, 1)

            def out_projection(c0, width, ready, oh, ol, freed):
                for c in range(c0, c0 + 2):
                    def tile_free(m):
                        if c > c0:
                            pe.wait_ge(residual, freed + m + 1)

                    def split_k(k):
                        pe.wait_ge(ol_ready, ready + k + 1)

                    chunk_products(c, 4, KD, WIDE, lambda m: ps[:, m, 0:width], part(oh, slice(0, width), width),
                                   part(ol, slice(0, width), width), tile_free, add_done,
                                   await_k=split_k if c == c0 else None)

            out_projection(C_SB_O, L, 0, b0["oh"], b0["ol"], 0)

            for i in range(N_UP):
                for kind in range(2):
                    c = C_UP + 2 * i + kind

                    def tile_free(m):
                        f = 4 * i + m
                        if f >= 4:
                            pe.wait_ge(prod_ready if kind else g_free, f - 3)
                        elif kind == 0:
                            pe.wait_ge(residual, 5 + f)
                        elif f == 3:
                            pe.wait_ge(rooted, 2)

                    def after_high(m):
                        if c == C_UP and m == 0:
                            norm_sum(1)

                    chunk_products(c, up_tiles(i), KD, up_tiles(i) * P, lambda m: ps[:, 4 * kind + m, 0:L],
                                   part(xh, slice(0, L), L), part(xl, slice(0, L), L), tile_free,
                                   u_done if kind else g_done, await_k=gained_parts(1) if c == C_UP else None,
                                   after_high=after_high)
            for i in range(N_DOWN):
                def split_k(k):
                    pe.wait_ge(al_ready, 4 * i + k + 1)

                def tile_free(m):
                    if i == 0 and m == 4:
                        pe.wait_ge(prod_ready, NF)

                chunk_products(C_DOWN + i, KD, up_tiles(i), D, lambda m: ps[:, m, 0:L],
                               lambda k: bf["ah"][:, 4 * i + k, :], lambda k: bf["al"][:, 4 * i + k, :], tile_free,
                               add_done if i == N_DOWN - 1 else None, await_k=split_k,
                               first=(i == 0), last=(i == N_DOWN - 1))

            swap = b1["con"][:, L:L + P]

            def swapped(tt):
                w = SEQ if tt < KD else L
                pe.wait_ge(tile_ev, 24 + tt + 1)
                if tt == 0:
                    pe.wait_ge(diff_in, 16)
                if tt >= 2:
                    pe.wait_ge(rope_done, tt - 1)
                pe.matmul(ps[:, 4 + tt % 2, 0:w], swap, xn3[:, tt % 8, 0:w], start=True, stop=True).then_inc(swap_done, 1)

            for c in range(6):
                def tile_free(m):
                    if c:
                        pe.wait_ge(tile_ev, 24 + 4 * c + m - 3)
                    else:
                        pe.wait_ge(residual, KD + m + 1)

                def after_high(m):
                    if (c, m) == (0, 0):
                        pe.wait_ge(residual, 2 * KD)
                        norm_sum(2)
                    if 1 <= c <= 4:
                        swapped(4 * c + m - 4)
                    if (c, m) == (5, 0):
                        pe.wait_ge(rope_done, 2 * KD)
                    if c == 5 and m < 3:
                        turn_values(6, 0, m, TOKENS1)

                s = slice(META, L) if c < 2 else slice(0, L)
                chunk_products(C_D_QKV + c, 4, KD, WIDE, lambda m: ps[:, m, 0:s.stop - s.start],
                               part(xh, s, L), part(xl, s, L), tile_free, tile_done,
                               await_k=gained_parts(2) if c == 0 else None, after_high=after_high)
            for t in range(3):
                turn_values(6, 1, t, TOKENS1)

            q1, k1, v1 = b1["q"], b1["k"], b1["v"]
            for n in range(DIFF_HEADS + 4):
                if n < DIFF_HEADS:
                    if n >= 2:
                        pe.wait_ge(ds_free, 2 * n - 2)
                    for t in range(2):
                        c0, w = t * (P + META), P + META if t == 0 else L
                        for comp in range(2):
                            rows_ = slice(HD * comp, HD * comp + HD)
                            ins = pe.matmul(ps[:, (2 * n + comp) % 4, c0:c0 + w],
                                            q1[rows_, n * SEQ + t * P:n * SEQ + (t + 1) * P],
                                            k1[rows_, n * L:n * L + w], start=True, stop=True)
                            if t:
                                ins.then_inc(ds_done, 1)
                m = n - 2
                if 0 <= m < DIFF_HEADS:
                    pr = h1["probs"][:, m % 2]
                    pe.wait_ge(mix_ready, 2 * m + 2)
                    if m >= 1:
                        pe.wait_ge(wt_ev_a, m)
                    pe.transpose(ps[:, 4, 0:P], pr[:, 0, META:META + P], ident)
                    pe.transpose(ps[:, 4, P:2 * P], pr[:, 2, META:META + P], ident)
                    pe.transpose(ps[:, 4, 2 * P:3 * P], pr[:, 2, META + P:L], ident)
                    if m >= 1:
                        pe.wait_ge(wt_ev_m, m)
                    pe.transpose(ps[0:META, 6, 0:P], pr[:, 0, 0:META], ident)
                    pe.transpose(ps[0:META, 6, P:2 * P], pr[:, 2, 0:META], ident).then_inc(wt_done, 1)
                m = n - 4
                if 0 <= m < DIFF_HEADS:
                    pe.wait_ge(do_ev, 2 * m + 2)
                    if m >= 1:
                        pe.wait_ge(sub_root, m)
                    pe.matmul(ps[:, 5, 0:SEQ], ones, h1["sq"][:, m % 2, :], start=True, stop=True).then_inc(sub_sum, 1)
                m = n - 3
                if 0 <= m < DIFF_HEADS:
                    wT = h1["wT"][:, m % 2, :]
                    pe.wait_ge(wt_ev_a, m + 1)
                    pe.wait_ge(wt_ev_m, m + 1)
                    if m >= 1:
                        pe.wait_ge(do_ev, 2 * m)
                    cs = slice(m * P, (m + 1) * P)
                    if m == 0:
                        pe.wait_ge(v_ev, 12)
                    pe.matmul(ps[:, 7, 0:SEQ], v1[0:META, 0, cs], wT[0:META, 3 * P:], start=True, stop=False)
                    pe.matmul(ps[:, 7, 0:SEQ], v1[:, 1, cs], wT[:, 0:2 * P], start=False, stop=False)
                    pe.matmul(ps[:, 7, P:SEQ], v1[:, 2, cs], wT[:, 2 * P:3 * P], start=False, stop=True).then_inc(do_done, 1)
            out_projection(C_D_O, SEQ, KD, b1["oh"], b1["ol"], 2 * KD)

            def turn_back(n):
                src = hT if n < 4 else xn3
                t, half = n % 2, n % 4 // 2
                for k in range(4 * half, 4 * half + 4):
                    ins = pe.transpose(ps[:, BACKS[n], k % 4 * P:(k % 4 + 1) * P],
                                       src[:, k, META + t * P:META + (t + 1) * P], ident)
                ins.then_inc(back_done, 1)

            for n in range(4):
                if n % 2 == 0:
                    pe.wait_ge(residual, 2 * KD + 2 * n + 4)
                turn_back(n)
            pe.wait_ge(route_in, 32)
            for k in range(KD):
                pe.wait_ge(gained, k + 1)
                for t in range(QT):
                    ins = pe.matmul(ps[:, 0, t * E:(t + 1) * E], xn3[:, k, META + t * P:META + (t + 1) * P],
                                    wr[:, k, :], start=(k == 0 and t == 0), stop=(k == KD - 1),
                                    skip_group_check=True)
            ins.then_inc(logit_done, 1)
            pe.wait_ge(acc_ev, 4)
            for n in range(4, 8):
                turn_back(n)
            before = rcon[:, 0:P]
            sel = bm["r"][:, 6]
            pe.wait_ge(sel_ready, 1)
            pe.matmul(ps[:, 7, 0:E], before, sel[:, 0], start=True, stop=True)
            pe.matmul(ps[:, 7, E:2 * E], ones, sel[:, 0], start=True, stop=False)
            pe.matmul(ps[:, 7, E:2 * E], before, sel[:, 1], start=False, stop=True)
            pe.matmul(ps[:, 7, 2 * E:3 * E], ones, sel[:, 0], start=True, stop=False)
            pe.matmul(ps[:, 7, 2 * E:3 * E], ones, sel[:, 1], start=False, stop=True).then_inc(pos_done, 1)

            def gather(k, half):
                pe.wait_ge(pick_ready, k + 1)
                for f in range(4 * half, 4 * half + 4):
                    for t in range(QT):
                        ins = pe.matmul(ps[:, 5 + f // 4, f % 4 * P:(f % 4 + 1) * P], bm["tok"][:, t, f * P:(f + 1) * P],
                                        bm["pick"][:, t, :], start=(t == 0), stop=(t == QT - 1))
                ins.then_inc(gathered, 1)

            pe.wait_ge(back_ev, 4)
            gather(0, 0)
            gather(0, 1)
            pe.nop().then_inc(sc_done, 4)
            pe.wait_ge(routed, 1)
            units = pe.value_load(bm["unit_i"][0:1, 15:16], min_val=E, max_val=MAX_UNITS)
            with pe.Fori(0, units) as u:
                gh, gl = bm["gh"], bm["gl"]

                def up(i, kind):
                    j, bank = at[kind, i], 0 if kind == "g" else 1
                    high, low = wh[:, j % 2, :], wl[:, j % 2, :]
                    if i:
                        pe.wait_ge(esil_ready if kind == "g" else eprod_ready, u * FC + i)
                    pe.wait_ge(wh_ready, u * PIECES + C_MOE + j + 1)
                    for k in range(KD):
                        w, s = high[:, k * WIDE:(k + 1) * WIDE], slice(k * P, (k + 1) * P)
                        pe.matmul(ps[:, bank, :], gh[:, s], w, start=(k == 0), stop=False)
                        ins = pe.matmul(ps[:, bank, :], gl[:, s], w, start=False, stop=False)
                    ins.then_inc(wh_used, 1)
                    pe.wait_ge(wl_ready, u * PIECES + C_MOE + j + 1)
                    for k in range(KD):
                        s = slice(k * P, (k + 1) * P)
                        ins = pe.matmul(ps[:, bank, :], gh[:, s], low[:, k * WIDE:(k + 1) * WIDE], start=False, stop=(k == KD - 1))
                    ins.then_inc(w_used, 1)

                def down(i, k0=0, n=4):
                    p = at["d", i] + k0 // 2
                    high, low = wh[:, p % 2, :], wl[:, p % 2, :]
                    ah, al = bm["eah"], bm["eal"]
                    pe.wait_ge(eal_ready, u * FC + i + 1)
                    pe.wait_ge(wh_ready, u * PIECES + C_MOE + p + 1)
                    for k in range(n):
                        s = slice((k0 + k) * P, (k0 + k + 1) * P)
                        for h in range(2):
                            w = high[:, k * D + h * BANK:k * D + (h + 1) * BANK]
                            pe.matmul(ps[:, 2 + h, :], ah[:, s], w, start=(i == 0 and k == 0), stop=False)
                            ins = pe.matmul(ps[:, 2 + h, :], al[:, s], w, start=False, stop=False)
                    ins.then_inc(wh_used, 1)
                    pe.wait_ge(wl_ready, u * PIECES + C_MOE + p + 1)
                    for k in range(n):
                        s = slice((k0 + k) * P, (k0 + k + 1) * P)
                        for h in range(2):
                            w = low[:, k * D + h * BANK:k * D + (h + 1) * BANK]
                            ins = pe.matmul(ps[:, 2 + h, :], ah[:, s], w, start=False,
                                            stop=(i == FC - 1 and k0 + k == 3))
                    ins.then_inc(w_used, 1)

                pe.wait_ge(gl_ready, u * 2 + 2)
                def turn(i):
                    pe.wait_ge(eprod_ready, u * FC + i + 1)
                    if i:
                        pe.wait_ge(eal_ready, u * FC + i)
                    else:
                        pe.wait_ge(acc_done, u * 4 + 1)
                    for k in range(4):
                        s = slice(k * P, (k + 1) * P)
                        ins = pe.transpose(ps[:, 4, s], bm["act"][:, s], ident)
                    ins.then_inc(eT_done, 1)

                for i in range(FC):
                    up(i, "g")
                    if i == 1:
                        turn(0)
                    up(i, "u")
                    if i >= 1:
                        down(i - 1)
                        turn(i)
                    if i == 3:
                        pe.wait_ge(pay_ready, u + 1)
                        pe.wait_ge(acc_done, u * 4 + 4)
                        for t in range(QT):
                            ins = pe.transpose(ps[:, 7, t * P:(t + 1) * P], bm["pay"][:, t, :], ident)
                        ins.then_inc(payT_done, 1)
                    if i == 4:
                        gather(u + 1, 0)
                gather(u + 1, 1)
                down(FC - 1, 0, 2)
                down(FC - 1, 2, 2)
                pe.wait_ge(payT_ev, u + 1)
                pe.wait_ge(gl_ready, u * 2 + 4)
                for n in range(4):
                    half, t = n // 2, n % 2
                    if t == 0:
                        pe.wait_ge(y_ev, u * 2 + half + 1)
                    pe.matmul(ps[:, SUMS[n], :], bm["payT"][:, t * P:(t + 1) * P],
                              bm["y"][:, half * BANK:(half + 1) * BANK], start=True, stop=True).then_inc(sc_done, 1)


_INS = ["x", "meta_tokens", "norm_gains", "sb_w_qkv", "sb_w_o", "diff_w_qkv", "diff_w_o", "diff_subln",
        "diff_lambda_q1", "diff_lambda_k1", "diff_lambda_q2", "diff_lambda_k2", "ffn_w_gate", "ffn_w_up",
        "ffn_w_down", "moe_router", "moe_w_gate", "moe_w_up", "moe_w_down", "final_norm"]


def kernel(**inputs):
    import concourse.bacc as bacc
    from concourse.bass_utils import run_bass_kernel_spmd

    nc = bacc.Bacc("TRN2", target_bir_lowering=False, num_devices=1)
    arrays, args = {}, []
    for name, a in [(n, inputs[n]) for n in _INS] + list(constants().items()):
        a = np.ascontiguousarray(a)
        arrays[f"in_{name}"] = a
        args.append(nc.dram_tensor(f"in_{name}", a.shape, mybir.dt.from_np(a.dtype), kind="ExternalInput").ap())
    args.append(nc.dram_tensor("out", (1, SEQ, D), F32, kind="ExternalOutput").ap())
    build(nc, *args)
    r = run_bass_kernel_spmd(nc, [arrays], core_ids=[0])
    return np.asarray(r.results[0]["out"])
```
